# Optimizing a Trainium2 kernel written in Bass

```python
import math
import jax, jax.numpy as jnp
from jax import lax
import numpy as np

D_MODEL = 1024
BATCH = 1
SEQ = 256
DEPTH = 2

CHUNK = 64
N_META = 16
Q_BLOCK = 128
N_MIXERS = 2
MLA_HEADS = 16
MLA_Q_RANK = 384
MLA_KV_RANK = 256
MLA_NOPE = 64
MLA_ROPE = 32
MLA_V = 64
MLA_QK = MLA_NOPE + MLA_ROPE
ROPE_THETA = 10000.0
GLA_HEADS = 4
GLA_DK = D_MODEL // 2 // GLA_HEADS
GLA_DV = D_MODEL // GLA_HEADS
GLA_GATE_RANK = 16
GLA_TAU = 16.0
N_GROUPS = 4
EXPERTS_PER_GROUP = 8
N_EXPERTS = N_GROUPS * EXPERTS_PER_GROUP
TOP_K = 2
D_EXPERT = 256
EPS = 1e-6

N_MLA_LAYERS = (DEPTH + 1) // 2
N_GLA_LAYERS = DEPTH // 2
MLA_IN = MLA_Q_RANK + MLA_KV_RANK + MLA_ROPE
GLA_NK = GLA_HEADS * GLA_DK
GLA_NV = GLA_HEADS * GLA_DV
GLA_IN = 2 * GLA_NK + GLA_NV + GLA_GATE_RANK + GLA_NV

kernel_name = "hybrid_mla_gla_hmoe_streaming"

def rms_norm(x, g):
    xf = x.astype(jnp.float32)
    y = xf * lax.rsqrt(jnp.mean(xf * xf, axis=-1, keepdims=True) + EPS)
    return (y * g.astype(jnp.float32)).astype(x.dtype)

def chunk_ids(n):
    p = jnp.arange(n)
    return jnp.where(p < N_META, 0, 1 + (p - N_META) // CHUNK)

def rope(x, pos):
    half = x.shape[-1] // 2
    inv = 1.0 / (ROPE_THETA ** (jnp.arange(half, dtype=jnp.float32) / half))
    ang = pos.astype(jnp.float32)[:, None] * inv[None, :]
    cos = jnp.cos(ang)[:, None, :]
    sin = jnp.sin(ang)[:, None, :]
    xf = x.astype(jnp.float32)
    x1, x2 = xf[..., :half], xf[..., half:]
    return jnp.concatenate([x1 * cos - x2 * sin, x2 * cos + x1 * sin], axis=-1).astype(x.dtype)

def block_causal_attention(q, k, v):
    B, L, H, dh = q.shape
    nblk = L // Q_BLOCK
    cid = chunk_ids(L)
    scale = dh ** -0.5
    qb = q.reshape(B, nblk, Q_BLOCK, H, dh).transpose(1, 0, 3, 2, 4)
    cb = cid.reshape(nblk, Q_BLOCK)
    kt = k.transpose(0, 2, 1, 3)
    vt = v.transpose(0, 2, 1, 3)

    def one_block(args):
        q_blk, c_blk = args
        s = jnp.einsum('bhqd,bhkd->bhqk', q_blk, kt,
                       preferred_element_type=jnp.float32) * scale
        mask = c_blk[:, None] >= cid[None, :]
        s = jnp.where(mask[None, None], s, -jnp.inf)
        p = jax.nn.softmax(s, axis=-1)
        return jnp.einsum('bhqk,bhkd->bhqd', p.astype(vt.dtype), vt)

    o = lax.map(one_block, (qb, cb))
    return o.transpose(1, 0, 3, 2, 4).reshape(B, L, H, -1)

def mla_mixer(h, w_in, g_q, w_uq, g_kv, w_ukv, g_qn, g_kn, w_o):
    B, L, _ = h.shape
    z = h @ w_in
    c_q, c_kv, k_r = jnp.split(z, [MLA_Q_RANK, MLA_Q_RANK + MLA_KV_RANK], axis=-1)
    q = (rms_norm(c_q, g_q) @ w_uq).reshape(B, L, MLA_HEADS, MLA_QK)
    kv = (rms_norm(c_kv, g_kv) @ w_ukv).reshape(B, L, MLA_HEADS, MLA_NOPE + MLA_V)
    k_nope, v = jnp.split(kv, [MLA_NOPE], axis=-1)
    k_r = jnp.broadcast_to(k_r[:, :, None, :], (B, L, MLA_HEADS, MLA_ROPE))
    k = jnp.concatenate([k_nope, k_r], axis=-1)
    q = rms_norm(q, g_qn)
    k = rms_norm(k, g_kn)
    pos = jnp.arange(L)
    q = jnp.concatenate([q[..., :MLA_NOPE], rope(q[..., MLA_NOPE:], pos)], axis=-1)
    k = jnp.concatenate([k[..., :MLA_NOPE], rope(k[..., MLA_NOPE:], pos)], axis=-1)
    o = block_causal_attention(q, k, v)
    return o.reshape(B, L, MLA_HEADS * MLA_V) @ w_o

def gla_mixer(h, w_in, w_gate_up, b_gate, g_out, w_o):
    B, L, _ = h.shape
    f32 = jnp.float32
    z = h @ w_in
    q, k, v, g_lr, r = jnp.split(
        z, [GLA_NK, 2 * GLA_NK, 2 * GLA_NK + GLA_NV, 2 * GLA_NK + GLA_NV + GLA_GATE_RANK], axis=-1)
    log_a = jax.nn.log_sigmoid((g_lr @ w_gate_up + b_gate).astype(f32)) / GLA_TAU
    n = L // CHUNK

    def heads(t, d):
        return t.astype(f32).reshape(B, n, CHUNK, GLA_HEADS, d).transpose(1, 0, 3, 2, 4)

    qc = heads(q, GLA_DK) * (GLA_DK ** -0.5)
    kc = heads(k, GLA_DK)
    vc = heads(v, GLA_DV)
    gc = heads(log_a, GLA_DK)
    tri = jnp.tril(jnp.ones((CHUNK, CHUNK), dtype=bool))

    def step(S, inp):
        qq, kk, vv, gg = inp
        b = jnp.cumsum(gg, axis=-2)
        o_inter = jnp.einsum('bhck,bhkv->bhcv', qq * jnp.exp(b), S)
        diff = b[:, :, :, None, :] - b[:, :, None, :, :]
        decay = jnp.exp(jnp.where(tri[:, :, None], diff, -jnp.inf))
        att = jnp.einsum('bhtk,bhtsk,bhsk->bhts', qq, decay, kk)
        o = o_inter + jnp.einsum('bhts,bhsv->bhtv', att, vv)
        b_last = b[:, :, -1:, :]
        S = jnp.exp(b_last[:, :, 0, :, None]) * S + jnp.einsum(
            'bhck,bhcv->bhkv', kk * jnp.exp(b_last - b), vv)
        return S, o

    S0 = jnp.zeros((B, GLA_HEADS, GLA_DK, GLA_DV), f32)
    _, o = lax.scan(step, S0, (qc, kc, vc, gc))
    o = o.transpose(1, 0, 3, 2, 4).reshape(B, L, GLA_HEADS, GLA_DV)
    o = rms_norm(o, g_out).astype(h.dtype).reshape(B, L, GLA_NV)
    o = o * jax.nn.silu(r)
    return o @ w_o

def hier_moe(h, w_rg, b_rg, w_re, b_re, w_gate, w_up, w_down):
    B, L, D = h.shape
    f32 = jnp.float32
    t = h.reshape(-1, D)
    g_logits = (t @ w_rg).astype(f32) + b_rg.astype(f32)
    g_prob = jax.nn.softmax(g_logits, axis=-1)
    g_sel = jnp.argmax(g_logits, axis=-1)
    p_g = jnp.take_along_axis(g_prob, g_sel[:, None], axis=-1)
    e_logits = ((t @ w_re).astype(f32) + b_re.astype(f32)).reshape(-1, N_GROUPS, EXPERTS_PER_GROUP)
    e_logits = jnp.take_along_axis(e_logits, g_sel[:, None, None], axis=1)[:, 0]
    e_prob = jax.nn.softmax(e_logits, axis=-1)
    top_p, top_i = lax.top_k(e_prob, TOP_K)
    top_w = top_p / jnp.sum(top_p, axis=-1, keepdims=True) * p_g
    expert_id = g_sel[:, None] * EXPERTS_PER_GROUP + top_i
    gates = jnp.einsum('tk,tke->te', top_w, jax.nn.one_hot(expert_id, N_EXPERTS, dtype=f32))
    out = jnp.zeros(t.shape, f32)
    for e in range(N_EXPERTS):
        hid = jax.nn.silu(t @ w_gate[e]) * (t @ w_up[e])
        out = out + gates[:, e:e + 1] * (hid @ w_down[e]).astype(f32)
    return out.astype(h.dtype).reshape(B, L, D)

def setup_inputs(seed: int = 0) -> dict:
    key = jax.random.key(seed)
    ks = iter(jax.random.split(key, 40))
    f32 = jnp.float32

    def dense(shape, fan_in):
        return jax.random.normal(next(ks), shape, f32) * (fan_in ** -0.5)

    def gain(shape):
        return 1.0 + 0.01 * jax.random.normal(next(ks), shape, f32)

    def bias(shape, s):
        return s * jax.random.normal(next(ks), shape, f32)

    nm, ng = N_MLA_LAYERS, N_GLA_LAYERS
    return {
        "x": jax.random.normal(next(ks), (BATCH, SEQ, D_MODEL), f32),
        "meta_tokens": jax.random.normal(next(ks), (N_META, D_MODEL), f32),
        "norm_mix": gain((DEPTH, D_MODEL)),
        "norm_ffn": gain((DEPTH, D_MODEL)),
        "mla_w_in": dense((nm, D_MODEL, MLA_IN), D_MODEL),
        "mla_g_q": gain((nm, MLA_Q_RANK)),
        "mla_w_uq": dense((nm, MLA_Q_RANK, MLA_HEADS * MLA_QK), MLA_Q_RANK),
        "mla_g_kv": gain((nm, MLA_KV_RANK)),
        "mla_w_ukv": dense((nm, MLA_KV_RANK, MLA_HEADS * (MLA_NOPE + MLA_V)), MLA_KV_RANK),
        "mla_g_qn": gain((nm, MLA_QK)),
        "mla_g_kn": gain((nm, MLA_QK)),
        "mla_w_o": dense((nm, MLA_HEADS * MLA_V, D_MODEL), MLA_HEADS * MLA_V),
        "gla_w_in": dense((ng, D_MODEL, GLA_IN), D_MODEL),
        "gla_w_gate_up": dense((ng, GLA_GATE_RANK, GLA_NK), GLA_GATE_RANK),
        "gla_b_gate": bias((ng, GLA_NK), 0.1),
        "gla_g_out": gain((ng, GLA_DV)),
        "gla_w_o": dense((ng, GLA_NV, D_MODEL), GLA_NV),
        "moe_w_rg": dense((DEPTH, D_MODEL, N_GROUPS), D_MODEL),
        "moe_b_rg": bias((DEPTH, N_GROUPS), 0.01),
        "moe_w_re": dense((DEPTH, D_MODEL, N_EXPERTS), D_MODEL),
        "moe_b_re": bias((DEPTH, N_EXPERTS), 0.01),
        "moe_w_gate": dense((DEPTH, N_EXPERTS, D_MODEL, D_EXPERT), D_MODEL),
        "moe_w_up": dense((DEPTH, N_EXPERTS, D_MODEL, D_EXPERT), D_MODEL),
        "moe_w_down": dense((DEPTH, N_EXPERTS, D_EXPERT, D_MODEL), D_EXPERT),
    }

def reference(x, meta_tokens, norm_mix, norm_ffn,
              mla_w_in, mla_g_q, mla_w_uq, mla_g_kv, mla_w_ukv, mla_g_qn, mla_g_kn, mla_w_o,
              gla_w_in, gla_w_gate_up, gla_b_gate, gla_g_out, gla_w_o,
              moe_w_rg, moe_b_rg, moe_w_re, moe_b_re, moe_w_gate, moe_w_up, moe_w_down):
    B, S, D = x.shape
    L = N_META + S
    Lp = ((L + Q_BLOCK - 1) // Q_BLOCK) * Q_BLOCK
    meta = jnp.broadcast_to(meta_tokens.astype(x.dtype)[None], (B, N_META, D))
    h = jnp.concatenate([meta, x, jnp.zeros((B, Lp - L, D), x.dtype)], axis=1)
    for i in range(DEPTH):
        j = i // N_MIXERS
        hn = rms_norm(h, norm_mix[i])
        if i % N_MIXERS == 0:
            h = h + mla_mixer(hn, mla_w_in[j], mla_g_q[j], mla_w_uq[j], mla_g_kv[j],
                              mla_w_ukv[j], mla_g_qn[j], mla_g_kn[j], mla_w_o[j])
        else:
            h = h + gla_mixer(hn, gla_w_in[j], gla_w_gate_up[j], gla_b_gate[j],
                              gla_g_out[j], gla_w_o[j])
        h = h + hier_moe(rms_norm(h, norm_ffn[i]), moe_w_rg[i], moe_b_rg[i], moe_w_re[i],
                         moe_b_re[i], moe_w_gate[i], moe_w_up[i], moe_w_down[i])
    return h[:, N_META:N_META + S]


_drawn_inputs = setup_inputs


def setup_inputs(seed=0):
    import zlib

    import numpy as np

    out = dict(_drawn_inputs(seed))
    spreads = {}
    factors = {'mla_g_q': 5.239,
     'mla_g_kn': 3.108,
     'gla_g_out': 81.321,
     'moe_b_re': 3.875,
     'moe_b_rg': 2.756}
    for name, (base, spread) in spreads.items():
        noise = np.random.default_rng([zlib.crc32(name.encode()), seed]).standard_normal(out[name].shape)
        drawn = base * np.exp(spread * noise) if base else spread * noise
        out[name] = __import__('jax').numpy.asarray(drawn.astype(out[name].dtype))
    for name, factor in factors.items():
        out[name] = (out[name] * factor).astype(out[name].dtype)
    return out
```

```python
from contextlib import ExitStack

import numpy as np

import concourse.bass as bass
from concourse import mybir

F32 = mybir.dt.float32
I32 = mybir.dt.int32
ALU = mybir.AluOpType
ACT = mybir.ActivationFunctionType
AX = mybir.AxisListType

P = 128
D = 1024
KD = D // P
SEQ, META = 256, 16
POS = META + SEQ
CHUNK = 64
COL = [META, META + P, 0]
WID = [P, P, META]
EPS = 1e-6

HEADS, NOPE, ROPE, VD = 16, 64, 32, 64
QK = NOPE + ROPE
QR, KVR = 384, 256
ZA, ZB = QR, KVR + ROPE
MASK_ROWS = 2
BIG = 1e30

GH, GDK, GDV, GRANK, TAU = 4, 128, 256, 16, 16.0
SUB = 32
NSUB = SEQ // SUB

NG, EPG, NE, FE = 4, 8, 32, 256
SLOTS = 32
GE = 4
GROUPS = NE // GE
OFF = 1000.0
COMBINE = [0, 1, 7, 3, 4, 2]
LOOP_LINKS = 4
ROUNDS = -(-POS // SLOTS) - 1


def constants():
    parts, at, w = [], {}, 0

    def put(name, a):
        nonlocal w
        full = np.zeros((P, a.shape[1]), np.float32)
        full[:a.shape[0]] = a
        parts.append(full)
        at[name] = (w, w + a.shape[1])
        w += a.shape[1]

    pr = np.arange(P)
    put("ident", np.eye(P))
    put("before", (pr[:, None] < pr[None, :]).astype(np.float32))
    put("ones", np.ones((P, POS)))
    put("slot", np.tile(np.arange(SLOTS) - OFF, (P, 1)))
    put("first", np.tile(np.arange(NE, 0, -1), (P, 1)))
    valid = np.ones((P, 3))
    valid[META:, 2] = 0
    put("valid", valid)
    col = np.arange(POS)
    put("causal", np.concatenate([(col[None, :] <= (COL[i] + pr)[:, None]) for i in (0, 1)], 1))
    half = ROPE // 2
    inv = 1.0 / (np.float32(10000.0) ** (np.arange(half, dtype=np.float32) / np.float32(half)))
    pos = np.stack([COL[i] + np.minimum(pr, WID[i] - 1) for i in range(3)], 1).astype(np.float32)
    ang = (pos[:, :, None] * inv.astype(np.float32)).astype(np.float32)
    cos, sin = np.cos(ang), np.sin(ang)
    put("cos", np.concatenate([cos, cos], 2).reshape(P, -1))
    put("sin", np.concatenate([sin, sin], 2).reshape(P, -1))
    cid = np.where(col < META, 0, 1 + (col - META) // CHUNK)
    rows = np.zeros((2, MASK_ROWS, POS), np.float32)
    for m in range(MASK_ROWS):
        rows[0, m] = cid == 2 * m + 1
        rows[1, m] = np.where(cid == 2 * m + 2, -BIG, 0.0)
    return np.ascontiguousarray(np.concatenate(parts, 1), dtype=np.float32), rows, at


class Links:

    def __init__(self, eng, sem):
        self.eng, self.sem, self.n, self.base = eng, sem, 0, 0

    def __call__(self, ins):
        self.n += 1
        ins.then_inc(self.sem, 1)
        self.eng.wait_ge(self.sem, self.base + self.n)


def program(nc, a, out):
    with ExitStack() as ctx:
        build(nc, a, out, ctx)


def build(nc, a, out, ctx):
    def sb(name, shape, dt=F32):
        return ctx.enter_context(nc.sbuf_tensor(name, shape, dt))

    def sem(name):
        return ctx.enter_context(nc.semaphore(name))

    _, _, at = constants()
    CW = max(e for _, e in at.values())

    cst = sb("cst", [P, CW])

    def c(name):
        return cst[:, at[name][0]:at[name][1]]

    ident, before, ones = c("ident"), c("before"), c("ones")
    h = sb("h", [P, 3, D])
    xn = sb("xn", [P, 3, KD, P])
    hT = sb("hT", [P, KD, POS])
    PART = 8192
    ring = sb("ring", [P, 3 * PART])
    RA, RB, RD = (ring[:, i * PART:(i + 1) * PART] for i in range(3))
    gn = sb("gn", [P, 4, KD])
    flag = sb("flag", [1, 2], I32)
    marker = sb("marker", [1, 2])
    ssq = sb("ssq", [P, 3])
    rstd = sb("rstd", [P, 3])
    fix = sb("fix", [P, 3])
    eps_b, epsqk_b, one_b = (fix[:, i:i + 1] for i in range(3))
    wr = sb("wr", [P, 2, KD, NG + NE])
    rb = sb("rb", [P, 2, NG + NE])
    wlr = sb("wlr", [P, KD, GRANK])
    wgu = sb("wgu", [P, GH * GDK])
    bg = sb("bg", [P, GH])
    gout = sb("gout", [P, GDV])
    ARENA = 17300
    arena = sb("arena", [P, ARENA])
    top = [0]

    def take(*shape):
        n = int(np.prod(shape))
        assert top[0] + n <= ARENA, (top[0], n)
        v = arena[:, top[0]:top[0] + n]
        top[0] += n
        if len(shape) == 2:
            v = v.rearrange("p (a b) -> p a b", a=shape[0])
        if len(shape) == 3:
            v = v.rearrange("p (a b c) -> p a b c", a=shape[0], b=shape[1])
        return v

    L = take(3, NG + NE)
    E5 = take(3, NG + 1)
    le, eq, s1, s2, sel = (take(3, NE) for _ in range(5))
    rm, gates = take(3, NE + GE), take(3, NE + GE)
    mg, m1, m2, pm, w1, w2 = (take(3) for _ in range(6))
    g4 = take(3, NG)
    most = take(1)
    lgT = take(POS)
    shared = top[0]
    Sg, Gg = take(3, GE * SLOTS), take(3, GE * SLOTS)
    xe = take(KD, P)
    ex, den = take(FE), take(FE)
    hid, hidT = take(2, P), take(2, P)
    GT = take(POS)
    ysb = take(D)
    top[0] = shared
    vt = take(3, HEADS, VD)
    qT, kT = take(HEADS, POS), take(HEADS, POS)
    zst, zrs = take(3, 2), take(3, 2)
    kr, krs = take(3, ROPE), take(3)
    tcq, tsq, tck, tsk = (take(3, ROPE) for _ in range(4))
    gqk = take(2, QK)
    gcol, gprod, gc5 = take(2), take(1), take(5)
    qst, kst, scl, krst = (take(3, HEADS) for _ in range(4))
    mx, rs, nb, ri = ([take(3), take(3)] for _ in range(4))
    att_top = top[0]
    cq = take(5, P)
    cT = take(5, POS)
    rp = take(2, HEADS * ROPE)
    top[0] = att_top
    PR = COL[1] + POS + META
    prob = [take(PR), take(PR)]
    pT = [take(3 * P + POS), take(3 * P + POS)]
    oT = hT
    xflat = xn[:, :, :, :].rearrange("p a k q -> p (a k q)")
    q_sb = xflat[:, 0:HEADS * QK].rearrange("p (h f) -> p h f", h=HEADS)
    k_sb = xflat[:, HEADS * QK:].rearrange("p (h f) -> p h f", h=HEADS)
    top[0] = shared
    gqT = take(GH, SEQ)
    gkT = take(GH, POS)
    ga, gb, gt = take(GH, POS), take(GH, POS), take(GH, POS)
    gv = take(3, GH * GDV)
    gr = take(2, D)
    gk = [take(GH, POS) for _ in range(3)]
    glr = take(POS)
    gos, gor = take(2, GH), take(2, GH)
    attM = take(GH, SEQ)
    gtq = gt[:, :, 0:SEQ]
    gsq = xflat[:, 2 * GH * POS:2 * GH * POS + GDV]
    att = xflat[:, 0:2 * GH * POS].rearrange("p (t g s) -> p t g s", t=2, g=GH)
    attT = [w.rearrange("p a b -> p (a b)")[:, o:o + 3 * P] for w in (ga, gt) for o in (0, 3 * P)]
    gyT = hT[:, :, 0:SEQ]

    ps = ctx.enter_context(nc.psum_tensor("ps", [P, 8, 512], F32))

    names = """in_h in_c in_small in_moe in_rows w_z w_q w_kv w_mo w_gqk w_gv w_gr w_go
        act_link dve_link zeroed consts
        rstd_ok xn_act xn_dve xn_turned hT_ok
        z_done z_rstd z_kr z_scaled c_turned cT_ok tabs_ok
        q_done kv_done q_copied q_squared v_copied k_squared q_sums k_sums k_rstd k_scaled qk_ready
        qk_turned qT_ok kT_ok
        s_done s_shift p_exp p_scaled p_turned pt_act pt_dve pv_done o_copied mo_done mo_add
        g_job g_act g_dve g_abs g_log gq_dif gq_exp gq_ok gk_dif gk_exp gk_ok g_att g_attm g_rexp
        g_attT g_aT_act g_aT_dve g_o g_orstd g_y g_yT g_yTc go_done go_add
        lg_done lg_copied lg_turned e_dif e_exp sel_ok rank_done
        flag_ok moe_done stored"""
    S = {n: sem(n) for n in names.split()}
    (in_h, in_c, in_small, in_moe, in_rows, w_z, w_q, w_kv, w_mo, w_gqk, w_gv, w_gr, w_go,
     act_link, dve_link, zeroed, consts,
     rstd_ok, xn_act, xn_dve, xn_turned, hT_ok,
     z_done, z_rstd, z_kr, z_scaled, c_turned, cT_ok, tabs_ok,
     q_done, kv_done, q_copied, q_squared, v_copied, k_squared, q_sums, k_sums, k_rstd, k_scaled, qk_ready,
     qk_turned, qT_ok, kT_ok,
     s_done, s_shift, p_exp, p_scaled, p_turned, pt_act, pt_dve, pv_done, o_copied, mo_done, mo_add,
     g_job, g_act, g_dve, g_abs, g_log, gq_dif, gq_exp, gq_ok, gk_dif, gk_exp, gk_ok, g_att, g_attm, g_rexp,
     g_attT, g_aT_act, g_aT_dve, g_o, g_orstd, g_y, g_yT, g_yTc, go_done, go_add,
     lg_done, lg_copied, lg_turned, e_dif, e_exp, sel_ok, rank_done,
     flag_ok, moe_done, stored) = S.values()

    class GroupSems:

        def __init__(self, tag):
            self.a, self.b, self.d = sem(f"{tag}_a"), sem(f"{tag}_b"), sem(f"{tag}_d")
            self.a_read, self.b_read, self.d_read = sem(f"{tag}_a_read"), sem(f"{tag}_b_read"), sem(f"{tag}_d_read")
            self.send = sem(f"{tag}_send")
            self.rows = sem(f"{tag}_rows")
            self.rows_in = sem(f"{tag}_rows_in")
            self.turn = sem(f"{tag}_turn")
            self.turned = sem(f"{tag}_turned")
            self.exp = sem(f"{tag}_exp")
            self.hid = sem(f"{tag}_hid")
            self.hid_t = sem(f"{tag}_hid_t")
            self.hid_c = sem(f"{tag}_hid_c")
            self.ya, self.yd = sem(f"{tag}_ya"), sem(f"{tag}_yd")
            self.comb = sem(f"{tag}_comb")
            self.add = sem(f"{tag}_add")
            self.step = sem(f"{tag}_step")
            self.seen = sem(f"{tag}_seen")

    FAST = GroupSems("fast")
    OVER = [GroupSems(f"over{l}") for l in range(2)]

    def rep(ap, n):
        return ap.unsqueeze(2).to_broadcast([ap.shape[0], ap.shape[1], n])

    def rep3(ap, n):
        return ap.unsqueeze(3).to_broadcast([*ap.shape, n])

    def over(ap, n):
        return ap.unsqueeze(1).to_broadcast([ap.shape[0], n, ap.shape[1]])

    def flat(ap):
        return ap.rearrange("p a b -> p (a b)")

    NT = [3, 2]
    COMB0 = [0, 2 * NT[0] * GROUPS]
    ADD0 = [0, 2 * NT[0] * GROUPS + 1]
    NORM_TILES = [3, 3, 3, 2]
    NB = [sum(NORM_TILES[:i]) for i in range(5)]
    H_DONE = [(in_h, 48), (mo_add, 6), (moe_done, 1), (go_add, 4)]
    N_SMALL, N_ROWS = 11, 2 * MASK_ROWS

    wz = ring[:, 0:KD * (ZA + ZB)].rearrange("p (k n) -> p k n", k=KD)
    o_q = KD * (ZA + ZB)
    wq = ring[:, o_q:o_q + 3 * HEADS * QK].rearrange("p (k n) -> p k n", k=3)
    o_kv = o_q + 3 * HEADS * QK
    wkv = ring[:, o_kv:o_kv + 2 * HEADS * (NOPE + VD)].rearrange("p (k n) -> p k n", k=2)
    o_sq = o_kv + 2 * HEADS * (NOPE + VD)
    sq = ring[:, o_sq:o_sq + HEADS * QK].rearrange("p (h f) -> p h f", h=HEADS)
    wmo, wqk, wv, wrr, wgo = (r.rearrange("p (k n) -> p k n", k=KD) for r in (RD, RA, RB, RD, RA))
    HK = KD // 2
    moeA, moeB = (r.rearrange("p (m e n) -> p m e n", m=2, e=GE) for r in (RA, RB))
    moeD = RD.rearrange("p (e n) -> p e n", e=GE)
    VO = 2 * GH * GDK
    LRO = VO + GH * GDV
    RO = LRO + GRANK

    JOBS = [("lr", 0, "act", 0)] + [("q", n, "act", 1 + n) for n in range(GH)]
    JOBS += [("a", n, "dve", (5 + n) % 8) for n in range(GH)] + [("k", n, "act", 1 + n) for n in range(GH)]
    JOBS += [("v", n, "act", (5 + n) % 8) for n in range(6)] + [("r", n, "dve", 4 + n) for n in range(4)]
    counts = {"act": 0, "dve": 0}
    emptied = []
    for _, _, who, _ in JOBS:
        counts[who] += 1
        emptied.append(({"act": g_act, "dve": g_dve}[who], counts[who]))
    before_me = [max((i for i in range(j) if JOBS[i][3] == JOBS[j][3]), default=None) for j in range(len(JOBS))]
    K_END, V_END, R_END = 13, 19, 23

    block = ctx.enter_context(nc.Block())

    def overflow(eng, l):
        eng.wait_ge(flag_ok, l + 1)
        return eng.value_load(flag[0:1, l:l + 1], min_val=0, max_val=1) != 0

    @block.sync
    def _(sp):
        sp.dma_start(h[:, 0, :], a["x"][0, 0:P, :]).then_inc(in_h, 16)
        sp.dma_start(h[:, 1, :], a["x"][0, P:SEQ, :]).then_inc(in_h, 16)
        sp.wait_ge(zeroed, 1)
        sp.dma_start(h[0:META, 2, :], a["meta_tokens"]).then_inc(in_h, 16)
        sp.dma_start(cst[:, :], a["const"]).then_inc(in_c, 16)
        with nc.allow_non_contiguous_dma(reason="gains, a column per block"):
            for n in range(4):
                src = a["norm_mix" if n % 2 == 0 else "norm_ffn"][n // 2]
                sp.dma_start(gn[:, n, :], src.rearrange("(p k) -> p k", k=KD)).then_inc(in_small, 16)
            sp.dma_start(gc5[:, 0:3], a["mla_g_q"][0].rearrange("(p k) -> p k", k=3)).then_inc(in_small, 16)
            sp.dma_start(gc5[:, 3:5], a["mla_g_kv"][0].rearrange("(p k) -> p k", k=2)).then_inc(in_small, 16)
            sp.dma_start(gcol[0:NOPE, 0:1], a["mla_g_qn"][0, 0:NOPE].rearrange("(p o) -> p o", o=1)).then_inc(in_small, 16)
            sp.dma_start(gcol[0:NOPE, 1:2], a["mla_g_kn"][0, 0:NOPE].rearrange("(p o) -> p o", o=1)).then_inc(in_small, 16)
            sp.dma_start(bg[:, :], a["gla_b_gate"][0].rearrange("(g p) -> p g", p=P)).then_inc(in_small, 16)
        sp.dma_start(gqk[:, 0, :], a["mla_g_qn"].to_broadcast([P, QK])).then_inc(in_small, 16)
        sp.dma_start(gqk[:, 1, :], a["mla_g_kn"].to_broadcast([P, QK])).then_inc(in_small, 16)
        sp.dma_start(wz, a["mla_w_in"][0].rearrange("(p k) n -> p k n", k=KD)).then_inc(w_z, 16)
        sp.dma_start(wq, a["mla_w_uq"][0].rearrange("(p k) n -> p k n", k=3)).then_inc(w_q, 16)
        sp.dma_start(wkv, a["mla_w_ukv"][0].rearrange("(p k) n -> p k n", k=2)).then_inc(w_kv, 16)
        for m, t in ((0, qT), (1, kT)):
            for r in range(MASK_ROWS):
                sp.dma_start(t[QK + r:QK + r + 1, :, :],
                             a["mask_rows"][m, r:r + 1].unsqueeze(1).to_broadcast([1, HEADS, POS])).then_inc(in_rows, 16)
        sp.dma_start(wmo, a["mla_w_o"][0].rearrange("(k p) n -> p k n", p=P)).then_inc(w_mo, 16)
        for l in range(2):
            sp.dma_start(wr[:, l, :, 0:NG], a["moe_w_rg"][l].rearrange("(p k) n -> p k n", k=KD)).then_inc(in_moe, 16)
            sp.dma_start(wr[:, l, :, NG:], a["moe_w_re"][l].rearrange("(p k) n -> p k n", k=KD)).then_inc(in_moe, 16)
            sp.dma_start(rb[:, l, 0:NG], a["moe_b_rg"][l:l + 1].to_broadcast([P, NG])).then_inc(in_moe, 16)
            sp.dma_start(rb[:, l, NG:], a["moe_b_re"][l:l + 1].to_broadcast([P, NE])).then_inc(in_moe, 16)
        sp.dma_start(wlr[:, :, :], a["gla_w_in"][0].rearrange("(p k) n -> p k n", k=KD)[:, :, LRO:RO]).then_inc(in_moe, 16)
        sp.dma_start(wgu[0:GRANK, :], a["gla_w_gate_up"][0]).then_inc(in_moe, 16)
        sp.dma_start(gout[:, :], a["gla_g_out"].to_broadcast([P, GDV])).then_inc(in_moe, 16)

        def load(l, K, g, waits):
            for p, dst, lo, landed in ((0, moeA, 0, K.a), (1, moeB, HK, K.b)):
                for s, v in waits[p]:
                    sp.wait_ge(s, v)
                for m, name in ((0, "moe_w_gate"), (1, "moe_w_up")):
                    src = a[name][l].rearrange("(g e) (p k) n -> g p e (k n)", e=GE, k=KD)
                    sp.dma_start(dst[:, m], src[bass.ds(g, 1), :, :, lo * FE:(lo + HK) * FE]
                                 .rearrange("g p e n -> (g p) e n")).then_inc(landed, 16)
            for s, v in waits[2]:
                sp.wait_ge(s, v)
            src = a["moe_w_down"][l].rearrange("(g e) (p k) n -> g p e (k n)", e=GE, k=2)
            sp.dma_start(moeD, src[bass.ds(g, 1)].rearrange("g p e n -> (g p) e n")).then_inc(K.d, 16)

        def experts(l, gate):
            K = FAST
            load(l, K, 0, gate)
            with sp.Fori(1, GROUPS) as g:
                n = g + GROUPS * l
                load(l, K, g, [[(K.a_read, n)], [(K.b_read, n)], [(K.d_read, n)]])
            with sp.If(overflow(sp, l)):
                K = OVER[l]
                for s in (FAST.a_read, FAST.b_read, FAST.d_read):
                    sp.wait_ge(s, GROUPS * (l + 1))
                with sp.Fori(0, ROUNDS) as r:
                    with sp.Fori(0, GROUPS) as g:
                        load(l, K, g, [[], [], []])
                        for s in (K.a_read, K.b_read, K.d_read):
                            sp.wait_ge(s, r * GROUPS + g + 1)
                        sp.sem_inc(K.seen, 1)

        experts(0, [[(q_done, 3)], [(kv_done, 3), (k_sums, 3)], [(mo_done, 6)]])
        gw_in = a["gla_w_in"][0].rearrange("(p k) n -> p k n", k=KD)
        sp.wait_ge(FAST.a_read, GROUPS)
        sp.dma_start(wqk, gw_in[:, :, 0:VO]).then_inc(w_gqk, 16)
        sp.wait_ge(FAST.b_read, GROUPS)
        sp.dma_start(wv, gw_in[:, :, VO:LRO]).then_inc(w_gv, 16)
        sp.wait_ge(FAST.d_read, GROUPS)
        sp.dma_start(wrr, gw_in[:, :, RO:RO + D]).then_inc(w_gr, 16)
        sp.wait_ge(g_job, K_END)
        sp.dma_start(wgo, a["gla_w_o"][0].rearrange("(k p) n -> p k n", p=P)).then_inc(w_go, 16)
        experts(1, [[(go_done, 4)], [(g_job, V_END)], [(g_job, R_END)]])
        for i in range(2):
            sp.wait_ge(moe_done, 2)
            sp.dma_start(out[0, i * P:(i + 1) * P, :], h[:, i, :]).then_inc(stored, 16)
        sp.wait_ge(stored, 32)

    @block.gpsimd
    def _(pool):
        pool.memset(h[:, 2, :], 0.0).then_inc(zeroed, 1)
        pool.memset(eps_b, EPS).then_inc(consts, 1)
        pool.memset(epsqk_b, QK * EPS).then_inc(consts, 1)
        pool.memset(one_b, 1.0).then_inc(consts, 1)
        pool.memset(vt[:, 2, :, :], 0.0).then_inc(zeroed, 1)
        pool.memset(gprod, 1.0).then_inc(zeroed, 1)
        pool.memset(scl, 0.0).then_inc(zeroed, 1)
        for i in range(2):
            pool.memset(mx[i], 0.0).then_inc(zeroed, 1)
            pool.memset(rs[i], 1.0).then_inc(zeroed, 1)
        pool.memset(L, 0.0).then_inc(zeroed, 1)
        pool.memset(rm, 0.0).then_inc(zeroed, 1)
        pool.memset(gates, 0.0).then_inc(zeroed, 1)
        pool.wait_ge(kT_ok, 12)
        pool.wait_ge(qT_ok, 12)
        for i in range(2):
            pool.memset(pT[i][:, 3 * P:], 0.0).then_inc(zeroed, 1)
        pool.wait_ge(moe_done, 1)
        pool.memset(gv[:, 2, :], 0.0).then_inc(zeroed, 1)
        pool.memset(attM, 0.0).then_inc(zeroed, 1)
        pool.wait_ge(xn_turned, NB[3])
        pool.memset(att, 0.0).then_inc(zeroed, 1)

    @block.tensor
    def _(pe):
        def norm(n):
            for i in range(NORM_TILES[n]):
                if i == 1:
                    pe.wait_ge(xn_dve, n + 1)
                else:
                    pe.wait_ge(xn_act, 2 * n + 1 + i // 2)
                for k in range(KD):
                    R = WID[i]
                    dst = ps[:, 2 * i + k // 4, (k % 4) * P:(k % 4 + 1) * P] if i < 2 else ps[:, 4, k * R:(k + 1) * R]
                    mm = pe.transpose(dst, xn[0:R, i, k, :], ident[0:R, 0:R])
                mm.then_inc(xn_turned, 1)

        def project(src, w, tiles, done):
            for i in range(tiles):
                c0 = COL[i] if tiles == 3 else i * P
                for b in range(2):
                    for k in range(KD):
                        mm = pe.matmul(ps[0:WID[i], 2 * i + b, :], src[:, k, c0:c0 + WID[i]],
                                       w[:, k, b * 512:(b + 1) * 512], start=k == 0, stop=k == KD - 1)
                    mm.then_inc(done, 1)

        def mla():
            pe.wait_ge(w_z, 16)
            pe.wait_ge(hT_ok, 3)
            for i in range(3):
                for n0, n1, b in ((0, ZA, 5 + 2 * i), (ZA, ZA + ZB, 6 + 2 * i)):
                    for k in range(KD):
                        mm = pe.matmul(ps[0:WID[i], b % 8, 0:n1 - n0], hT[:, k, COL[i]:COL[i] + WID[i]],
                                       wz[:, k, n0:n1], start=k == 0, stop=k == KD - 1)
                mm.then_inc(z_done, 1)
            for i in range(3):
                pe.wait_ge(z_scaled, i + 1)
                if i:
                    pe.wait_ge(cT_ok, i)
                R = WID[i]
                for k in range(5):
                    b, o = (3, k * R) if k < 3 else (4, (k - 3) * R)
                    mm = pe.transpose(ps[:, b, o:o + R], cq[0:R, k, :], ident[0:R, 0:R])
                mm.then_inc(c_turned, 1)
            pe.wait_ge(w_q, 16)
            pe.wait_ge(w_kv, 16)
            pe.wait_ge(cT_ok, 3)
            pe.wait_ge(z_kr, 3)
            for i in range(3):
                R, cols = WID[i], slice(COL[i], COL[i] + WID[i])
                if i:
                    pe.wait_ge(qT_ok, 4 * i)
                    pe.wait_ge(kT_ok, 4 * i)
                for b in range(3):
                    for k in range(3):
                        mm = pe.matmul(ps[0:R, b, :], cT[:, k, cols], wq[:, k, b * 512:(b + 1) * 512],
                                       start=k == 0, stop=k == 2)
                mm.then_inc(q_done, 1)
                for b in range(4):
                    for k in range(2):
                        mm = pe.matmul(ps[0:R, 3 + b, :], cT[:, 3 + k, cols], wkv[:, k, b * 512:(b + 1) * 512],
                                       start=k == 0, stop=k == 1)
                mm.then_inc(kv_done, 1)
                pe.wait_ge(qk_ready, i + 1)
                for n in range(8):
                    if n >= 4:
                        pe.wait_ge(qT_ok, 4 * i + n - 3)
                    for j in range(4):
                        mm = pe.transpose(ps[0:QK, [7, 0, 1, 2][n % 4], j * R:(j + 1) * R],
                                          (q_sb if n < 4 else k_sb)[0:R, 4 * (n % 4) + j, :], ident[0:R, 0:R])
                    mm.then_inc(qk_turned, 1)
            pe.wait_ge(qT_ok, 12)
            pe.wait_ge(kT_ok, 12)
            pe.wait_ge(in_rows, 16 * N_ROWS)

            def scores(hd):
                if hd >= 2:
                    pe.wait_ge(p_exp, hd - 1)
                o = 0
                for i, n in ((0, COL[1]), (1, POS), (2, META)):
                    mm = pe.matmul(ps[0:WID[i], hd % 2, o:o + n], qT[0:QK + MASK_ROWS, hd, COL[i]:COL[i] + WID[i]],
                                   kT[0:QK + MASK_ROWS, hd, 0:n], start=True, stop=True)
                    o += n
                mm.then_inc(s_done, 1)

            def weights(hd):
                pe.wait_ge(p_scaled, hd + 1)
                if hd >= 2:
                    pe.wait_ge(pt_dve, hd - 1)
                    pe.wait_ge(pt_act, hd - 1)
                pr, b = prob[hd % 2], 2 + 2 * (hd % 2)
                o1, o2 = COL[1], COL[1] + POS
                pe.transpose(ps[:, b, 0:P], pr[:, META:META + P], ident)
                pe.transpose(ps[:, b, P:2 * P], pr[:, o1 + META:o1 + META + P], ident)
                pe.transpose(ps[:, b, 2 * P:3 * P], pr[:, o1 + COL[1]:o1 + POS], ident)
                pe.transpose(ps[0:META, b + 1, 0:META], pr[0:META, o2:o2 + META], ident[0:META, 0:META])
                pe.transpose(ps[0:META, b + 1, META:META + P], pr[:, 0:META], ident)
                pe.transpose(ps[0:META, b + 1, META + P:POS], pr[:, o1:o1 + META], ident).then_inc(p_turned, 1)

            def values(hd):
                pe.wait_ge(pt_dve, hd + 1)
                pe.wait_ge(pt_act, hd + 1)
                if hd % 2 == 0 and hd >= 4:
                    pe.wait_ge(o_copied, hd // 2 - 1)
                dst = ps[VD * (hd % 2):VD * (hd % 2) + VD, 6 + hd // 2 % 2, :]
                t = pT[hd % 2]
                pe.matmul(dst[:, 0:POS], vt[:, 2, hd, :], t[:, 3 * P:], start=True, stop=False)
                pe.matmul(dst[:, META:POS], vt[:, 0, hd, :], t[:, 0:2 * P], start=False, stop=False)
                pe.matmul(dst[:, COL[1]:POS], vt[:, 1, hd, :], t[:, 2 * P:3 * P], start=False, stop=True)\
                  .then_inc(pv_done, 1)

            scores(0)
            scores(1)
            for hd in range(HEADS):
                weights(hd)
                if hd + 2 < HEADS:
                    scores(hd + 2)
                if hd:
                    values(hd - 1)
            values(HEADS - 1)
            pe.wait_ge(w_mo, 16)
            pe.wait_ge(o_copied, HEADS // 2)
            project(oT, wmo, 3, mo_done)

        def moe(l):
            nt = NT[l]
            c0 = 0 if nt == 3 else META
            pe.wait_ge(hT_ok, NB[2 * l + 2])
            pe.wait_ge(in_moe, 16 * 11)
            for k in range(KD):
                mm = pe.matmul(ps[0:NG + NE, 5, 0:POS - c0], wr[:, l, k, :], hT[:, k, c0:POS],
                               start=k == 0, stop=k == KD - 1)
            mm.then_inc(lg_done, 1)
            pe.wait_ge(lg_copied, l + 1)
            for i in range(nt):
                mm = pe.transpose(ps[0:WID[i], 6, (NG + NE) * i:(NG + NE) * (i + 1)],
                                  lgT[0:NG + NE, COL[i]:COL[i] + WID[i]], ident[0:NG + NE, 0:NG + NE])
            mm.then_inc(lg_turned, 1)
            pe.wait_ge(sel_ok, l + 1)
            for i in range(nt):
                for j in range(i + 1):
                    mm = pe.matmul(ps[:, 7, NE * i:NE * (i + 1)], before if j == i else ones[:, 0:P], sel[:, j, :],
                                   start=j == 0, stop=j == i)
            for j in range(nt):
                mm = pe.matmul(ps[:, 7, NE * 3:NE * 4], ones[:, 0:P], sel[:, j, :], start=j == 0, stop=j == nt - 1)
            mm.then_inc(rank_done, 1)

            def group(K, n, sent, added):
                pe.wait_ge(K.send, sent)
                pe.wait_ge(K.add, added)
                for k in range(KD):
                    for i in range(nt):
                        mm = pe.matmul(ps[:, k // 4, (k % 4) * P:(k % 4 + 1) * P], xn[:, i, k, :], Sg[:, i, :],
                                       start=i == 0, stop=i == nt - 1)
                mm.then_inc(K.rows, 1)
                for i in range(nt):
                    R = WID[i]
                    mm = pe.transpose(ps[:, 4, COL[i]:COL[i] + R], Gg[0:R, i, :], ident[0:R, 0:R])
                mm.then_inc(K.turn, 1)
                pe.wait_ge(K.rows_in, n + 1)
                for part, w, landed, read in ((0, moeA, K.a, K.a_read), (1, moeB, K.b, K.b_read)):
                    pe.wait_ge(landed, 32 * n + 32)
                    for kk in range(HK):
                        k = part * HK + kk
                        for m in range(2):
                            for j in range(GE):
                                mm = pe.matmul(ps[32 * j:32 * j + 32, 2, m * FE:(m + 1) * FE],
                                               xe[:, k, 32 * j:32 * j + 32], w[:, m, j, kk * FE:(kk + 1) * FE],
                                               start=k == 0 and m == 0, stop=k == KD - 1, skip_group_check=True)
                    mm.then_inc(read, 1)
                pe.wait_ge(K.hid, n + 1)
                for k in range(2):
                    mm = pe.transpose(ps[:, 3, k * P:(k + 1) * P], hid[:, k, :], ident)
                mm.then_inc(K.hid_t, 1)
                pe.wait_ge(K.hid_c, n + 1)
                pe.wait_ge(K.d, 16 * n + 16)
                for k in range(2):
                    for b in range(2):
                        for j in range(GE):
                            mm = pe.matmul(ps[32 * j:32 * j + 32, 5 + b, :], hidT[:, k, 32 * j:32 * j + 32],
                                           moeD[:, j, k * D + b * 512:k * D + (b + 1) * 512], start=k == 0, stop=k == 1)
                mm.then_inc(K.d_read, 1)
                pe.wait_ge(K.turned, n + 1)
                pe.wait_ge(K.ya, n + 1)
                pe.wait_ge(K.yd, n + 1)
                for i in range(nt):
                    for b in range(2):
                        pe.matmul(ps[0:WID[i], COMBINE[2 * i + b], :], GT[:, COL[i]:COL[i] + WID[i]],
                                  ysb[:, b * 512:(b + 1) * 512], start=True, stop=True).then_inc(K.comb, 1)

            late = overflow(pe, l)
            with pe.Fori(0, GROUPS) as g:
                group(FAST, g + GROUPS * l, g + ((GROUPS + 1) * l + 1), 2 * nt * g + (ADD0[l] + 1))
            with pe.If(late):
                with pe.Fori(0, ROUNDS) as r:
                    with pe.Fori(0, GROUPS) as g:
                        n = r * GROUPS + g
                        group(OVER[l], n, n + r + 1, 2 * nt * n + r + 1)

        def gla():
            pe.wait_ge(hT_ok, NB[3])

            def job(j):
                kind, n, _, bank = JOBS[j]
                if before_me[j] is not None:
                    pe.wait_ge(*emptied[before_me[j]])
                b = ps[:, bank, :]
                if kind == "a":
                    if n == 0:
                        pe.wait_ge(*emptied[0])
                    mm = pe.matmul(b[:, 0:POS], wgu[0:GRANK, n * GDK:(n + 1) * GDK], glr[0:GRANK, :], start=True, stop=True)
                elif kind in ("lr", "q", "k"):
                    if kind == "q" and n == 0:
                        pe.wait_ge(w_gqk, 16)
                    o = (n if kind == "q" else GH + n) * GDK
                    c0 = META if kind == "q" else 0
                    for k in range(KD):
                        w = wlr[:, k, :] if kind == "lr" else wqk[:, k, o:o + GDK]
                        mm = pe.matmul(b[0:w.shape[1], 0:POS - c0], w, hT[:, k, c0:POS], start=k == 0, stop=k == KD - 1)
                else:
                    i, hb = divmod(n, 2)
                    if n == 0:
                        pe.wait_ge(w_gv if kind == "v" else w_gr, 16)
                    w = wv if kind == "v" else wrr
                    for k in range(KD):
                        mm = pe.matmul(b[0:WID[i], :], hT[:, k, COL[i]:COL[i] + WID[i]],
                                       w[:, k, hb * 512:(hb + 1) * 512], start=k == 0, stop=k == KD - 1)
                mm.then_inc(g_job, 1)

            for j in range(V_END):
                job(j)
            pe.wait_ge(*emptied[V_END - 1])
            pe.wait_ge(gq_ok, 1)
            for s in range(NSUB):
                t, j = divmod(s, NSUB // 2)
                n = META + SUB * (s + 1)
                if s == NSUB // 2:
                    pe.wait_ge(g_attm, s)
                pe.wait_ge(gk_ok, s + 1)
                for g in range(GH):
                    mm = pe.matmul(ps[32 * j:32 * j + 32, g, 0:n], gqT[:, g, s * SUB:(s + 1) * SUB],
                                   gk[s % 3][:, g, 0:n], start=True, stop=True)
                mm.then_inc(g_att, 1)
                if s < NSUB // 2:
                    job(V_END + s)
            pe.wait_ge(g_attm, NSUB)
            pe.wait_ge(g_dve, counts["dve"])
            for g in range(GH):
                pe.transpose(ps[:, 2 * g, 0:P], att[:, 0, g, META:META + P], ident)
                pe.transpose(ps[:, 2 * g, P:2 * P], att[:, 1, g, META:META + P], ident)
                pe.transpose(ps[:, 2 * g, 2 * P:3 * P], att[:, 1, g, META + P:POS], ident)
                for t in range(2):
                    mm = pe.transpose(ps[0:META, 2 * g + 1, t * P:(t + 1) * P], att[:, t, g, 0:META], ident)
                mm.then_inc(g_attT, 1)
            pe.wait_ge(g_aT_act, GH)
            pe.wait_ge(g_aT_dve, GH)
            for t in range(2):
                for g in range(GH):
                    dst = ps[:, 2 * t + g // 2, (g % 2) * GDV:(g % 2 + 1) * GDV]
                    cols = slice(g * GDV, (g + 1) * GDV)
                    pe.matmul(dst, attM[:, g, t * P:(t + 1) * P], gv[:, 2, cols], start=True, stop=False)
                    mm = pe.matmul(dst, attT[g][:, t * P:(t + 1) * P], gv[:, 0, cols], start=False, stop=t == 0)
                    if t:
                        mm = pe.matmul(dst, attT[g][:, 2 * P:3 * P], gv[:, 1, cols], start=False, stop=True)
                mm.then_inc(g_o, 1)
            for t in range(2):
                pe.wait_ge(g_y, t + 1)
                for k in range(KD):
                    mm = pe.transpose(ps[:, 4 + 2 * t + k // 4, (k % 4) * P:(k % 4 + 1) * P],
                                      gr[:, t, k * P:(k + 1) * P], ident)
                mm.then_inc(g_yT, 1)
            pe.wait_ge(w_go, 16)
            pe.wait_ge(g_yTc, 2)
            project(gyT, wgo, 2, go_done)

        pe.wait_ge(in_c, 16)
        norm(0)
        mla()
        norm(1)
        moe(0)
        norm(2)
        gla()
        norm(3)
        moe(1)

    @block.scalar
    def _(act):
        link = Links(act, act_link)

        def norm(n):
            act.wait_ge(*H_DONE[n])
            nt = NORM_TILES[n]
            for i in range(nt):
                ins = act.activation(xflat[:, i * D:(i + 1) * D], h[:, i, :], ACT.Square, scale=D ** -0.5,
                                     accum_out=ssq[:, i:i + 1])
            link(ins)
            link(act.activation(ssq[:, 0:nt], ssq[:, 0:nt], ACT.Ln, bias=eps_b))
            act.activation(rstd[:, 0:nt], ssq[:, 0:nt], ACT.Exp, scale=-0.5).then_inc(rstd_ok, 1)
            act.wait_ge(rstd_ok, n + 1)
            for i in range(0, nt, 2):
                act.activation(xn[:, i], h[:, i, :].rearrange("p (q k) -> p k q", k=KD), ACT.Copy,
                               scale=rstd[:, i:i + 1]).then_inc(xn_act, 1)

        def mla():
            sqf = flat(sq)
            for i in range(3):
                R = WID[i]
                act.wait_ge(z_done, i + 1)
                ba, bb = (5 + 2 * i) % 8, (6 + 2 * i) % 8
                link(act.copy(kr[0:R, i, :], ps[0:R, bb, KVR:KVR + ROPE]))
                act.activation(sqf[0:R, QR + KVR:QR + KVR + ROPE], kr[0:R, i, :], ACT.Square, scale=QK ** -0.5,
                               accum_out=krs[0:R, i:i + 1]).then_inc(z_kr, 1)
                act.activation(sqf[0:R, 0:QR], ps[0:R, ba, 0:QR], ACT.Square, scale=QR ** -0.5, accum_out=zst[0:R, i, 0:1])
                link(act.activation(sqf[0:R, QR:QR + KVR], ps[0:R, bb, 0:KVR], ACT.Square, scale=KVR ** -0.5,
                                    accum_out=zst[0:R, i, 1:2]))
                link(act.activation(zst[0:R, i, :], zst[0:R, i, :], ACT.Ln, bias=eps_b[0:R]))
                act.activation(zrs[0:R, i, :], zst[0:R, i, :], ACT.Exp, scale=-0.5).then_inc(z_rstd, 1)
            act.wait_ge(z_kr, 3)
            for i in range(3):
                R = WID[i]
                act.wait_ge(q_done, i + 1)
                for b in range(3):
                    ins = act.copy(flat(q_sb)[0:R, b * 512:(b + 1) * 512], ps[0:R, b, :])
                ins.then_inc(q_copied, 1)
                act.wait_ge(q_copied, i + 1)
                act.activation(sq[0:R], q_sb[0:R], ACT.Square, scale=QK ** -0.5).then_inc(q_squared, 1)
                act.wait_ge(kv_done, i + 1)
                for b in range(4):
                    ins = act.copy(vt[0:R, i, 4 * b:4 * b + 4, :],
                                   ps[0:R, 3 + b, :].rearrange("p (h f) -> p h f", h=4)[:, :, NOPE:])
                ins.then_inc(v_copied, 1)
                act.wait_ge(q_sums, i + 1)
                for b in range(4):
                    ins = act.activation(sq[0:R, 4 * b:4 * b + 4, 0:NOPE],
                                         ps[0:R, 3 + b, :].rearrange("p (h f) -> p h f", h=4)[:, :, 0:NOPE],
                                         ACT.Square, scale=QK ** -0.5)
                ins.then_inc(k_squared, 1)
                link(act.activation(qst[0:R, i, :], qst[0:R, i, :], ACT.Ln, scale=float(QK), bias=epsqk_b[0:R]))
                act.activation(scl[0:R, i, :], qst[0:R, i, :], ACT.Exp, scale=-0.5)
                act.wait_ge(k_sums, i + 1)
                link(act.activation(kst[0:R, i, :], kst[0:R, i, :], ACT.Ln, bias=eps_b[0:R]))
                act.activation(krst[0:R, i, :], kst[0:R, i, :], ACT.Exp, scale=-0.5).then_inc(k_rstd, 1)
                for n in range(4):
                    act.wait_ge(qk_turned, 8 * i + n + 1)
                    act.copy(qT[0:QK, 4 * n:4 * n + 4, COL[i]:COL[i] + R],
                             ps[0:QK, [7, 0, 1, 2][n], 0:4 * R].rearrange("p (h t) -> p h t", h=4)).then_inc(qT_ok, 1)

            def exps(hd):
                act.wait_ge(s_shift, hd + 1)
                if hd >= 2:
                    act.wait_ge(p_turned, hd - 1)
                o = 0
                for i, n in ((0, COL[1]), (1, POS), (2, META)):
                    R = WID[i]
                    ins = act.activation(prob[hd % 2][0:R, o:o + n], ps[0:R, hd % 2, o:o + n], ACT.Exp,
                                         bias=nb[hd % 2][0:R, i:i + 1], scale=scl[0:R, i, hd:hd + 1],
                                         accum_out=rs[hd % 2][0:R, i:i + 1])
                    o += n
                ins.then_inc(p_exp, 1)

            def meta_weights(hd):
                act.wait_ge(p_turned, hd + 1)
                if hd >= 2:
                    act.wait_ge(pv_done, hd - 1)
                act.copy(pT[hd % 2][0:META, 3 * P:], ps[0:META, 3 + 2 * (hd % 2), 0:POS]).then_inc(pt_act, 1)

            def heads_out(hp):
                act.wait_ge(pv_done, 2 * hp + 2)
                act.copy(oT[:, hp, :], ps[:, 6 + hp % 2, 0:POS]).then_inc(o_copied, 1)

            act.wait_ge(kT_ok, 12)
            act.wait_ge(zeroed, 13)
            exps(0)
            for hd in range(HEADS):
                if hd + 1 < HEADS:
                    exps(hd + 1)
                meta_weights(hd)
                if hd >= 3 and hd % 2:
                    heads_out((hd - 3) // 2)
            heads_out(HEADS // 2 - 1)

        def moe(l):
            c0 = 0 if NT[l] == 3 else META
            act.wait_ge(lg_done, l + 1)
            act.copy(lgT[0:NG + NE, c0:POS], ps[0:NG + NE, 5, 0:POS - c0]).then_inc(lg_copied, 1)
            act.wait_ge(e_dif, l + 1)
            act.activation(E5[:, 0:NT[l], :], E5[:, 0:NT[l], :], ACT.Exp).then_inc(e_exp, 1)

            def group(K, n):
                act.wait_ge(K.turn, n + 1)
                act.copy(GT[:, c0:POS], ps[:, 4, c0:POS]).then_inc(K.turned, 1)
                act.wait_ge(K.b_read, n + 1)
                act.activation(ex, ps[:, 2, 0:FE], ACT.Exp, scale=-1.0).then_inc(K.exp, 1)
                act.wait_ge(K.hid_t, n + 1)
                act.copy(flat(hidT), ps[:, 3, 0:2 * P]).then_inc(K.hid_c, 1)
                act.wait_ge(K.d_read, n + 1)
                act.copy(ysb[:, 0:512], ps[:, 5, :]).then_inc(K.ya, 1)

            late = overflow(act, l)
            with act.Fori(0, GROUPS) as g:
                group(FAST, g + GROUPS * l)
            with act.If(late):
                with act.Fori(0, ROUNDS) as r:
                    with act.Fori(0, GROUPS) as g:
                        group(OVER[l], r * GROUPS + g)

        def gla():
            def evac(j):
                kind, n, _, bank = JOBS[j]
                act.wait_ge(g_job, j + 1)
                b = ps[:, bank, :]
                if kind == "lr":
                    ins = act.copy(glr[0:GRANK, :], b[0:GRANK, 0:POS])
                elif kind == "q":
                    ins = act.mul(gqT[:, n, :], b[:, 0:SEQ], GDK ** -0.5)
                elif kind == "k":
                    ins = act.copy(gkT[:, n, :], b[:, 0:POS])
                else:
                    i, hb = divmod(n, 2)
                    ins = act.copy(gv[0:WID[i], i, hb * 512:(hb + 1) * 512], b[0:WID[i], :])
                ins.then_inc(g_act, 1)

            mine = [j for j in range(len(JOBS)) if JOBS[j][2] == "act"]
            for j in mine[:5]:
                evac(j)
            act.wait_ge(g_abs, 1)
            link(act.activation(gt, gt, ACT.Exp, scale=-1.0))
            act.activation(gt, gt, ACT.Ln, bias=one_b).then_inc(g_log, 1)
            for j in mine[5:9]:
                evac(j)
            act.wait_ge(gq_dif, 1)
            act.activation(gtq, gtq, ACT.Exp, scale=1.0 / TAU).then_inc(gq_exp, 1)
            act.wait_ge(zeroed, 14)
            rest = mine[9:]
            for s in range(NSUB):
                n = META + SUB * (s + 1)
                act.wait_ge(gk_dif, s + 1)
                act.activation(gk[s % 3][:, :, 0:n], gk[s % 3][:, :, 0:n], ACT.Exp, scale=-1.0 / TAU).then_inc(gk_exp, 1)
                for _ in range(2 if s < 3 else 0):
                    evac(rest.pop(0))
                if s >= 4:
                    n = s - 4
                    act.wait_ge(g_job, V_END + n + 1)
                    act.activation(gr[:, n // 2, (n % 2) * 512:(n % 2 + 1) * 512], ps[:, 4 + n, :],
                                   ACT.Exp, scale=-1.0).then_inc(g_rexp, 1)
            act.wait_ge(zeroed, 15)
            for g in range(GH):
                act.wait_ge(g_attT, g + 1)
                act.copy(attM[0:META, g, :], ps[0:META, 2 * g + 1, 0:SEQ]).then_inc(g_aT_act, 1)
            for t in range(2):
                act.wait_ge(g_o, t + 1)
                for g in range(GH):
                    ins = act.activation(gsq, ps[:, 2 * t + g // 2, (g % 2) * GDV:(g % 2 + 1) * GDV],
                                         ACT.Square, scale=GDV ** -0.5, accum_out=gos[:, t, g:g + 1])
                    link(ins)
                link(act.activation(gos[:, t, :], gos[:, t, :], ACT.Ln, bias=eps_b))
                act.activation(gor[:, t, :], gos[:, t, :], ACT.Exp, scale=-0.5).then_inc(g_orstd, 1)
            for t in range(2):
                act.wait_ge(g_yT, t + 1)
                for b in range(2):
                    ins = act.copy(gyT[:, 4 * b:4 * b + 4, t * P:(t + 1) * P],
                                   ps[:, 4 + 2 * t + b, :].rearrange("p (k q) -> p k q", k=4))
                ins.then_inc(g_yTc, 1)

        act.wait_ge(consts, 3)
        norm(0)
        mla()
        norm(1)
        moe(0)
        norm(2)
        gla()
        norm(3)
        moe(1)

    @block.vector
    def _(dve):
        link = Links(dve, dve_link)
        TT, TS, STT = dve.tensor_tensor, dve.tensor_scalar, dve.scalar_tensor_tensor

        def norm(n):
            dve.wait_ge(rstd_ok, n + 1)
            TS(xn[:, 1], h[:, 1, :].rearrange("p (q k) -> p k q", k=KD), rstd[:, 1:2], None, ALU.mult).then_inc(xn_dve, 1)
            if n == 0:
                dve.wait_ge(in_small, 16 * N_SMALL)
            for i in range(NORM_TILES[n]):
                dve.wait_ge(xn_turned, NB[n] + i + 1)
                cols = slice(COL[i], COL[i] + WID[i])
                if i < 2:
                    for b in range(2):
                        ins = TT(hT[:, 4 * b:4 * b + 4, cols], ps[:, 2 * i + b, :].rearrange("p (k q) -> p k q", k=4),
                                 rep(gn[:, n, 4 * b:4 * b + 4], P), ALU.mult)
                else:
                    ins = TT(hT[:, :, cols], ps[:, 4, 0:KD * META].rearrange("p (k q) -> p k q", k=KD),
                             rep(gn[:, n, :], META), ALU.mult)
                ins.then_inc(hT_ok, 1)

        def mla():
            dve.wait_ge(in_c, 16)
            dve.wait_ge(zeroed, 11)
            cos, sin = (c(n).rearrange("p (t f) -> p t f", t=3) for n in ("cos", "sin"))
            for tab, trig, m in ((tcq, cos, 0), (tsq, sin, 0), (tck, cos, 1), (tsk, sin, 1)):
                TT(tab, trig, over(gqk[:, m, NOPE:], 3), ALU.mult)
            link(TT(gprod[0:NOPE, :], gcol[0:NOPE, 0:1], gcol[0:NOPE, 1:2], ALU.mult))
            H = ROPE // 2
            for i in range(3):
                R = WID[i]
                ba, bb = (5 + 2 * i) % 8, (6 + 2 * i) % 8
                dve.wait_ge(z_rstd, i + 1)
                if i:
                    dve.wait_ge(c_turned, i)
                TS(cq[0:R, 0:3, :], ps[0:R, ba, 0:QR].rearrange("p (q k) -> p k q", k=3), zrs[0:R, i, 0:1], None, ALU.mult)
                TS(cq[0:R, 3:5, :], ps[0:R, bb, 0:KVR].rearrange("p (q k) -> p k q", k=2), zrs[0:R, i, 1:2], None,
                   ALU.mult).then_inc(z_scaled, 1)
                dve.wait_ge(z_kr, i + 1)
                TT(rp[0:R, 0, 0:ROPE], kr[0:R, i, :], tck[0:R, i, :], ALU.mult)
                link(TT(rp[0:R, 1, 0:ROPE], kr[0:R, i, :], tsk[0:R, i, :], ALU.mult))
                TT(kr[0:R, i, 0:H], rp[0:R, 0, 0:H], rp[0:R, 1, H:ROPE], ALU.subtract)
                link(TT(kr[0:R, i, H:ROPE], rp[0:R, 0, H:ROPE], rp[0:R, 1, 0:H], ALU.add))
                dve.wait_ge(c_turned, i + 1)
                cols = slice(COL[i], COL[i] + R)
                TT(cT[:, 0:3, cols], ps[:, 3, 0:3 * R].rearrange("p (k q) -> p k q", k=3), rep(gc5[:, 0:3], R), ALU.mult)
                TT(cT[:, 3:5, cols], ps[:, 4, 0:2 * R].rearrange("p (k q) -> p k q", k=2), rep(gc5[:, 3:5], R),
                   ALU.mult).then_inc(cT_ok, 1)
            ra, rbb = (rp[:, m].rearrange("p (h f) -> p h f", h=HEADS) for m in range(2))
            for i in range(3):
                R = WID[i]
                dve.wait_ge(q_squared, i + 1)
                dve.tensor_reduce(qst[0:R, i, :], sq[0:R], AX.X, ALU.add).then_inc(q_sums, 1)
                x = q_sb[0:R, :, NOPE:QK]
                TT(ra[0:R], x, over(tcq[0:R, i, :], HEADS), ALU.mult)
                link(TT(rbb[0:R], x, over(tsq[0:R, i, :], HEADS), ALU.mult))
                TT(q_sb[0:R, :, NOPE:NOPE + H], ra[0:R, :, 0:H], rbb[0:R, :, H:ROPE], ALU.subtract)
                link(TT(q_sb[0:R, :, NOPE + H:QK], ra[0:R, :, H:ROPE], rbb[0:R, :, 0:H], ALU.add))
                dve.wait_ge(k_squared, i + 1)
                link(dve.tensor_reduce(kst[0:R, i, :], sq[0:R, :, 0:NOPE], AX.X, ALU.add))
                TS(kst[0:R, i, :], kst[0:R, i, :], krs[0:R, i:i + 1], None, ALU.add).then_inc(k_sums, 1)
                dve.wait_ge(k_rstd, i + 1)
                for b in range(4):
                    TT(k_sb[0:R, 4 * b:4 * b + 4, 0:NOPE], ps[0:R, 3 + b, :].rearrange("p (h f) -> p h f", h=4)[:, :, 0:NOPE],
                       rep(krst[0:R, i, 4 * b:4 * b + 4], NOPE), ALU.mult)
                TT(k_sb[0:R, :, NOPE:QK], over(kr[0:R, i, :], HEADS), rep(krst[0:R, i, :], ROPE), ALU.mult).then_inc(qk_ready, 1)
                for n in range(4):
                    dve.wait_ge(qk_turned, 8 * i + 4 + n + 1)
                    TS(kT[0:QK, 4 * n:4 * n + 4, COL[i]:COL[i] + R],
                       ps[0:QK, [7, 0, 1, 2][n], 0:4 * R].rearrange("p (h t) -> p h t", h=4),
                       gprod[0:QK, 0:1], None, ALU.mult).then_inc(kT_ok, 1)

            def shift(hd):
                dve.wait_ge(s_done, hd + 1)
                if hd >= 2:
                    dve.wait_ge(p_exp, hd - 1)
                o = 0
                for i, n in ((0, COL[1]), (1, POS), (2, META)):
                    ins = dve.tensor_reduce(mx[hd % 2][0:WID[i], i:i + 1], ps[0:WID[i], hd % 2, o:o + n], AX.X, ALU.max)
                    o += n
                link(ins)
                STT(nb[hd % 2], mx[hd % 2], -1.0, scl[:, :, hd], ALU.mult, ALU.mult).then_inc(s_shift, 1)

            def scale(hd):
                dve.wait_ge(p_exp, hd + 1)
                link(dve.reciprocal(ri[hd % 2], rs[hd % 2]))
                o = 0
                for i, n in ((0, COL[1]), (1, POS), (2, META)):
                    pr = prob[hd % 2][0:WID[i], o:o + n]
                    ins = TS(pr, pr, ri[hd % 2][0:WID[i], i:i + 1], None, ALU.mult)
                    o += n
                ins.then_inc(p_scaled, 1)

            def frame_weights(hd):
                dve.wait_ge(p_turned, hd + 1)
                if hd >= 2:
                    dve.wait_ge(pv_done, hd - 1)
                dve.tensor_copy(pT[hd % 2][:, 0:3 * P], ps[:, 2 + 2 * (hd % 2), 0:3 * P]).then_inc(pt_dve, 1)

            shift(0)
            for hd in range(HEADS):
                if hd + 1 < HEADS:
                    shift(hd + 1)
                scale(hd)
                if hd:
                    frame_weights(hd - 1)
            frame_weights(HEADS - 1)
            for i in range(3):
                for b in range(2):
                    dve.wait_ge(mo_done, 2 * i + b + 1)
                    hh = h[0:WID[i], i, b * 512:(b + 1) * 512]
                    TT(hh, hh, ps[0:WID[i], 2 * i + b, :], ALU.add).then_inc(mo_add, 1)

        def route(l):
            nt = NT[l]
            V = slice(0, nt)
            first = c("first")
            dve.wait_ge(lg_turned, l + 1)
            W = NG + NE
            src = ps[:, 6, 0:nt * W].rearrange("p (t n) -> p t n", t=nt)
            ins = TT(L[:, 0:2, :], src[:, 0:2, :], over(rb[:, l, :], 2), ALU.add)
            if nt == 3:
                ins = TT(L[0:META, 2, :], src[0:META, 2, :], rb[0:META, l, :], ALU.add)
            link(ins)

            def choose(x, best, out):
                n = x.shape[2]
                link(TT(out, x, rep(best, n), ALU.is_equal))
                link(TT(out, out, over(first[:, NE - n:], nt), ALU.mult))
                link(dve.tensor_reduce(pm[:, V], out, AX.X, ALU.max))
                link(TT(out, out, rep(pm[:, V], n), ALU.is_equal))

            lg, lx = L[:, V, 0:NG], L[:, V, NG:]
            link(dve.tensor_reduce(mg[:, V], lg, AX.X, ALU.max))
            TT(E5[:, V, 0:NG], lg, rep(mg[:, V], NG), ALU.subtract)
            choose(lg, mg[:, V], g4[:, V, :])
            link(TS(g4[:, V, :], g4[:, V, :], BIG, -BIG, ALU.mult, ALU.add))
            link(TT(le[:, V, :].rearrange("p t (g e) -> p t g e", g=NG), lx.rearrange("p t (g e) -> p t g e", g=NG),
                    rep3(g4[:, V, :], EPG), ALU.add))
            link(dve.tensor_reduce(m1[:, V], le[:, V, :], AX.X, ALU.max))
            choose(le[:, V, :], m1[:, V], s1[:, V, :])
            link(STT(le[:, V, :], s1[:, V, :], -3 * BIG, le[:, V, :], ALU.mult, ALU.add))
            link(dve.tensor_reduce(m2[:, V], le[:, V, :], AX.X, ALU.max))
            TT(E5[:, V, NG:], rep(m2[:, V], 1), rep(m1[:, V], 1), ALU.subtract).then_inc(e_dif, 1)
            choose(le[:, V, :], m2[:, V], s2[:, V, :])
            link(TT(sel[:, V, :], s1[:, V, :], s2[:, V, :], ALU.add))
            TT(sel[:, V, :], sel[:, V, :], rep(c("valid")[:, V], NE), ALU.mult).then_inc(sel_ok, 1)
            dve.wait_ge(e_exp, l + 1)
            link(dve.tensor_reduce(mg[:, V], E5[:, V, 0:NG], AX.X, ALU.add))
            e2 = E5[:, V, NG:].rearrange("p t o -> p (t o)")
            link(STT(m1[:, V], e2, 1.0, mg[:, V], ALU.add, ALU.mult))
            link(dve.reciprocal(w1[:, V], m1[:, V]))
            link(TT(w2[:, V], w1[:, V], e2, ALU.mult))
            TT(s1[:, V, :], s1[:, V, :], rep(w1[:, V], NE), ALU.mult)
            link(TT(s2[:, V, :], s2[:, V, :], rep(w2[:, V], NE), ALU.mult))
            TT(gates[:, V, 0:NE], s1[:, V, :], s2[:, V, :], ALU.add).then_inc(FAST.add, 1)
            dve.wait_ge(rank_done, l + 1)
            link(dve.tensor_reduce(most[0:1], ps[0:1, 7, 3 * NE:4 * NE], AX.X, ALU.max))
            TS(flag[0:1, l:l + 1], most[0:1], float(SLOTS), None, ALU.is_gt).then_inc(flag_ok, 1)
            link(STT(rm[:, V, 0:NE], sel[:, V, :], -OFF, ps[:, 7, 0:nt * NE].rearrange("p (t n) -> p t n", t=nt),
                     ALU.mult, ALU.add))

        def moe(l):
            route(l)
            nt, norm_n = NT[l], 2 * l + 1

            def dispatch(K, e0, lk):
                s4, g4_ = (t[:, 0:nt, :].rearrange("p t (e s) -> p t e s", e=GE) for t in (Sg, Gg))
                slot = c("slot").unsqueeze(1).unsqueeze(1).to_broadcast([P, nt, GE, SLOTS])
                lk(TT(s4, slot, rep3(rm[:, 0:nt, e0], SLOTS), ALU.is_equal))
                TT(g4_, s4, rep3(gates[:, 0:nt, e0], SLOTS), ALU.mult).then_inc(K.send, 1)

            def group(K, n, g, base, combined):
                lk = Links(dve, K.step)
                lk.base = base
                dve.wait_ge(K.rows, n + 1)
                for b in range(2):
                    ins = TT(xe[:, 4 * b:4 * b + 4, :], ps[:, b, :].rearrange("p (k q) -> p k q", k=4),
                             rep(gn[:, norm_n, 4 * b:4 * b + 4], P), ALU.mult)
                ins.then_inc(K.rows_in, 1)
                dve.wait_ge(K.turn, n + 1)
                dispatch(K, bass.ds(GE * g + GE, GE), lk)
                dve.wait_ge(K.exp, n + 1)
                lk(TS(den, ex, 1.0, None, ALU.add))
                lk(dve.reciprocal(den, den))
                lk(TT(den, den, ps[:, 2, 0:FE], ALU.mult))
                TT(hid.rearrange("p k q -> p q k"), den.rearrange("p (q k) -> p q k", k=2),
                   ps[:, 2, FE:2 * FE].rearrange("p (q k) -> p q k", k=2), ALU.mult).then_inc(K.hid, 1)
                dve.wait_ge(K.d_read, n + 1)
                dve.tensor_copy(ysb[:, 512:], ps[:, 6, :]).then_inc(K.yd, 1)
                for i in range(nt):
                    for b in range(2):
                        dve.wait_ge(K.comb, combined + (2 * i + b + 1))
                        hh = h[0:WID[i], i, b * 512:(b + 1) * 512]
                        TT(hh, hh, ps[0:WID[i], COMBINE[2 * i + b], :], ALU.add).then_inc(K.add, 1)
                assert lk.n == LOOP_LINKS

            K = FAST
            dispatch(K, slice(0, GE), link)
            with dve.Fori(0, GROUPS) as g:
                group(K, g + GROUPS * l, g, (g + GROUPS * l) * LOOP_LINKS, g * (2 * nt) + COMB0[l])
            with dve.If(overflow(dve, l)):
                K = OVER[l]
                with dve.Fori(0, ROUNDS) as r:
                    opened = r * (2 * nt * GROUPS + 1) + 1
                    TS(flat(rm), flat(rm), -float(SLOTS), None, ALU.add).then_inc(K.add, 1)
                    dve.wait_ge(K.add, opened)
                    lk = Links(dve, K.step)
                    per = GROUPS * LOOP_LINKS + 1
                    lk.base = r * per
                    dispatch(K, slice(0, GE), lk)
                    with dve.Fori(0, GROUPS) as g:
                        n = r * GROUPS + g
                        group(K, n, g, r * per + g * LOOP_LINKS + 1, n * (2 * nt))
            dve.memset(marker[0:1, l:l + 1], 0.0).then_inc(moe_done, 1)

        def gla():
            mine = [j for j in range(len(JOBS)) if JOBS[j][2] == "dve"]
            for j in mine[:4]:
                _, n, _, bank = JOBS[j]
                dve.wait_ge(g_job, j + 1)
                TS(ga[:, n, :], ps[:, bank, 0:POS], bg[:, n:n + 1], None, ALU.add).then_inc(g_dve, 1)
            dve.wait_ge(g_dve, 4)
            STT(flat(gt), flat(ga), -1.0, flat(ga), ALU.mult, ALU.max).then_inc(g_abs, 1)
            dve.wait_ge(g_log, 1)
            link(STT(flat(ga), flat(ga), 0.0, flat(gt), ALU.min, ALU.subtract))
            for g in range(GH):
                ins = dve.tensor_tensor_scan(gb[:, g, :], ones, ga[:, g, :], 0.0, ALU.mult, ALU.add)
            link(ins)
            blocks = gb[:, :, META:POS].rearrange("p g (s j) -> p g s j", s=NSUB)
            ref = blocks[:, :, :, SUB // 2 - 1:SUB // 2]
            tq4 = gtq.rearrange("p g (s j) -> p g s j", s=NSUB)
            TT(tq4, blocks, ref.to_broadcast([P, GH, NSUB, SUB]), ALU.subtract).then_inc(gq_dif, 1)

            def dif(s):
                n = META + SUB * (s + 1)
                if s >= 3:
                    dve.wait_ge(g_att, s - 2)
                TT(gk[s % 3][:, :, 0:n], gb[:, :, 0:n], ref[:, :, s, :].to_broadcast([P, GH, n]), ALU.subtract)\
                    .then_inc(gk_dif, 1)

            def mul(s):
                n = META + SUB * (s + 1)
                dve.wait_ge(gk_exp, s + 1)
                v = gk[s % 3][:, :, 0:n]
                TT(v, v, gkT[:, :, 0:n], ALU.mult).then_inc(gk_ok, 1)

            def masked(s):
                t, j = divmod(s, NSUB // 2)
                n = META + SUB * (s + 1)
                rows = slice(32 * j, 32 * j + 32)
                dve.wait_ge(g_att, s + 1)
                TT(att[rows, t, :, 0:n], ps[rows, 0:GH, 0:n],
                   over(c("causal")[rows, t * POS:t * POS + n], GH), ALU.mult).then_inc(g_attm, 1)

            dif(0)
            dve.wait_ge(gq_exp, 1)
            TT(gqT, gqT, gtq, ALU.mult).then_inc(gq_ok, 1)
            dif(1)
            dve.wait_ge(zeroed, 16)
            for s in range(NSUB):
                mul(s)
                if s >= 1:
                    masked(s - 1)
                if s + 2 < NSUB:
                    dif(s + 2)
            masked(NSUB - 1)
            for n in range(4):
                dve.wait_ge(g_rexp, n + 1)
                v = gr[:, n // 2, (n % 2) * 512:(n % 2 + 1) * 512]
                link(TS(v, v, 1.0, None, ALU.add))
                link(dve.reciprocal(v, v))
                TT(v, v, ps[:, 4 + n, :], ALU.mult).then_inc(g_dve, 1)
                dve.wait_ge(g_dve, 4 + n + 1)
                v2 = v.rearrange("p (g f) -> p g f", g=2)
                link(TT(v2, v2, over(gout[:, :], 2), ALU.mult))
            for g in range(GH):
                dve.wait_ge(g_attT, g + 1)
                dve.tensor_copy(attT[g], ps[:, 2 * g, 0:3 * P]).then_inc(g_aT_dve, 1)
            for t in range(2):
                dve.wait_ge(g_orstd, t + 1)
                for g in range(GH):
                    v = gr[:, t, g * GDV:(g + 1) * GDV]
                    ins = STT(v, ps[:, 2 * t + g // 2, (g % 2) * GDV:(g % 2 + 1) * GDV], gor[:, t, g:g + 1], v,
                              ALU.mult, ALU.mult)
                ins.then_inc(g_y, 1)
            for i in range(2):
                for b in range(2):
                    dve.wait_ge(go_done, 2 * i + b + 1)
                    hh = h[:, i, b * 512:(b + 1) * 512]
                    TT(hh, hh, ps[:, 2 * i + b, :], ALU.add).then_inc(go_add, 1)

        dve.wait_ge(in_h, 48)
        norm(0)
        mla()
        norm(1)
        moe(0)
        norm(2)
        gla()
        norm(3)
        moe(1)


NAMES = ["x", "meta_tokens", "norm_mix", "norm_ffn", "mla_w_in", "mla_g_q", "mla_w_uq", "mla_g_kv", "mla_w_ukv",
         "mla_g_qn", "mla_g_kn", "mla_w_o", "gla_w_in", "gla_w_gate_up", "gla_b_gate", "gla_g_out", "gla_w_o",
         "moe_w_rg", "moe_b_rg", "moe_w_re", "moe_b_re", "moe_w_gate", "moe_w_up", "moe_w_down"]


def kernel(**inputs):
    import concourse.bacc as bacc
    from concourse.bass_utils import run_bass_kernel_spmd

    nc = bacc.Bacc("TRN2", target_bir_lowering=False, num_devices=1)
    table, rows, _ = constants()
    arrays = {n: np.ascontiguousarray(inputs[n]) for n in NAMES}
    arrays["const"], arrays["mask_rows"] = table, rows
    aps = {n: nc.dram_tensor(f"in_{n}", v.shape, F32, kind="ExternalInput").ap() for n, v in arrays.items()}
    out = nc.dram_tensor("out_0", (1, SEQ, D), F32, kind="ExternalOutput").ap()
    program(nc, aps, out)
    r = run_bass_kernel_spmd(nc, [{f"in_{n}": v for n, v in arrays.items()}], core_ids=[0])
    return r.results[0]["out_0"]
```

```python
from contextlib import ExitStack

import numpy as np

import concourse.bass as bass
from concourse import mybir

F32 = mybir.dt.float32
BF16 = mybir.dt.bfloat16
I32 = mybir.dt.int32
ALU = mybir.AluOpType
ACT = mybir.ActivationFunctionType
AX = mybir.AxisListType

P = 128
D = 1024
KD = D // P
SEQ, META = 256, 16
POS = META + SEQ
CHUNK = 64
COL = [META, META + P, 0]
WID = [P, P, META]
QUAD = 32
EPS = 1e-6

HEADS, NOPE, ROPE, VD = 16, 64, 32, 64
MH = HEADS // 4
QK = NOPE + ROPE
QR, KVR = 384, 256
ZA, ZB = QR, KVR + ROPE
MASK_ROWS = 2
BIG = 1e30

GH, GDK, GDV, GRANK, TAU = 4, 128, 256, 16, 16.0
SUB = 32
NSUB = SEQ // SUB

NG, EPG, NE, FE = 4, 8, 32, 256
SLOTS = 32
GE = 4
GROUPS = NE // GE
OFF = 1000.0
COMBINE = [0, 1, 7, 3, 4, 2]
LOOP_LINKS = 1
ROUNDS = -(-POS // SLOTS) - 1


def constants():
    parts, at, w = [], {}, 0

    def put(name, a):
        nonlocal w
        full = np.zeros((P, a.shape[1]), np.float32)
        full[:a.shape[0]] = a
        parts.append(full)
        at[name] = (w, w + a.shape[1])
        w += a.shape[1]

    pr = np.arange(P)
    put("ident", np.eye(P))
    put("before", (pr[:, None] < pr[None, :]).astype(np.float32))
    put("ones", np.ones((P, POS)))
    put("slot", np.tile(np.arange(SLOTS) - OFF, (P, 1)))
    put("first", np.tile(np.arange(NE, 0, -1), (P, 1)))
    valid = np.ones((P, 3))
    valid[META:, 2] = 0
    put("valid", valid)
    col = np.arange(POS)
    put("causal", np.concatenate([(col[None, :] <= (COL[i] + pr)[:, None]) for i in (0, 1)], 1))
    half = ROPE // 2
    inv = 1.0 / (np.float32(10000.0) ** (np.arange(half, dtype=np.float32) / np.float32(half)))
    pos = np.stack([COL[0] + pr, COL[1] + pr, np.minimum(pr % QUAD, META - 1)], 1).astype(np.float32)
    ang = (pos[:, :, None] * inv.astype(np.float32)).astype(np.float32)
    cos, sin = np.cos(ang), np.sin(ang)
    put("cos", np.concatenate([cos, cos], 2).reshape(P, -1))
    put("sin", np.concatenate([sin, sin], 2).reshape(P, -1))
    cid = np.where(col < META, 0, 1 + (col - META) // CHUNK)
    rows = np.zeros((2, MASK_ROWS, POS), np.float32)
    for m in range(MASK_ROWS):
        rows[0, m] = cid == 2 * m + 1
        rows[1, m] = np.where(cid == 2 * m + 2, -BIG, 0.0)
    return np.ascontiguousarray(np.concatenate(parts, 1), dtype=np.float32), rows, at


class Links:

    def __init__(self, eng, sem):
        self.eng, self.sem, self.n, self.base = eng, sem, 0, 0

    def __call__(self, ins):
        self.n += 1
        ins.then_inc(self.sem, 1)
        self.eng.wait_ge(self.sem, self.base + self.n)


def program(nc, a, out):
    with ExitStack() as ctx:
        build(nc, a, out, ctx)


def build(nc, a, out, ctx):
    def sb(name, shape, dt=F32):
        return ctx.enter_context(nc.sbuf_tensor(name, shape, dt))

    def sem(name):
        return ctx.enter_context(nc.semaphore(name))

    _, _, at = constants()
    CW = max(e for _, e in at.values())

    cst = sb("cst", [P, CW])

    def c(name):
        return cst[:, at[name][0]:at[name][1]]

    ident, before, ones = c("ident"), c("before"), c("ones")
    h = sb("h", [P, 3, D])
    xn = sb("xn", [P, 3, KD, P])
    hT = sb("hT", [P, KD, POS])
    PART = 8192
    ring = sb("ring", [P, 3 * PART])
    RA, RB, RD = (ring[:, i * PART:(i + 1) * PART] for i in range(3))
    gn = sb("gn", [P, 4, KD])
    flag = sb("flag", [1, 2], I32)
    marker = sb("marker", [1, 2])
    ssq = sb("ssq", [P, 3])
    rstd = sb("rstd", [P, 3])
    fix = sb("fix", [P, 3])
    eps_b, epsqk_b, one_b = (fix[:, i:i + 1] for i in range(3))
    wr = sb("wr", [P, 2, KD, NG + NE])
    rb = sb("rb", [P, 2, NG + NE])
    wlr = sb("wlr", [P, KD, GRANK])
    wgu = sb("wgu", [P, GH * GDK])
    bg = sb("bg", [P, GH])
    gout = sb("gout", [P, GDV // P])
    before01, ones01 = (sb(n, [P, P], BF16)[:, :] for n in ("before01", "ones01"))
    sel01 = sb("sel01", [P, 3, NE], BF16)
    ARENA = 17300
    arena = sb("arena", [P, ARENA])
    top = [0]

    def take(*shape):
        n = int(np.prod(shape))
        assert top[0] + n <= ARENA, (top[0], n)
        v = arena[:, top[0]:top[0] + n]
        top[0] += n
        if len(shape) == 2:
            v = v.rearrange("p (a b) -> p a b", a=shape[0])
        if len(shape) == 3:
            v = v.rearrange("p (a b c) -> p a b c", a=shape[0], b=shape[1])
        return v

    L = take(3, NG + NE)
    E5 = take(3, NG + 1)
    le, s1, s2, sel = (take(3, NE) for _ in range(4))
    rm, gates = take(3, NE + GE), take(3, NE + GE)
    mg, m1, m2, pm, w1, w2 = (take(3) for _ in range(6))
    g4 = take(3, NG)
    most = take(1)
    lgT = take(POS)
    shared = top[0]
    Sg, Gg = take(3, GE * SLOTS), take(3, GE * SLOTS)
    xe = take(KD, P)
    ex = take(FE)
    hid, hidT = take(2, P), take(2, P)
    GT = take(POS)
    ysb = take(D)
    top[0] = shared
    vt = take(3, HEADS, VD)
    qT, kT = take(HEADS, POS), take(HEADS, POS)
    zst, zrs = take(3, 2), take(3, 2)
    junk = take(QR + KVR)
    kr, krs = take(3, ROPE), take(3)
    tcq, tsq, tck, tsk = (take(3, ROPE) for _ in range(4))
    gqk = take(2, QK)
    gcol, gprod, gc5 = take(2), take(1), take(5)
    qst, kst, scl, krst = (take(3, HEADS) for _ in range(4))
    mx, rs, nb, ri = ([take(2), take(2)] for _ in range(4))
    mmx, mri = take(MH), take(MH)
    mp = take(MH, META)
    mpT = take(HEADS, META)
    att_top = top[0]
    cT = take(5, POS)
    rp = take(2, HEADS * ROPE)
    top[0] = att_top
    PR = COL[1] + POS
    prob = [take(PR), take(PR)]
    pT = [take(3 * P), take(3 * P)]
    pM = [take(SEQ), take(SEQ)]
    oT = hT
    xflat = xn[:, :, :, :].rearrange("p a k q -> p (a k q)")

    def heads(ap, n=HEADS):
        return ap.rearrange("p (h f) -> p h f", h=n)

    QW = HEADS * QK
    q_sb = [heads(xflat[:, 0:QW]), heads(ring[:, 0:QW]), heads(ring[:, 2 * QW:2 * QW + MH * QK], MH)]
    k_sb = [heads(xflat[:, QW:2 * QW]), heads(ring[:, QW:2 * QW]),
            heads(ring[:, 2 * QW + MH * QK:2 * QW + 2 * MH * QK], MH)]
    o_sq = 2 * QW + 2 * MH * QK
    sq = heads(ring[:, o_sq:o_sq + QW])
    top[0] = shared
    gqT = take(GH, SEQ)
    gkT = take(GH, POS)
    ga, gb, gt = take(GH, POS), take(GH, POS), take(GH, POS)
    gv = take(3, GH * GDV)
    gr = take(2, D)
    gk = [take(GH, POS) for _ in range(3)]
    glr = take(POS)
    gos, gor = take(2, GH), take(2, GH)
    attM = take(GH, SEQ)
    gtq = gt[:, :, 0:SEQ]
    gsq = xflat[:, 2 * GH * POS:2 * GH * POS + GDV]
    att = xflat[:, 0:2 * GH * POS].rearrange("p (t g s) -> p t g s", t=2, g=GH)
    attT = [w.rearrange("p a b -> p (a b)")[:, o:o + 3 * P] for w in (ga, gt) for o in (0, 3 * P)]
    gyT = hT[:, :, META:]

    ps = ctx.enter_context(nc.psum_tensor("ps", [P, 8, 512], F32))

    names = """in_h in_c in_small in_moe in_rows w_z w_q w_kv w_mo w_gqk w_gv w_gr w_go
        act_link dve_link zeroed consts tables01
        rstd_ok xn_act xn_dve xn_turned hT_ok
        z_done z_rstd z_kr z_scaled c_turned cT_ok tabs_ok
        a_job a_act a_dve q_squared k_squared q_sums k_sums k_rstd qk_ready
        mq_s mq_dif mq_exp mq_p mq_t mq_c
        s_done s_shift p_exp p_scaled p_turned pt_act pt_dve pv_done o_copied mo_done mo_add
        g_job g_act g_dve g_abs g_log gq_dif gq_exp gq_ok gk_dif gk_exp gk_ok g_att g_attm
        g_attT g_aT_act g_aT_dve g_o g_orstd g_y g_yT g_yT_act g_yT_dve go_done go_add
        lg_done lg_copied lg_turned e_dif e_exp sel_ok rank_done count_done
        flag_ok moe_done stored"""
    S = {n: sem(n) for n in names.split()}
    (in_h, in_c, in_small, in_moe, in_rows, w_z, w_q, w_kv, w_mo, w_gqk, w_gv, w_gr, w_go,
     act_link, dve_link, zeroed, consts, tables01,
     rstd_ok, xn_act, xn_dve, xn_turned, hT_ok,
     z_done, z_rstd, z_kr, z_scaled, c_turned, cT_ok, tabs_ok,
     a_job, a_act, a_dve, q_squared, k_squared, q_sums, k_sums, k_rstd, qk_ready,
     mq_s, mq_dif, mq_exp, mq_p, mq_t, mq_c,
     s_done, s_shift, p_exp, p_scaled, p_turned, pt_act, pt_dve, pv_done, o_copied, mo_done, mo_add,
     g_job, g_act, g_dve, g_abs, g_log, gq_dif, gq_exp, gq_ok, gk_dif, gk_exp, gk_ok, g_att, g_attm,
     g_attT, g_aT_act, g_aT_dve, g_o, g_orstd, g_y, g_yT, g_yT_act, g_yT_dve, go_done, go_add,
     lg_done, lg_copied, lg_turned, e_dif, e_exp, sel_ok, rank_done, count_done,
     flag_ok, moe_done, stored) = S.values()

    class GroupSems:

        def __init__(self, tag):
            self.a, self.b, self.d = sem(f"{tag}_a"), sem(f"{tag}_b"), sem(f"{tag}_d")
            self.a_read, self.b_read, self.d_read = sem(f"{tag}_a_read"), sem(f"{tag}_b_read"), sem(f"{tag}_d_read")
            self.send = sem(f"{tag}_send")
            self.rows = sem(f"{tag}_rows")
            self.rows_in = sem(f"{tag}_rows_in")
            self.turn = sem(f"{tag}_turn")
            self.turned = sem(f"{tag}_turned")
            self.silu = sem(f"{tag}_silu")
            self.hid = sem(f"{tag}_hid")
            self.hid_t = sem(f"{tag}_hid_t")
            self.hid_c = sem(f"{tag}_hid_c")
            self.ya, self.yd = sem(f"{tag}_ya"), sem(f"{tag}_yd")
            self.comb = sem(f"{tag}_comb")
            self.add = sem(f"{tag}_add")
            self.step = sem(f"{tag}_step")
            self.seen = sem(f"{tag}_seen")

    FAST = GroupSems("fast")
    OVER = [GroupSems(f"over{l}") for l in range(2)]

    def rep(ap, n):
        return ap.unsqueeze(2).to_broadcast([ap.shape[0], ap.shape[1], n])

    def rep3(ap, n):
        return ap.unsqueeze(3).to_broadcast([*ap.shape, n])

    def over(ap, n):
        return ap.unsqueeze(1).to_broadcast([ap.shape[0], n, ap.shape[1]])

    def flat(ap):
        return ap.rearrange("p a b -> p (a b)")

    NT = [3, 2]
    COMB0 = [0, 2 * NT[0] * GROUPS]
    ADD0 = [0, 2 * NT[0] * GROUPS + 1]
    NORM_TILES = [3, 3, 3, 2]
    NB = [sum(NORM_TILES[:i]) for i in range(5)]
    ORDER = [[0, 1, 2], [2, 0, 1], [0, 1, 2], [0, 1]]
    H_DONE = [{0: (in_h, 48), 1: (in_h, 48), 2: (in_h, 48)}, {2: (mo_add, 4), 0: (mo_add, 6), 1: (mo_add, 8)},
              {0: (moe_done, 1), 1: (moe_done, 1), 2: (moe_done, 1)}, {0: (go_add, 2), 1: (go_add, 4)}]
    N_SMALL, N_ROWS = 11, 2 * MASK_ROWS

    wz = ring[:, 0:KD * (ZA + ZB)].rearrange("p (k n) -> p k n", k=KD)
    o_q = KD * (ZA + ZB)
    wq = ring[:, o_q:o_q + 3 * HEADS * QK].rearrange("p (k n) -> p k n", k=3)
    o_kv = o_q + 3 * HEADS * QK
    wkv = ring[:, o_kv:o_kv + 2 * HEADS * (NOPE + VD)].rearrange("p (k n) -> p k n", k=2)
    o_cq = o_kv + 2 * HEADS * (NOPE + VD)
    cq = [ring[:, o_cq + i * 5 * P:o_cq + (i + 1) * 5 * P].rearrange("p (k q) -> p k q", k=5) for i in range(3)]
    assert o_sq + QW <= o_q and o_cq + 15 * P <= 2 * PART
    wmo, wqk, wv, wrr, wgo = (r.rearrange("p (k n) -> p k n", k=KD) for r in (RD, RA, RB, RD, RA))
    HK = KD // 2
    moeA, moeB = (r.rearrange("p (m e n) -> p m e n", m=2, e=GE) for r in (RA, RB))
    moeD = RD.rearrange("p (e n) -> p e n", e=GE)
    VO = 2 * GH * GDK
    LRO = VO + GH * GDV
    RO = LRO + GRANK

    AJOBS = []
    for i in range(3):
        AJOBS += [("q", i, n, "act") for n in range(3 if i < 2 else 1)]
        AJOBS += [("kv", i, n, "dve") for n in range(4 if i < 2 else 1)]
    for i in range(3):
        AJOBS += [("tq", i, n, "act") for n in range(4 if i < 2 else 1)]
        AJOBS += [("tk", i, n, "dve") for n in range(4 if i < 2 else 1)]
    a_counts = {"act": 0, "dve": 0}
    a_empty = []
    for *_, who in AJOBS:
        a_counts[who] += 1
        a_empty.append(({"act": a_act, "dve": a_dve}[who], a_counts[who]))

    def ajobs(kind, i):
        return [j for j, (k, t, _, _) in enumerate(AJOBS) if (k, t) == (kind, i)]

    JOBS = [("lr", 0, "act", 0)] + [("q", n, "act", 1 + n) for n in range(GH)]
    JOBS += [("a", n, "dve", (5 + n) % 8) for n in range(GH)] + [("k", n, "act", 1 + n) for n in range(GH)]
    JOBS += [("v", n, "act", (5 + n) % 8) for n in range(5)] + [("r", n, "act", 4 + n) for n in range(4)]
    counts = {"act": 0, "dve": 0}
    emptied = []
    for _, _, who, _ in JOBS:
        counts[who] += 1
        emptied.append(({"act": g_act, "dve": g_dve}[who], counts[who]))
    before_me = [max((i for i in range(j) if JOBS[i][3] == JOBS[j][3]), default=None) for j in range(len(JOBS))]
    K_END, V_END, R_END = 13, 18, 22

    BY_ACT = [(n, i) for n in range(4) for i in ORDER[n] if i or n % 2]
    RSTD = [(n, i) for n in range(4) for i in ORDER[n] if not i or n % 2]

    def xn_ready(n, i):
        return (xn_act, BY_ACT.index((n, i)) + 1) if (n, i) in BY_ACT else (xn_dve, n // 2 + 1)

    def rstd_count(n, i):
        return RSTD.index((n, i)) + 1

    block = ctx.enter_context(nc.Block())

    def overflow(eng, l):
        eng.wait_ge(flag_ok, l + 1)
        return eng.value_load(flag[0:1, l:l + 1], min_val=0, max_val=1) != 0

    @block.sync
    def _(sp):
        sp.dma_start(h[:, 0, :], a["x"][0, 0:P, :]).then_inc(in_h, 16)
        sp.dma_start(h[:, 1, :], a["x"][0, P:SEQ, :]).then_inc(in_h, 16)
        sp.wait_ge(zeroed, 1)
        sp.dma_start(h[0:META, 2, :], a["meta_tokens"]).then_inc(in_h, 16)
        sp.dma_start(cst[:, :], a["const"]).then_inc(in_c, 16)
        with nc.allow_non_contiguous_dma(reason="gains, a column per block"):
            for n in range(4):
                src = a["norm_mix" if n % 2 == 0 else "norm_ffn"][n // 2]
                sp.dma_start(gn[:, n, :], src.rearrange("(p k) -> p k", k=KD)).then_inc(in_small, 16)
            sp.dma_start(gc5[:, 0:3], a["mla_g_q"][0].rearrange("(p k) -> p k", k=3)).then_inc(in_small, 16)
            sp.dma_start(gc5[:, 3:5], a["mla_g_kv"][0].rearrange("(p k) -> p k", k=2)).then_inc(in_small, 16)
            sp.dma_start(gcol[0:NOPE, 0:1], a["mla_g_qn"][0, 0:NOPE].rearrange("(p o) -> p o", o=1)).then_inc(in_small, 16)
            sp.dma_start(gcol[0:NOPE, 1:2], a["mla_g_kn"][0, 0:NOPE].rearrange("(p o) -> p o", o=1)).then_inc(in_small, 16)
            sp.dma_start(bg[:, :], a["gla_b_gate"][0].rearrange("(g p) -> p g", p=P)).then_inc(in_small, 16)
        sp.dma_start(gqk[:, 0, :], a["mla_g_qn"].to_broadcast([P, QK])).then_inc(in_small, 16)
        sp.dma_start(gqk[:, 1, :], a["mla_g_kn"].to_broadcast([P, QK])).then_inc(in_small, 16)
        sp.dma_start(wz, a["mla_w_in"][0].rearrange("(p k) n -> p k n", k=KD)).then_inc(w_z, 16)
        sp.dma_start(wq, a["mla_w_uq"][0].rearrange("(p k) n -> p k n", k=3)).then_inc(w_q, 16)
        sp.dma_start(wkv, a["mla_w_ukv"][0].rearrange("(p k) n -> p k n", k=2)).then_inc(w_kv, 16)
        for m, t in ((0, qT), (1, kT)):
            for r in range(MASK_ROWS):
                sp.dma_start(t[QK + r:QK + r + 1, :, :],
                             a["mask_rows"][m, r:r + 1].unsqueeze(1).to_broadcast([1, HEADS, POS])).then_inc(in_rows, 16)
        sp.dma_start(wmo, a["mla_w_o"][0].rearrange("(k p) n -> p k n", p=P)).then_inc(w_mo, 16)
        for l in range(2):
            sp.dma_start(wr[:, l, :, 0:NG], a["moe_w_rg"][l].rearrange("(p k) n -> p k n", k=KD)).then_inc(in_moe, 16)
            sp.dma_start(wr[:, l, :, NG:], a["moe_w_re"][l].rearrange("(p k) n -> p k n", k=KD)).then_inc(in_moe, 16)
            sp.dma_start(rb[:, l, 0:NG], a["moe_b_rg"][l:l + 1].to_broadcast([P, NG])).then_inc(in_moe, 16)
            sp.dma_start(rb[:, l, NG:], a["moe_b_re"][l:l + 1].to_broadcast([P, NE])).then_inc(in_moe, 16)
        sp.dma_start(wlr[:, :, :], a["gla_w_in"][0].rearrange("(p k) n -> p k n", k=KD)[:, :, LRO:RO]).then_inc(in_moe, 16)
        sp.dma_start(wgu[0:GRANK, :], a["gla_w_gate_up"][0]).then_inc(in_moe, 16)
        with nc.allow_non_contiguous_dma(reason="gains, a column per block"):
            sp.dma_start(gout[:, :], a["gla_g_out"][0].rearrange("(k p) -> p k", p=P)).then_inc(in_moe, 16)

        def load(l, K, g, waits, order="ABD"):
            for part in order:
                for s, v in waits["ABD".index(part)]:
                    sp.wait_ge(s, v)
                if part == "D":
                    src = a["moe_w_down"][l].rearrange("(g e) (p k) n -> g p e (k n)", e=GE, k=2)
                    sp.dma_start(moeD, src[bass.ds(g, 1)].rearrange("g p e n -> (g p) e n")).then_inc(K.d, 16)
                    continue
                dst, lo, landed = (moeA, 0, K.a) if part == "A" else (moeB, HK, K.b)
                for m, name in ((0, "moe_w_gate"), (1, "moe_w_up")):
                    src = a[name][l].rearrange("(g e) (p k) n -> g p e (k n)", e=GE, k=KD)
                    sp.dma_start(dst[:, m], src[bass.ds(g, 1), :, :, lo * FE:(lo + HK) * FE]
                                 .rearrange("g p e n -> (g p) e n")).then_inc(landed, 16)

        def experts(l, gate, order):
            K = FAST
            load(l, K, 0, gate, order)
            with sp.Fori(1, GROUPS) as g:
                n = g + GROUPS * l
                load(l, K, g, [[(K.a_read, n)], [(K.b_read, n)], [(K.d_read, n)]])
            with sp.If(overflow(sp, l)):
                K = OVER[l]
                for s in (FAST.a_read, FAST.b_read, FAST.d_read):
                    sp.wait_ge(s, GROUPS * (l + 1))
                with sp.Fori(0, ROUNDS) as r:
                    with sp.Fori(0, GROUPS) as g:
                        load(l, K, g, [[], [], []])
                        for s in (K.a_read, K.b_read, K.d_read):
                            sp.wait_ge(s, r * GROUPS + g + 1)
                        sp.sem_inc(K.seen, 1)

        turned = [(a_job, len(AJOBS)), (k_sums, 3)]
        experts(0, [turned, turned, [(mo_done, 8)]], "ABD")
        gw_in = a["gla_w_in"][0].rearrange("(p k) n -> p k n", k=KD)
        sp.wait_ge(FAST.a_read, GROUPS)
        sp.dma_start(wqk, gw_in[:, :, 0:VO]).then_inc(w_gqk, 16)
        sp.wait_ge(FAST.b_read, GROUPS)
        sp.dma_start(wv, gw_in[:, :, VO:LRO]).then_inc(w_gv, 16)
        sp.wait_ge(FAST.d_read, GROUPS)
        sp.dma_start(wrr, gw_in[:, :, RO:RO + D]).then_inc(w_gr, 16)
        sp.wait_ge(g_job, K_END)
        sp.dma_start(wgo, a["gla_w_o"][0].rearrange("(k p) n -> p k n", p=P)).then_inc(w_go, 16)
        experts(1, [[(go_done, 4)], [(g_job, V_END)], [(g_job, R_END)]], "BDA")
        for i in range(2):
            sp.wait_ge(moe_done, 2)
            sp.dma_start(out[0, i * P:(i + 1) * P, :], h[:, i, :]).then_inc(stored, 16)
        sp.wait_ge(stored, 32)

    @block.gpsimd
    def _(pool):
        pool.memset(h[:, 2, :], 0.0).then_inc(zeroed, 1)
        pool.memset(eps_b, EPS).then_inc(consts, 1)
        pool.memset(epsqk_b, QK * EPS).then_inc(consts, 1)
        pool.memset(one_b, 1.0).then_inc(consts, 1)
        pool.memset(vt[:, 2, :, :], 0.0).then_inc(zeroed, 1)
        pool.memset(gprod, 1.0).then_inc(zeroed, 1)
        pool.memset(zst, 1.0).then_inc(zeroed, 1)
        pool.memset(mpT, 0.0).then_inc(zeroed, 1)
        pool.memset(L, 0.0).then_inc(zeroed, 1)
        pool.memset(rm, 0.0).then_inc(zeroed, 1)
        pool.memset(gates, 0.0).then_inc(zeroed, 1)
        pool.wait_ge(a_act, a_counts["act"])
        pool.wait_ge(a_dve, a_counts["dve"])
        for i in range(2):
            pool.memset(pM[i], 0.0).then_inc(zeroed, 1)
        pool.wait_ge(moe_done, 1)
        pool.memset(gv[:, 2, :], 0.0).then_inc(zeroed, 1)
        pool.memset(attM, 0.0).then_inc(zeroed, 1)
        pool.wait_ge(xn_turned, NB[3])
        pool.memset(att, 0.0).then_inc(zeroed, 1)

    @block.tensor
    def _(pe):
        def norm(n):
            for i in ORDER[n]:
                pe.wait_ge(*xn_ready(n, i))
                turn(i, xn[:, i])

        def turn(i, src):
            for k in range(KD):
                R = WID[i]
                dst = ps[:, 2 * i + k // 4, (k % 4) * P:(k % 4 + 1) * P] if i < 2 else ps[:, 4, k * R:(k + 1) * R]
                mm = pe.transpose(dst, src[0:R, k, :], ident[0:R, 0:R])
            mm.then_inc(xn_turned, 1)

        def mixer_out(l, w, done, ready):
            n = 2 * l + 1
            for i in range(2):
                for sem_, v in ready[i]:
                    pe.wait_ge(sem_, v)
                for b in range(2):
                    if (i, b) == (1, 1):
                        for t in ORDER[n][:-1]:
                            pe.wait_ge(*H_DONE[n][t])
                            turn(t, h[:, t, :].rearrange("p (q k) -> p k q", k=KD))
                    for k in range(KD):
                        mm = pe.matmul(ps[:, 2 * i + b, :], hT[:, k, META + i * P:META + (i + 1) * P],
                                       w[:, k, b * 512:(b + 1) * 512], start=k == 0, stop=k == KD - 1)
                    mm.then_inc(done, 1)
            pe.wait_ge(hT_ok, NB[n] + NORM_TILES[n] - 1)
            pe.wait_ge(in_moe, 16 * 11)
            c0 = COL[2] if NT[l] == 3 else META
            logits(l, 5, c0, COL[1])
            pe.wait_ge(*H_DONE[n][1])
            turn(1, h[:, 1, :].rearrange("p (q k) -> p k q", k=KD))
            pe.wait_ge(hT_ok, NB[n] + NORM_TILES[n])
            logits(l, 7, COL[1], POS)

        def logits(l, bank, c0, c1):
            for k in range(KD):
                mm = pe.matmul(ps[0:NG + NE, bank, 0:c1 - c0], wr[:, l, k, :], hT[:, k, c0:c1],
                               start=k == 0, stop=k == KD - 1)
            mm.then_inc(lg_done, 1)

        def meta_product(bank, src, ks, w, width):
            for n, k in enumerate(ks):
                for j in range(4):
                    mm = pe.matmul(ps[QUAD * j:QUAD * (j + 1), bank, 0:width], src[:, k, 0:QUAD],
                                   w[:, n, j * width:(j + 1) * width], start=n == 0, stop=n == len(ks) - 1)
            return mm

        def mla():
            pe.wait_ge(w_z, 16)
            for i in range(2):
                pe.wait_ge(hT_ok, i + 1)
                for n0, n1, b in ((0, ZA, 5 + 2 * i), (ZA, ZA + ZB, 6 + 2 * i)):
                    if b % 8 == 0:
                        pe.wait_ge(hT_ok, 1)
                    for k in range(KD):
                        mm = pe.matmul(ps[:, b % 8, 0:n1 - n0], hT[:, k, COL[i]:COL[i] + P],
                                       wz[:, k, n0:n1], start=k == 0, stop=k == KD - 1)
                mm.then_inc(z_done, 1)
            pe.wait_ge(hT_ok, 3)
            for k in range(KD):
                pe.matmul(ps[0:QUAD, 1, 0:ZA], hT[:, k, 0:QUAD], wz[:, k, 0:ZA], start=k == 0, stop=k == KD - 1)
                mm = pe.matmul(ps[QUAD:2 * QUAD, 2, 0:ZB], hT[:, k, 0:QUAD], wz[:, k, ZA:ZA + ZB],
                               start=k == 0, stop=k == KD - 1)
            mm.then_inc(z_done, 1)
            for i in range(3):
                pe.wait_ge(z_scaled, i + 1)
                if i == 2:
                    pe.wait_ge(cT_ok, 1)
                R = WID[i]
                for k in range(5):
                    q = QUAD if i == 2 and k >= 3 else 0
                    b, o = ((7, 3 + 2 * i)[i < 2], k * R) if k < 3 else ((4, 4 + 2 * i)[i < 2], (k - 3) * R)
                    mm = pe.transpose(ps[:, b, o:o + R], cq[i][q:q + R, k, :], ident[q:q + R, q:q + R])
                mm.then_inc(c_turned, 1)
            pe.wait_ge(w_q, 16)
            pe.wait_ge(w_kv, 16)
            for j, (kind, i, n, _) in enumerate(AJOBS):
                b = j % 8
                if j >= 8:
                    pe.wait_ge(*a_empty[j - 8])
                elif j == 0:
                    pe.wait_ge(cT_ok, 1)
                elif j == 3:
                    pe.wait_ge(cT_ok, 2)
                elif j == 4:
                    pe.wait_ge(cT_ok, 3)
                ks, w, width = (range(3), wq, 512) if kind == "q" else (range(3, 5), wkv, 512)
                if kind in ("q", "kv") and i < 2:
                    for m, k in enumerate(ks):
                        mm = pe.matmul(ps[:, b, :], cT[:, k, COL[i]:COL[i] + P], w[:, m, n * 512:(n + 1) * 512],
                                       start=m == 0, stop=k == ks[-1])
                elif kind in ("q", "kv"):
                    mm = meta_product(b, cT, ks, w, MH * QK if kind == "q" else MH * (NOPE + VD))
                else:
                    if kind == "tq":
                        pe.wait_ge(qk_ready, i + 1)
                    src = (q_sb if kind == "tq" else k_sb)[i]
                    for m in range(4):
                        mm = pe.transpose(ps[0:QK, b, m * P:(m + 1) * P], src[:, 4 * n + m, :], ident)
                mm.then_inc(a_job, 1)
            pe.wait_ge(a_act, a_counts["act"])
            pe.wait_ge(a_dve, a_counts["dve"])
            pe.wait_ge(in_rows, 16 * N_ROWS)
            KM = QK + MASK_ROWS

            def scores(hd):
                if hd >= 2:
                    pe.wait_ge(p_exp, hd - 1)
                pe.matmul(ps[:, hd % 2, 0:COL[1]], qT[0:KM, hd, META:META + P], kT[0:KM, hd, 0:COL[1]],
                          start=True, stop=True)
                pe.matmul(ps[:, hd % 2, COL[1]:PR], qT[0:KM, hd, COL[1]:POS], kT[0:KM, hd, :],
                          start=True, stop=True).then_inc(s_done, 1)

            def weights(hd):
                pe.wait_ge(p_scaled, hd + 1)
                if hd >= 2:
                    pe.wait_ge(pt_dve, hd - 1)
                    pe.wait_ge(pt_act, hd - 1)
                pr, b, o = prob[hd % 2], 2 + 2 * (hd % 2), COL[1]
                pe.transpose(ps[:, b, 0:P], pr[:, META:META + P], ident)
                pe.transpose(ps[:, b, P:2 * P], pr[:, o + META:o + META + P], ident)
                pe.transpose(ps[:, b, 2 * P:3 * P], pr[:, o + COL[1]:o + POS], ident)
                pe.transpose(ps[0:META, b + 1, 0:P], pr[:, 0:META], ident)
                pe.transpose(ps[0:META, b + 1, P:2 * P], pr[:, o:o + META], ident).then_inc(p_turned, 1)

            def values(hd):
                pe.wait_ge(pt_dve, hd + 1)
                pe.wait_ge(pt_act, hd + 1)
                if hd % 2 == 0 and hd >= 4:
                    pe.wait_ge(o_copied, hd // 2 - 1)
                dst = ps[VD * (hd % 2):VD * (hd % 2) + VD, 6 + hd // 2 % 2, :]
                t = pT[hd % 2]
                pe.matmul(dst[:, 0:META], vt[:, 2, hd, :], mpT[:, hd, :], start=True, stop=True)
                pe.matmul(dst[:, META:POS], vt[:, 2, hd, :], pM[hd % 2], start=True, stop=False)
                pe.matmul(dst[:, META:POS], vt[:, 0, hd, :], t[:, 0:2 * P], start=False, stop=False)
                pe.matmul(dst[:, COL[1]:POS], vt[:, 1, hd, :], t[:, 2 * P:3 * P], start=False, stop=True)\
                  .then_inc(pv_done, 1)

            for s in range(MH):
                for j in range(4):
                    hd = j * MH + s
                    mm = pe.matmul(ps[QUAD * j:QUAD * (j + 1), 7, s * META:(s + 1) * META], qT[0:KM, hd, 0:QUAD],
                                   kT[0:KM, hd, 0:META], start=True, stop=True)
            mm.then_inc(mq_s, 1)
            scores(0)
            scores(1)
            pe.wait_ge(mq_p, 1)
            for s in range(MH):
                mm = pe.transpose(ps[0:META, 6, s * P:(s + 1) * P], mp[:, s, :], ident)
            mm.then_inc(mq_t, 1)
            pe.wait_ge(mq_c, 1)
            for hd in range(HEADS):
                weights(hd)
                if hd + 2 < HEADS:
                    scores(hd + 2)
                if hd:
                    values(hd - 1)
            values(HEADS - 1)
            pe.wait_ge(w_mo, 16)
            pe.wait_ge(o_copied, HEADS // 2)
            meta_product(4, oT, range(KD), wmo, D // 4).then_inc(mo_done, 4)
            mixer_out(0, wmo, mo_done, [[], []])

        def moe(l):
            nt = NT[l]
            for m, i in enumerate(ORDER[2 * l + 1]):
                if m == 0:
                    pe.wait_ge(lg_copied, 2 * l + 1)
                if i == 1:
                    pe.wait_ge(lg_copied, 2 * l + 2)
                mm = pe.transpose(ps[0:WID[i], 6, (NG + NE) * i:(NG + NE) * (i + 1)],
                                  lgT[0:NG + NE, COL[i]:COL[i] + WID[i]], ident[0:NG + NE, 0:NG + NE])
            mm.then_inc(lg_turned, 1)
            pe.wait_ge(tables01, 1)
            pe.wait_ge(sel_ok, l + 1)
            for i in range(nt):
                for j in range(i + 1):
                    mm = pe.matmul(ps[:, 7, NE * i:NE * (i + 1)], before01 if j == i else ones01, sel01[:, j, :],
                                   start=j == 0, stop=j == i)
            mm.then_inc(rank_done, 1)
            for j in range(nt):
                mm = pe.matmul(ps[:, 5, 0:NE], ones01, sel01[:, j, :], start=j == 0, stop=j == nt - 1)
            mm.then_inc(count_done, 1)
            pe.wait_ge(*xn_ready(2 * l + 1, 1))

            def group(K, n, sent, added):
                pe.wait_ge(K.send, sent)
                pe.wait_ge(K.add, added)
                for k in range(KD):
                    for i in range(nt):
                        mm = pe.matmul(ps[:, k // 4, (k % 4) * P:(k % 4 + 1) * P], xn[:, i, k, :], Sg[:, i, :],
                                       start=i == 0, stop=i == nt - 1)
                    if k % 4 == 3:
                        mm.then_inc(K.rows, 1)
                for i in range(nt):
                    R = WID[i]
                    mm = pe.transpose(ps[:, 4, COL[i]:COL[i] + R], Gg[0:R, i, :], ident[0:R, 0:R])
                mm.then_inc(K.turn, 1)
                for part, w, landed, read in ((0, moeA, K.a, K.a_read), (1, moeB, K.b, K.b_read)):
                    pe.wait_ge(K.rows_in, 2 * n + (part + 1))
                    pe.wait_ge(landed, 32 * n + 32)
                    for kk in range(HK):
                        k = part * HK + kk
                        for m in range(2):
                            for j in range(GE):
                                mm = pe.matmul(ps[32 * j:32 * j + 32, 2, m * FE:(m + 1) * FE],
                                               xe[:, k, 32 * j:32 * j + 32], w[:, m, j, kk * FE:(kk + 1) * FE],
                                               start=k == 0 and m == 0, stop=k == KD - 1, skip_group_check=True)
                    mm.then_inc(read, 1)
                pe.wait_ge(K.hid, n + 1)
                for k in range(2):
                    mm = pe.transpose(ps[:, 3, k * P:(k + 1) * P], hid[:, k, :], ident)
                mm.then_inc(K.hid_t, 1)
                pe.wait_ge(K.hid_c, n + 1)
                pe.wait_ge(K.d, 16 * n + 16)
                for k in range(2):
                    for b in range(2):
                        for j in range(GE):
                            mm = pe.matmul(ps[32 * j:32 * j + 32, 5 + b, :], hidT[:, k, 32 * j:32 * j + 32],
                                           moeD[:, j, k * D + b * 512:k * D + (b + 1) * 512], start=k == 0, stop=k == 1)
                mm.then_inc(K.d_read, 1)
                pe.wait_ge(K.turned, n + 1)
                pe.wait_ge(K.ya, n + 1)
                pe.wait_ge(K.yd, n + 1)
                for i in range(nt):
                    for b in range(2):
                        pe.matmul(ps[0:WID[i], COMBINE[2 * i + b], :], GT[:, COL[i]:COL[i] + WID[i]],
                                  ysb[:, b * 512:(b + 1) * 512], start=True, stop=True).then_inc(K.comb, 1)

            with pe.Fori(0, GROUPS) as g:
                group(FAST, g + GROUPS * l, g + ((GROUPS + 1) * l + 1), 2 * nt * g + (ADD0[l] + 1))
            with pe.If(overflow(pe, l)):
                with pe.Fori(0, ROUNDS) as r:
                    with pe.Fori(0, GROUPS) as g:
                        n = r * GROUPS + g
                        group(OVER[l], n, n + r + 1, 2 * nt * n + r + 1)

        def gla():
            pe.wait_ge(hT_ok, NB[3])

            def job(j):
                kind, n, _, bank = JOBS[j]
                if before_me[j] is not None:
                    pe.wait_ge(*emptied[before_me[j]])
                b = ps[:, bank, :]
                if kind == "a":
                    if n == 0:
                        pe.wait_ge(*emptied[0])
                    mm = pe.matmul(b[:, 0:POS], wgu[0:GRANK, n * GDK:(n + 1) * GDK], glr[0:GRANK, :], start=True, stop=True)
                elif kind in ("lr", "q", "k"):
                    if kind == "q" and n == 0:
                        pe.wait_ge(w_gqk, 16)
                    o = (n if kind == "q" else GH + n) * GDK
                    c0 = META if kind == "q" else 0
                    for k in range(KD):
                        w = wlr[:, k, :] if kind == "lr" else wqk[:, k, o:o + GDK]
                        mm = pe.matmul(b[0:w.shape[1], 0:POS - c0], w, hT[:, k, c0:POS], start=k == 0, stop=k == KD - 1)
                elif kind == "v" and n == 4:
                    mm = meta_product(bank, hT, range(KD), wv, GDV)
                else:
                    i, hb = divmod(n, 2)
                    if n == 0:
                        pe.wait_ge(w_gv if kind == "v" else w_gr, 16)
                    w = wv if kind == "v" else wrr
                    for k in range(KD):
                        mm = pe.matmul(b[0:WID[i], :], hT[:, k, COL[i]:COL[i] + WID[i]],
                                       w[:, k, hb * 512:(hb + 1) * 512], start=k == 0, stop=k == KD - 1)
                mm.then_inc(g_job, 1)

            for j in range(V_END):
                job(j)
            pe.wait_ge(*emptied[V_END - 1])
            pe.wait_ge(gq_ok, 1)
            for s in range(NSUB):
                t, j = divmod(s, NSUB // 2)
                n = META + SUB * (s + 1)
                if s == NSUB // 2:
                    pe.wait_ge(g_attm, s)
                pe.wait_ge(gk_ok, s + 1)
                for g in range(GH):
                    mm = pe.matmul(ps[32 * j:32 * j + 32, g, 0:n], gqT[:, g, s * SUB:(s + 1) * SUB],
                                   gk[s % 3][:, g, 0:n], start=True, stop=True)
                mm.then_inc(g_att, 1)
                if s < NSUB // 2:
                    job(V_END + s)
            pe.wait_ge(g_attm, NSUB)
            pe.wait_ge(*emptied[R_END - 1])
            for g in range(GH):
                pe.transpose(ps[:, 2 * g, 0:P], att[:, 0, g, META:META + P], ident)
                pe.transpose(ps[:, 2 * g, P:2 * P], att[:, 1, g, META:META + P], ident)
                pe.transpose(ps[:, 2 * g, 2 * P:3 * P], att[:, 1, g, META + P:POS], ident)
                for t in range(2):
                    mm = pe.transpose(ps[0:META, 2 * g + 1, t * P:(t + 1) * P], att[:, t, g, 0:META], ident)
                mm.then_inc(g_attT, 1)
            pe.wait_ge(g_aT_act, GH)
            pe.wait_ge(g_aT_dve, GH)
            for t in range(2):
                for g in range(GH):
                    dst = ps[:, 2 * t + g // 2, (g % 2) * GDV:(g % 2 + 1) * GDV]
                    cols = slice(g * GDV, (g + 1) * GDV)
                    pe.matmul(dst, attM[:, g, t * P:(t + 1) * P], gv[:, 2, cols], start=True, stop=False)
                    mm = pe.matmul(dst, attT[g][:, t * P:(t + 1) * P], gv[:, 0, cols], start=False, stop=t == 0)
                    if t:
                        mm = pe.matmul(dst, attT[g][:, 2 * P:3 * P], gv[:, 1, cols], start=False, stop=True)
                mm.then_inc(g_o, 1)
            for t in range(2):
                pe.wait_ge(g_y, t + 1)
                for k in range(KD):
                    mm = pe.transpose(ps[:, 4 + 2 * t + k // 4, (k % 4) * P:(k % 4 + 1) * P],
                                      gr[:, t, k * P:(k + 1) * P], ident)
                mm.then_inc(g_yT, 1)
            mixer_out(1, wgo, go_done, [[(w_go, 16), (g_yT_act, 1), (g_yT_dve, 1)], [(g_yT_act, 2), (g_yT_dve, 2)]])

        pe.wait_ge(in_c, 16)
        norm(0)
        mla()
        moe(0)
        norm(2)
        gla()
        moe(1)

    @block.scalar
    def _(act):
        link = Links(act, act_link)

        def scale_of(n, i):
            act.wait_ge(*H_DONE[n][i])
            v = ssq[:, i:i + 1]
            link(act.activation(xflat[:, i * D:(i + 1) * D], h[:, i, :], ACT.Square, scale=D ** -0.5, accum_out=v))
            link(act.activation(v, v, ACT.Ln, bias=eps_b))
            return act.activation(rstd[:, i:i + 1], v, ACT.Exp, scale=-0.5)

        def scaled(i):
            act.activation(xn[:, i], h[:, i, :].rearrange("p (q k) -> p k q", k=KD), ACT.Copy,
                           scale=rstd[:, i:i + 1]).then_inc(xn_act, 1)

        def norm(n):
            for i in ORDER[n]:
                ins = scale_of(n, i)
                if i == 0:
                    ins.then_inc(rstd_ok, 1)
                else:
                    link(ins)
                    scaled(i)

        def mla():
            act.wait_ge(zeroed, 8)
            for i in range(3):
                act.wait_ge(z_done, i + 1)
                if i < 2:
                    ba, bb, ra, rb_ = (5 + 2 * i) % 8, (6 + 2 * i) % 8, slice(0, P), slice(0, P)
                    link(act.copy(kr[:, i, :], ps[:, bb, KVR:KVR + ROPE]))
                else:
                    ba, bb, ra, rb_ = 1, 2, slice(0, QUAD), slice(QUAD, 2 * QUAD)
                    for j in range(4):
                        ins = act.copy(kr[QUAD * j:QUAD * (j + 1), i, :], ps[rb_, bb, KVR:KVR + ROPE])
                    link(ins)
                act.activation(junk[:, 0:ROPE], kr[:, i, :], ACT.Square, scale=QK ** -0.5,
                               accum_out=krs[:, i:i + 1]).then_inc(z_kr, 1)
                act.wait_ge(z_kr, i + 1)
                act.activation(junk[ra, 0:QR], ps[ra, ba, 0:QR], ACT.Square, scale=QR ** -0.5,
                               accum_out=zst[ra, i, 0:1])
                link(act.activation(junk[rb_, QR:], ps[rb_, bb, 0:KVR], ACT.Square, scale=KVR ** -0.5,
                                    accum_out=zst[rb_, i, 1:2]))
                link(act.activation(zst[:, i, :], zst[:, i, :], ACT.Ln, bias=eps_b))
                act.activation(zrs[:, i, :], zst[:, i, :], ACT.Exp, scale=-0.5).then_inc(z_rstd, 1)

            def copies(i):
                H = HEADS if i < 2 else MH
                act.wait_ge(z_done, 3)
                W = 512 if i < 2 else MH * QK
                for n, j in enumerate(ajobs("q", i)):
                    act.wait_ge(a_job, j + 1)
                    act.copy(flat(q_sb[i])[:, n * W:(n + 1) * W], ps[:, j % 8, 0:W]).then_inc(a_act, 1)
                act.wait_ge(a_act, a_empty[j][1])
                if i:
                    act.wait_ge(k_sums, i)
                act.activation(sq[:, 0:H], q_sb[i], ACT.Square, scale=QK ** -0.5).then_inc(q_squared, 1)
                act.wait_ge(q_sums, i + 1)
                act.wait_ge(*a_empty[ajobs("kv", i)[-1]])
                act.activation(sq[:, 0:H, 0:NOPE], k_sb[i][:, :, 0:NOPE], ACT.Square, scale=QK ** -0.5)\
                    .then_inc(k_squared, 1)
                link(act.activation(qst[:, i, 0:H], qst[:, i, 0:H], ACT.Ln, scale=float(QK), bias=epsqk_b))
                act.activation(scl[:, i, 0:H], qst[:, i, 0:H], ACT.Exp, scale=-0.5)
                act.wait_ge(k_sums, i + 1)
                link(act.activation(kst[:, i, 0:H], kst[:, i, 0:H], ACT.Ln, bias=eps_b))
                act.activation(krst[:, i, 0:H], kst[:, i, 0:H], ACT.Exp, scale=-0.5).then_inc(k_rstd, 1)

            def turned(i):
                for n, j in enumerate(ajobs("tq", i)):
                    act.wait_ge(a_job, j + 1)
                    src = ps[0:QK, j % 8, :].rearrange("p (h t) -> p h t", h=4)
                    if i < 2:
                        ins = act.copy(qT[0:QK, 4 * n:4 * n + 4, COL[i]:COL[i] + P], src)
                    else:
                        ins = act.copy(qT[0:QK, :, 0:META].rearrange("p (j s) t -> p s j t", j=4),
                                       src.rearrange("p s (j t) -> p s j t", j=4)[:, :, :, 0:META])
                    ins.then_inc(a_act, 1)

            for i in range(3):
                copies(i)
            for i in range(3):
                turned(i)

            def exps(hd):
                act.wait_ge(s_shift, hd + 1)
                if hd >= 2:
                    act.wait_ge(p_turned, hd - 1)
                for i, o, n in ((0, 0, COL[1]), (1, COL[1], POS)):
                    ins = act.activation(prob[hd % 2][:, o:o + n], ps[:, hd % 2, o:o + n], ACT.Exp,
                                         bias=nb[hd % 2][:, i:i + 1], scale=scl[:, i, hd:hd + 1],
                                         accum_out=rs[hd % 2][:, i:i + 1])
                ins.then_inc(p_exp, 1)

            def meta_weights(hd):
                act.wait_ge(p_turned, hd + 1)
                if hd >= 2:
                    act.wait_ge(pv_done, hd - 1)
                act.copy(pM[hd % 2][0:META, :], ps[0:META, 3 + 2 * (hd % 2), 0:SEQ]).then_inc(pt_act, 1)

            def heads_out(hp):
                act.wait_ge(pv_done, 2 * hp + 2)
                act.copy(oT[:, hp, :], ps[:, 6 + hp % 2, 0:POS]).then_inc(o_copied, 1)

            act.wait_ge(a_dve, a_counts["dve"])
            act.wait_ge(zeroed, 10)
            act.wait_ge(mq_dif, 1)
            act.activation(mp, mp, ACT.Exp).then_inc(mq_exp, 1)
            exps(0)
            for hd in range(HEADS):
                if hd + 1 < HEADS:
                    exps(hd + 1)
                meta_weights(hd)
                if hd >= 3 and hd % 2:
                    heads_out((hd - 3) // 2)
            heads_out(HEADS // 2 - 1)

        def moe(l):
            n = 2 * l + 1
            c0 = 0 if NT[l] == 3 else META
            for i in ORDER[n]:
                scale_of(n, i).then_inc(rstd_ok, 1)
                act.wait_ge(rstd_ok, rstd_count(n, i))
                if i != 1:
                    scaled(i)
            for m, (bank, lo, hi) in enumerate(((5, c0, COL[1]), (7, COL[1], POS))):
                act.wait_ge(lg_done, 2 * l + m + 1)
                act.copy(lgT[0:NG + NE, lo:hi], ps[0:NG + NE, bank, 0:hi - lo]).then_inc(lg_copied, 1)
            scaled(1)
            act.wait_ge(e_dif, l + 1)
            act.activation(E5[:, 0:NT[l], :], E5[:, 0:NT[l], :], ACT.Exp).then_inc(e_exp, 1)

            def group(K, n):
                act.wait_ge(K.turn, n + 1)
                act.copy(GT[:, c0:POS], ps[:, 4, c0:POS]).then_inc(K.turned, 1)
                act.wait_ge(K.b_read, n + 1)
                act.activation(ex, ps[:, 2, 0:FE], ACT.Silu).then_inc(K.silu, 1)
                act.wait_ge(K.hid_t, n + 1)
                act.copy(flat(hidT), ps[:, 3, 0:2 * P]).then_inc(K.hid_c, 1)
                act.wait_ge(K.d_read, n + 1)
                act.copy(ysb[:, 0:512], ps[:, 5, :]).then_inc(K.ya, 1)

            with act.Fori(0, GROUPS) as g:
                group(FAST, g + GROUPS * l)
            with act.If(overflow(act, l)):
                with act.Fori(0, ROUNDS) as r:
                    with act.Fori(0, GROUPS) as g:
                        group(OVER[l], r * GROUPS + g)

        def gla():
            def evac(j):
                kind, n, _, bank = JOBS[j]
                act.wait_ge(g_job, j + 1)
                b = ps[:, bank, :]
                if kind == "lr":
                    ins = act.copy(glr[0:GRANK, :], b[0:GRANK, 0:POS])
                elif kind == "q":
                    ins = act.mul(gqT[:, n, :], b[:, 0:SEQ], GDK ** -0.5)
                elif kind == "k":
                    ins = act.copy(gkT[:, n, :], b[:, 0:POS])
                elif kind == "r":
                    ins = act.activation(gr[:, n // 2, (n % 2) * 512:(n % 2 + 1) * 512], b, ACT.Silu)
                elif n == 4:
                    for g in range(GH):
                        ins = act.copy(gv[0:META, 2, g * GDV:(g + 1) * GDV], b[QUAD * g:QUAD * g + META, 0:GDV])
                else:
                    i, hb = divmod(n, 2)
                    ins = act.copy(gv[0:WID[i], i, hb * 512:(hb + 1) * 512], b[0:WID[i], :])
                ins.then_inc(g_act, 1)

            mine = [j for j in range(len(JOBS)) if JOBS[j][2] == "act"]
            for j in mine[:5]:
                evac(j)
            act.wait_ge(g_abs, 1)
            link(act.activation(gt, gt, ACT.Exp, scale=-1.0))
            act.activation(gt, gt, ACT.Ln, bias=one_b).then_inc(g_log, 1)
            for j in mine[5:9]:
                evac(j)
            act.wait_ge(gq_dif, 1)
            act.activation(gtq, gtq, ACT.Exp, scale=1.0 / TAU).then_inc(gq_exp, 1)
            act.wait_ge(zeroed, 11)
            for s in range(NSUB):
                n = META + SUB * (s + 1)
                act.wait_ge(gk_dif, s + 1)
                act.activation(gk[s % 3][:, :, 0:n], gk[s % 3][:, :, 0:n], ACT.Exp, scale=-1.0 / TAU).then_inc(gk_exp, 1)
                for j in mine[9 + 2 * s:11 + 2 * s]:
                    if j < V_END:
                        evac(j)
            for j in range(V_END, R_END):
                evac(j)
            act.wait_ge(zeroed, 12)
            for g in range(GH):
                act.wait_ge(g_attT, g + 1)
                act.copy(attM[0:META, g, :], ps[0:META, 2 * g + 1, 0:SEQ]).then_inc(g_aT_act, 1)
            for t in range(2):
                act.wait_ge(g_o, t + 1)
                for g in range(GH):
                    ins = act.activation(gsq, ps[:, 2 * t + g // 2, (g % 2) * GDV:(g % 2 + 1) * GDV],
                                         ACT.Square, scale=GDV ** -0.5, accum_out=gos[:, t, g:g + 1])
                    link(ins)
                link(act.activation(gos[:, t, :], gos[:, t, :], ACT.Ln, bias=eps_b))
                act.activation(gor[:, t, :], gos[:, t, :], ACT.Exp, scale=-0.5).then_inc(g_orstd, 1)
            for t in range(2):
                act.wait_ge(g_yT, t + 1)
                for j in range(2):
                    ins = act.activation(gyT[:, j:4:2, t * P:(t + 1) * P],
                                         ps[:, 4 + 2 * t, :].rearrange("p (k q) -> p k q", k=4)[:, j::2, :],
                                         ACT.Copy, scale=gout[:, j:j + 1])
                ins.then_inc(g_yT_act, 1)

        act.wait_ge(consts, 3)
        norm(0)
        mla()
        moe(0)
        norm(2)
        gla()
        moe(1)

    @block.vector
    def _(dve):
        link = Links(dve, dve_link)
        TT, TS, STT = dve.tensor_tensor, dve.tensor_scalar, dve.scalar_tensor_tensor

        def gained(n, i):
            dve.wait_ge(xn_turned, NB[n] + ORDER[n].index(i) + 1)
            cols = slice(COL[i], COL[i] + WID[i])
            if i < 2:
                for b in range(2):
                    ins = TT(hT[:, 4 * b:4 * b + 4, cols], ps[:, 2 * i + b, :].rearrange("p (k q) -> p k q", k=4),
                             rep(gn[:, n, 4 * b:4 * b + 4], P), ALU.mult)
            else:
                ins = TT(hT[:, :, cols], ps[:, 4, 0:KD * META].rearrange("p (k q) -> p k q", k=KD),
                         rep(gn[:, n, :], META), ALU.mult)
            ins.then_inc(hT_ok, 1)

        def mixer_added(l, done, done0, added):
            n = 2 * l + 1
            for i in range(2):
                for b in range(2):
                    if (i, b) == (1, 1):
                        for t in ORDER[n][:-1]:
                            gained(n, t)
                    dve.wait_ge(done, done0 + 2 * i + b + 1)
                    hh = h[:, i, b * 512:(b + 1) * 512]
                    TT(hh, hh, ps[:, 2 * i + b, :], ALU.add).then_inc(added, 1)
            gained(n, 1)

        def norm(n):
            for m, i in enumerate(ORDER[n]):
                if i == 0:
                    dve.wait_ge(rstd_ok, rstd_count(n, i))
                    TS(xn[:, 0], h[:, 0, :].rearrange("p (q k) -> p k q", k=KD), rstd[:, 0:1], None, ALU.mult)\
                        .then_inc(xn_dve, 1)
                if m == 0 and n == 0:
                    dve.wait_ge(in_small, 16 * N_SMALL)
                gained(n, i)

        def mla():
            dve.wait_ge(in_c, 16)
            dve.tensor_copy(before01, before)
            dve.tensor_copy(ones01, ones[:, 0:P]).then_inc(tables01, 1)
            dve.wait_ge(zeroed, 8)
            cos, sin = (c(n).rearrange("p (t f) -> p t f", t=3) for n in ("cos", "sin"))
            for tab, trig, m in ((tcq, cos, 0), (tsq, sin, 0), (tck, cos, 1), (tsk, sin, 1)):
                TT(tab, trig, over(gqk[:, m, NOPE:], 3), ALU.mult)
            link(TT(gprod[0:NOPE, :], gcol[0:NOPE, 0:1], gcol[0:NOPE, 1:2], ALU.mult))
            H = ROPE // 2
            for i in range(3):
                ba, bb, ra, rb_ = ((5 + 2 * i) % 8, (6 + 2 * i) % 8, slice(0, P), slice(0, P)) if i < 2 else \
                    (1, 2, slice(0, QUAD), slice(QUAD, 2 * QUAD))
                dve.wait_ge(z_rstd, i + 1)
                TS(cq[i][ra, 0:3, :], ps[ra, ba, 0:QR].rearrange("p (q k) -> p k q", k=3), zrs[ra, i, 0:1], None, ALU.mult)
                TS(cq[i][rb_, 3:5, :], ps[rb_, bb, 0:KVR].rearrange("p (q k) -> p k q", k=2), zrs[rb_, i, 1:2], None,
                   ALU.mult).then_inc(z_scaled, 1)
                TT(rp[:, 0, 0:ROPE], kr[:, i, :], tck[:, i, :], ALU.mult)
                link(TT(rp[:, 1, 0:ROPE], kr[:, i, :], tsk[:, i, :], ALU.mult))
                TT(kr[:, i, 0:H], rp[:, 0, 0:H], rp[:, 1, H:ROPE], ALU.subtract)
                link(TT(kr[:, i, H:ROPE], rp[:, 0, H:ROPE], rp[:, 1, 0:H], ALU.add))
                dve.wait_ge(c_turned, i + 1)
                R = WID[i]
                cols = slice(COL[i], COL[i] + R)
                src = [ps[:, 7, 0:3 * R], ps[:, 4, 0:2 * R]] if i == 2 else \
                    [ps[:, 3 + 2 * i, 0:3 * R], ps[:, 4 + 2 * i, 0:2 * R]]
                TT(cT[:, 0:3, cols], src[0].rearrange("p (k q) -> p k q", k=3), rep(gc5[:, 0:3], R), ALU.mult)
                TT(cT[:, 3:5, cols], src[1].rearrange("p (k q) -> p k q", k=2), rep(gc5[:, 3:5], R),
                   ALU.mult).then_inc(cT_ok, 1)

            def keys_values(i):
                for n, j in enumerate(ajobs("kv", i)):
                    dve.wait_ge(a_job, j + 1)
                    src = ps[:, j % 8, :].rearrange("p (h f) -> p h f", h=4)
                    dve.tensor_copy(k_sb[i][:, 4 * n:4 * n + 4, 0:NOPE], src[:, :, 0:NOPE])
                    if i < 2:
                        ins = dve.tensor_copy(vt[:, i, 4 * n:4 * n + 4, :], src[:, :, NOPE:])
                    else:
                        for q in range(4):
                            ins = dve.tensor_copy(vt[0:META, i, MH * q:MH * (q + 1), :],
                                                  src[QUAD * q:QUAD * q + META, :, NOPE:])
                    ins.then_inc(a_dve, 1)

            def rotary(i):
                Hn = HEADS if i < 2 else MH
                ra, rb_ = (rp[:, m].rearrange("p (h f) -> p h f", h=HEADS)[:, 0:Hn] for m in range(2))
                dve.wait_ge(q_squared, i + 1)
                dve.tensor_reduce(qst[:, i, 0:Hn], sq[:, 0:Hn], AX.X, ALU.add).then_inc(q_sums, 1)
                x = q_sb[i][:, :, NOPE:QK]
                TT(ra, x, over(tcq[:, i, :], Hn), ALU.mult)
                link(TT(rb_, x, over(tsq[:, i, :], Hn), ALU.mult))
                TT(q_sb[i][:, :, NOPE:NOPE + H], ra[:, :, 0:H], rb_[:, :, H:ROPE], ALU.subtract)
                link(TT(q_sb[i][:, :, NOPE + H:QK], ra[:, :, H:ROPE], rb_[:, :, 0:H], ALU.add))
                dve.wait_ge(k_squared, i + 1)
                link(dve.tensor_reduce(kst[:, i, 0:Hn], sq[:, 0:Hn, 0:NOPE], AX.X, ALU.add))
                TS(kst[:, i, 0:Hn], kst[:, i, 0:Hn], krs[:, i:i + 1], None, ALU.add).then_inc(k_sums, 1)
                dve.wait_ge(k_rstd, i + 1)
                TT(k_sb[i][:, :, 0:NOPE], k_sb[i][:, :, 0:NOPE], rep(krst[:, i, 0:Hn], NOPE), ALU.mult)
                TT(k_sb[i][:, :, NOPE:QK], over(kr[:, i, :], Hn), rep(krst[:, i, 0:Hn], ROPE), ALU.mult)\
                    .then_inc(qk_ready, 1)

            keys_values(0)
            rotary(0)
            keys_values(1)
            keys_values(2)
            rotary(1)
            rotary(2)
            for i in range(3):
                for n, j in enumerate(ajobs("tk", i)):
                    dve.wait_ge(a_job, j + 1)
                    src = ps[0:QK, j % 8, :].rearrange("p (h t) -> p h t", h=4)
                    if i < 2:
                        dst = kT[0:QK, 4 * n:4 * n + 4, COL[i]:COL[i] + P]
                    else:
                        dst = kT[0:QK, :, 0:META].rearrange("p (j s) t -> p s j t", j=4)
                        src = src.rearrange("p s (j t) -> p s j t", j=4)[:, :, :, 0:META]
                    TS(dst, src, gprod[0:QK, 0:1], None, ALU.mult).then_inc(a_dve, 1)

            dve.wait_ge(mq_s, 1)
            sm = ps[:, 7, 0:MH * META].rearrange("p (s k) -> p s k", s=MH)
            link(dve.tensor_reduce(mmx, sm, AX.X, ALU.max))
            link(TT(mp, sm, rep(mmx, META), ALU.subtract))
            TT(mp, mp, rep(scl[:, 2, 0:MH], META), ALU.mult).then_inc(mq_dif, 1)

            def shift(hd):
                dve.wait_ge(s_done, hd + 1)
                if hd >= 2:
                    dve.wait_ge(p_exp, hd - 1)
                dve.tensor_reduce(mx[hd % 2][:, 0:1], ps[:, hd % 2, 0:COL[1]], AX.X, ALU.max)
                link(dve.tensor_reduce(mx[hd % 2][:, 1:2], ps[:, hd % 2, COL[1]:PR], AX.X, ALU.max))
                STT(nb[hd % 2], mx[hd % 2], -1.0, scl[:, 0:2, hd], ALU.mult, ALU.mult).then_inc(s_shift, 1)

            def scale(hd):
                dve.wait_ge(p_exp, hd + 1)
                link(dve.reciprocal(ri[hd % 2], rs[hd % 2]))
                for i, o, n in ((0, 0, COL[1]), (1, COL[1], POS)):
                    pr = prob[hd % 2][:, o:o + n]
                    ins = TS(pr, pr, ri[hd % 2][:, i:i + 1], None, ALU.mult)
                ins.then_inc(p_scaled, 1)

            def frame_weights(hd):
                dve.wait_ge(p_turned, hd + 1)
                if hd >= 2:
                    dve.wait_ge(pv_done, hd - 1)
                dve.tensor_copy(pT[hd % 2], ps[:, 2 + 2 * (hd % 2), 0:3 * P]).then_inc(pt_dve, 1)

            shift(0)
            dve.wait_ge(mq_exp, 1)
            link(dve.tensor_reduce(mmx, mp, AX.X, ALU.add))
            link(dve.reciprocal(mri, mmx))
            TT(mp, mp, rep(mri, META), ALU.mult).then_inc(mq_p, 1)
            dve.wait_ge(mq_t, 1)
            dve.tensor_copy(mpT[0:META].rearrange("p (j s) t -> p s j t", j=4),
                            ps[0:META, 6, :].rearrange("p (s j t) -> p s j t", s=MH, j=4)[:, :, :, 0:META])\
                .then_inc(mq_c, 1)
            for hd in range(HEADS):
                if hd + 1 < HEADS:
                    shift(hd + 1)
                scale(hd)
                if hd:
                    frame_weights(hd - 1)
            frame_weights(HEADS - 1)
            dve.wait_ge(mo_done, 4)
            for j in range(4):
                hh = h[0:META, 2, j * 256:(j + 1) * 256]
                TT(hh, hh, ps[QUAD * j:QUAD * j + META, 4, 0:256], ALU.add).then_inc(mo_add, 1)
            mixer_added(0, mo_done, 4, mo_add)

        def route(l):
            nt = NT[l]
            V = slice(0, nt)
            first = c("first")
            dve.wait_ge(lg_turned, l + 1)
            W = NG + NE
            src = ps[:, 6, 0:nt * W].rearrange("p (t n) -> p t n", t=nt)
            dve.wait_ge(rstd_ok, rstd_count(2 * l + 1, 1))
            for i in range(nt):
                R = slice(0, WID[i])
                ins = STT(L[R, i, :], src[R, i, :], rstd[R, i:i + 1], rb[R, l, :], ALU.mult, ALU.add)
            link(ins)

            def choose(x, best, out):
                n = x.shape[2]
                link(TT(out, x, rep(best, n), ALU.is_equal))
                link(TT(out, out, over(first[:, NE - n:], nt), ALU.mult))
                link(dve.tensor_reduce(pm[:, V], out, AX.X, ALU.max))
                link(TT(out, out, rep(pm[:, V], n), ALU.is_equal))

            lg, lx = L[:, V, 0:NG], L[:, V, NG:]
            link(dve.tensor_reduce(mg[:, V], lg, AX.X, ALU.max))
            TT(E5[:, V, 0:NG], lg, rep(mg[:, V], NG), ALU.subtract)
            choose(lg, mg[:, V], g4[:, V, :])
            link(TS(g4[:, V, :], g4[:, V, :], BIG, -BIG, ALU.mult, ALU.add))
            link(TT(le[:, V, :].rearrange("p t (g e) -> p t g e", g=NG), lx.rearrange("p t (g e) -> p t g e", g=NG),
                    rep3(g4[:, V, :], EPG), ALU.add))
            link(dve.tensor_reduce(m1[:, V], le[:, V, :], AX.X, ALU.max))
            choose(le[:, V, :], m1[:, V], s1[:, V, :])
            link(STT(le[:, V, :], s1[:, V, :], -3 * BIG, le[:, V, :], ALU.mult, ALU.add))
            link(dve.tensor_reduce(m2[:, V], le[:, V, :], AX.X, ALU.max))
            TT(E5[:, V, NG:], rep(m2[:, V], 1), rep(m1[:, V], 1), ALU.subtract).then_inc(e_dif, 1)
            choose(le[:, V, :], m2[:, V], s2[:, V, :])
            link(TT(sel[:, V, :], s1[:, V, :], s2[:, V, :], ALU.add))
            TT(sel01[:, V, :], sel[:, V, :], rep(c("valid")[:, V], NE), ALU.mult).then_inc(sel_ok, 1)
            dve.wait_ge(e_exp, l + 1)
            link(dve.tensor_reduce(mg[:, V], E5[:, V, 0:NG], AX.X, ALU.add))
            e2 = E5[:, V, NG:].rearrange("p t o -> p (t o)")
            link(STT(m1[:, V], e2, 1.0, mg[:, V], ALU.add, ALU.mult))
            link(dve.reciprocal(w1[:, V], m1[:, V]))
            link(TT(w2[:, V], w1[:, V], e2, ALU.mult))
            TT(s1[:, V, :], s1[:, V, :], rep(w1[:, V], NE), ALU.mult)
            link(TT(s2[:, V, :], s2[:, V, :], rep(w2[:, V], NE), ALU.mult))
            TT(gates[:, V, 0:NE], s1[:, V, :], s2[:, V, :], ALU.add).then_inc(FAST.add, 1)
            dve.wait_ge(rank_done, l + 1)
            link(STT(rm[:, V, 0:NE], sel01[:, V, :], -OFF, ps[:, 7, 0:nt * NE].rearrange("p (t n) -> p t n", t=nt),
                     ALU.mult, ALU.add))

        def moe(l):
            route(l)
            nt, norm_n = NT[l], 2 * l + 1

            def dispatch(K, e0, lk):
                s4, g4_ = (t[:, 0:nt, :].rearrange("p t (e s) -> p t e s", e=GE) for t in (Sg, Gg))
                slot = c("slot").unsqueeze(1).unsqueeze(1).to_broadcast([P, nt, GE, SLOTS])
                lk(TT(s4, slot, rep3(rm[:, 0:nt, e0], SLOTS), ALU.is_equal))
                TT(g4_, s4, rep3(gates[:, 0:nt, e0], SLOTS), ALU.mult).then_inc(K.send, 1)

            def group(K, n, g, base, combined):
                lk = Links(dve, K.step)
                lk.base = base
                for b in range(2):
                    dve.wait_ge(K.rows, 2 * n + (b + 1))
                    TT(xe[:, 4 * b:4 * b + 4, :], ps[:, b, :].rearrange("p (k q) -> p k q", k=4),
                       rep(gn[:, norm_n, 4 * b:4 * b + 4], P), ALU.mult).then_inc(K.rows_in, 1)
                dve.wait_ge(K.turn, n + 1)
                dispatch(K, bass.ds(GE * g + GE, GE), lk)
                dve.wait_ge(K.silu, n + 1)
                TT(hid.rearrange("p k q -> p q k"), ex.rearrange("p (q k) -> p q k", k=2),
                   ps[:, 2, FE:2 * FE].rearrange("p (q k) -> p q k", k=2), ALU.mult).then_inc(K.hid, 1)
                dve.wait_ge(K.d_read, n + 1)
                dve.tensor_copy(ysb[:, 512:], ps[:, 6, :]).then_inc(K.yd, 1)
                for i in range(nt):
                    for b in range(2):
                        dve.wait_ge(K.comb, combined + (2 * i + b + 1))
                        hh = h[0:WID[i], i, b * 512:(b + 1) * 512]
                        TT(hh, hh, ps[0:WID[i], COMBINE[2 * i + b], :], ALU.add).then_inc(K.add, 1)
                assert lk.n == LOOP_LINKS

            K = FAST
            dispatch(K, slice(0, GE), link)
            dve.wait_ge(count_done, l + 1)
            link(dve.tensor_reduce(most[0:1], ps[0:1, 5, 0:NE], AX.X, ALU.max))
            TS(flag[0:1, l:l + 1], most[0:1], float(SLOTS), None, ALU.is_gt).then_inc(flag_ok, 1)
            with dve.Fori(0, GROUPS) as g:
                group(K, g + GROUPS * l, g, (g + GROUPS * l) * LOOP_LINKS, g * (2 * nt) + COMB0[l])
            with dve.If(overflow(dve, l)):
                K = OVER[l]
                with dve.Fori(0, ROUNDS) as r:
                    opened = r * (2 * nt * GROUPS + 1) + 1
                    TS(flat(rm), flat(rm), -float(SLOTS), None, ALU.add).then_inc(K.add, 1)
                    dve.wait_ge(K.add, opened)
                    lk = Links(dve, K.step)
                    per = GROUPS * LOOP_LINKS + 1
                    lk.base = r * per
                    dispatch(K, slice(0, GE), lk)
                    with dve.Fori(0, GROUPS) as g:
                        n = r * GROUPS + g
                        group(K, n, g, r * per + g * LOOP_LINKS + 1, n * (2 * nt))
            dve.memset(marker[0:1, l:l + 1], 0.0).then_inc(moe_done, 1)

        def gla():
            mine = [j for j in range(len(JOBS)) if JOBS[j][2] == "dve"]
            for j in mine[:4]:
                _, n, _, bank = JOBS[j]
                dve.wait_ge(g_job, j + 1)
                TS(ga[:, n, :], ps[:, bank, 0:POS], bg[:, n:n + 1], None, ALU.add).then_inc(g_dve, 1)
            dve.wait_ge(g_dve, 4)
            STT(flat(gt), flat(ga), -1.0, flat(ga), ALU.mult, ALU.max).then_inc(g_abs, 1)
            dve.wait_ge(g_log, 1)
            link(STT(flat(ga), flat(ga), 0.0, flat(gt), ALU.min, ALU.subtract))
            for g in range(GH):
                ins = dve.tensor_tensor_scan(gb[:, g, :], ones, ga[:, g, :], 0.0, ALU.mult, ALU.add)
            link(ins)
            blocks = gb[:, :, META:POS].rearrange("p g (s j) -> p g s j", s=NSUB)
            ref = blocks[:, :, :, SUB // 2 - 1:SUB // 2]
            tq4 = gtq.rearrange("p g (s j) -> p g s j", s=NSUB)
            TT(tq4, blocks, ref.to_broadcast([P, GH, NSUB, SUB]), ALU.subtract).then_inc(gq_dif, 1)

            def dif(s):
                n = META + SUB * (s + 1)
                if s >= 3:
                    dve.wait_ge(g_att, s - 2)
                TT(gk[s % 3][:, :, 0:n], gb[:, :, 0:n], ref[:, :, s, :].to_broadcast([P, GH, n]), ALU.subtract)\
                    .then_inc(gk_dif, 1)

            def mul(s):
                n = META + SUB * (s + 1)
                dve.wait_ge(gk_exp, s + 1)
                v = gk[s % 3][:, :, 0:n]
                TT(v, v, gkT[:, :, 0:n], ALU.mult).then_inc(gk_ok, 1)

            def masked(s):
                t, j = divmod(s, NSUB // 2)
                n = META + SUB * (s + 1)
                rows = slice(32 * j, 32 * j + 32)
                dve.wait_ge(g_att, s + 1)
                TT(att[rows, t, :, 0:n], ps[rows, 0:GH, 0:n],
                   over(c("causal")[rows, t * POS:t * POS + n], GH), ALU.mult).then_inc(g_attm, 1)

            dif(0)
            dve.wait_ge(gq_exp, 1)
            TT(gqT, gqT, gtq, ALU.mult).then_inc(gq_ok, 1)
            dif(1)
            dve.wait_ge(zeroed, 13)
            for s in range(NSUB):
                mul(s)
                if s >= 1:
                    masked(s - 1)
                if s + 2 < NSUB:
                    dif(s + 2)
            masked(NSUB - 1)
            for g in range(GH):
                dve.wait_ge(g_attT, g + 1)
                dve.tensor_copy(attT[g], ps[:, 2 * g, 0:3 * P]).then_inc(g_aT_dve, 1)
            for t in range(2):
                dve.wait_ge(g_orstd, t + 1)
                for g in range(GH):
                    v = gr[:, t, g * GDV:(g + 1) * GDV]
                    ins = STT(v, ps[:, 2 * t + g // 2, (g % 2) * GDV:(g % 2 + 1) * GDV], gor[:, t, g:g + 1], v,
                              ALU.mult, ALU.mult)
                ins.then_inc(g_y, 1)
            for t in range(2):
                dve.wait_ge(g_yT, t + 1)
                TT(gyT[:, 4:8, t * P:(t + 1) * P].rearrange("p (g j) q -> p g j q", j=2),
                   ps[:, 5 + 2 * t, :].rearrange("p (g j q) -> p g j q", g=2, j=2),
                   gout[:, :].unsqueeze(1).unsqueeze(3).to_broadcast([P, 2, 2, P]), ALU.mult).then_inc(g_yT_dve, 1)
            mixer_added(1, go_done, 0, go_add)

        dve.wait_ge(in_h, 48)
        norm(0)
        mla()
        moe(0)
        norm(2)
        gla()
        moe(1)


NAMES = ["x", "meta_tokens", "norm_mix", "norm_ffn", "mla_w_in", "mla_g_q", "mla_w_uq", "mla_g_kv", "mla_w_ukv",
         "mla_g_qn", "mla_g_kn", "mla_w_o", "gla_w_in", "gla_w_gate_up", "gla_b_gate", "gla_g_out", "gla_w_o",
         "moe_w_rg", "moe_b_rg", "moe_w_re", "moe_b_re", "moe_w_gate", "moe_w_up", "moe_w_down"]


def kernel(**inputs):
    import concourse.bacc as bacc
    from concourse.bass_utils import run_bass_kernel_spmd

    nc = bacc.Bacc("TRN2", target_bir_lowering=False, num_devices=1)
    table, rows, _ = constants()
    arrays = {n: np.ascontiguousarray(inputs[n]) for n in NAMES}
    arrays["const"], arrays["mask_rows"] = table, rows
    aps = {n: nc.dram_tensor(f"in_{n}", v.shape, F32, kind="ExternalInput").ap() for n, v in arrays.items()}
    out = nc.dram_tensor("out_0", (1, SEQ, D), F32, kind="ExternalOutput").ap()
    program(nc, aps, out)
    r = run_bass_kernel_spmd(nc, [{f"in_{n}": v for n, v in arrays.items()}], core_ids=[0])
    return r.results[0]["out_0"]
```

```python
from contextlib import ExitStack

import numpy as np

import concourse.bass as bass
from concourse import mybir

F32 = mybir.dt.float32
BF16 = mybir.dt.bfloat16
I32 = mybir.dt.int32
ALU = mybir.AluOpType
ACT = mybir.ActivationFunctionType
AX = mybir.AxisListType

P = 128
D = 1024
KD = D // P
SEQ, META = 256, 16
POS = META + SEQ
CHUNK = 64
COL = [META, META + P, 0]
WID = [P, P, META]
QUAD = 32
EPS = 1e-6

HEADS, NOPE, ROPE, VD = 16, 64, 32, 64
MH = HEADS // 4
QK = NOPE + ROPE
QR, KVR = 384, 256
ZA, ZB = QR, KVR + ROPE
MASK_ROWS = 2
BIG = 1e30

GH, GDK, GDV, GRANK, TAU = 4, 128, 256, 16, 16.0
SUB = 32
NSUB = SEQ // SUB

NG, EPG, NE, FE = 4, 8, 32, 256
SLOTS = 32
GE = 4
GROUPS = NE // GE
OFF = 1000.0
COMBINE = [0, 1, 7, 3, 4, 2]
ROUNDS = -(-POS // SLOTS) - 1


def constants():
    parts, at, w = [], {}, 0

    def put(name, a):
        nonlocal w
        full = np.zeros((P, a.shape[1]), np.float32)
        full[:a.shape[0]] = a
        parts.append(full)
        at[name] = (w, w + a.shape[1])
        w += a.shape[1]

    pr = np.arange(P)
    put("ident", np.eye(P))
    put("before", (pr[:, None] < pr[None, :]).astype(np.float32))
    put("ones", np.ones((P, POS)))
    put("slot", np.tile(np.arange(SLOTS) - OFF, (P, 1)))
    put("first", np.tile(np.arange(NE, 0, -1), (P, 1)))
    valid = np.ones((P, 3))
    valid[META:, 2] = 0
    put("valid", valid)
    col = np.arange(POS)
    put("causal", np.concatenate([(col[None, :] <= (COL[i] + pr)[:, None]) for i in (0, 1)], 1))
    half = ROPE // 2
    inv = 1.0 / (np.float32(10000.0) ** (np.arange(half, dtype=np.float32) / np.float32(half)))
    pos = np.stack([COL[0] + pr, COL[1] + pr, np.minimum(pr % QUAD, META - 1)], 1).astype(np.float32)
    ang = (pos[:, :, None] * inv.astype(np.float32)).astype(np.float32)
    cos, sin = np.cos(ang), np.sin(ang)
    put("cos", np.concatenate([cos, cos], 2).reshape(P, -1))
    put("sin", np.concatenate([sin, sin], 2).reshape(P, -1))
    cid = np.where(col < META, 0, 1 + (col - META) // CHUNK)
    rows = np.zeros((2, MASK_ROWS, POS), np.float32)
    for m in range(MASK_ROWS):
        rows[0, m] = cid == 2 * m + 1
        rows[1, m] = np.where(cid == 2 * m + 2, -BIG, 0.0)
    return np.ascontiguousarray(np.concatenate(parts, 1), dtype=np.float32), rows, at


class Links:

    def __init__(self, eng, sem):
        self.eng, self.sem, self.n = eng, sem, 0

    def __call__(self, ins):
        self.n += 1
        ins.then_inc(self.sem, 1)
        self.eng.wait_ge(self.sem, self.n)


def program(nc, a, out):
    with ExitStack() as ctx:
        build(nc, a, out, ctx)


def build(nc, a, out, ctx):
    def sb(name, shape, dt=F32):
        return ctx.enter_context(nc.sbuf_tensor(name, shape, dt))

    def sem(name):
        return ctx.enter_context(nc.semaphore(name))

    _, _, at = constants()
    CW = max(e for _, e in at.values())

    cst = sb("cst", [P, CW])

    def c(name):
        return cst[:, at[name][0]:at[name][1]]

    ident, before, ones = c("ident"), c("before"), c("ones")
    h = sb("h", [P, 3, D])
    xn = sb("xn", [P, 3, KD, P])
    hT = sb("hT", [P, KD, POS])
    PART = 8192
    ring = sb("ring", [P, 3 * PART])
    RA, RB, RD = (ring[:, i * PART:(i + 1) * PART] for i in range(3))
    gn = sb("gn", [P, 4, KD])
    flag = sb("flag", [1, 2], I32)
    marker = sb("marker", [1, 2])
    ssq = sb("ssq", [P, 3])
    rstd = sb("rstd", [P, 3])
    fix = sb("fix", [P, 3])
    eps_b, epsqk_b, one_b = (fix[:, i:i + 1] for i in range(3))
    wr = sb("wr", [P, 2, KD, NG + NE])
    rb = sb("rb", [P, 2, NG + NE])
    wlr = sb("wlr", [P, KD, GRANK])
    wgu = sb("wgu", [P, GH * GDK])
    bg = sb("bg", [P, GH])
    gout = sb("gout", [P, GDV // P])
    before01, ones01 = (sb(n, [P, P], BF16)[:, :] for n in ("before01", "ones01"))
    sel01 = sb("sel01", [P, 3, NE], BF16)
    ARENA = 17300
    arena = sb("arena", [P, ARENA])
    top = [0]

    def take(*shape):
        n = int(np.prod(shape))
        assert top[0] + n <= ARENA, (top[0], n)
        v = arena[:, top[0]:top[0] + n]
        top[0] += n
        if len(shape) == 2:
            v = v.rearrange("p (a b) -> p a b", a=shape[0])
        if len(shape) == 3:
            v = v.rearrange("p (a b c) -> p a b c", a=shape[0], b=shape[1])
        return v

    L = take(3, NG + NE)
    E5 = take(3, NG + 1)
    le, s1, s2, sel = (take(3, NE) for _ in range(4))
    rm, gates = take(3, NE + GE), take(3, NE + GE)
    mg, m1, m2, pm, w1, w2 = (take(3) for _ in range(6))
    g4 = take(3, NG)
    most = take(1)
    lgT = take(POS)
    shared = top[0]
    Sg, Gg = take(3, GE * SLOTS), take(3, GE * SLOTS)
    xe = take(KD, P)
    ex = take(FE)
    hid, hidT = take(2, P), take(2, P)
    GT = take(POS)
    ysb = take(D)
    assert top[0] <= ARENA - PART
    RA1 = arena[:, ARENA - PART:]
    top[0] = shared
    vt = take(3, HEADS, VD)
    qT, kT = take(HEADS, POS), take(HEADS, POS)
    zst, zrs = take(3, 2), take(3, 2)
    junk = take(QR + KVR)
    kr, krs = take(3, ROPE), take(3)
    tcq, tsq, tck, tsk = (take(3, ROPE) for _ in range(4))
    gqk = take(2, QK)
    gcol, gprod, gc5 = take(2), take(1), take(5)
    qst, kst, scl, krst = (take(3, HEADS) for _ in range(4))
    mx, rs, nb, ri = ([take(2), take(2)] for _ in range(4))
    mmx, mri = take(MH), take(MH)
    mp = take(MH, META)
    mpT = take(HEADS, META)
    att_top = top[0]
    cT = take(5, POS)
    rp = take(2, HEADS * ROPE)
    rpp = hT[:, :, :].rearrange("p k n -> p (k n)")[:, 0:4 * HEADS * ROPE].rearrange("p (i m n) -> p i m n", i=2, m=2)
    top[0] = att_top
    PR = COL[1] + POS
    prob = [take(PR), take(PR)]
    pT = [take(3 * P), take(3 * P)]
    pM = [take(SEQ), take(SEQ)]
    oT = hT
    xflat = xn[:, :, :, :].rearrange("p a k q -> p (a k q)")

    def heads(ap, n=HEADS):
        return ap.rearrange("p (h f) -> p h f", h=n)

    QW = HEADS * QK
    q_sb = [heads(xflat[:, 0:QW]), heads(ring[:, 0:QW]), heads(ring[:, 2 * QW:2 * QW + MH * QK], MH)]
    k_sb = [heads(xflat[:, QW:2 * QW]), heads(ring[:, QW:2 * QW]),
            heads(ring[:, 2 * QW + MH * QK:2 * QW + 2 * MH * QK], MH)]
    o_sq = 2 * QW + 2 * MH * QK
    sq = heads(ring[:, o_sq:o_sq + QW])
    top[0] = shared
    gqT = take(GH, SEQ)
    gkT = take(GH, POS)
    ga, gb, gt = take(GH, POS), take(GH, POS), take(GH, POS)
    gv = take(3, GH * GDV)
    gr = take(2, D)
    gk = [take(GH, POS) for _ in range(3)]
    glr = take(POS)
    gos, gor = take(2, GH), take(2, GH)
    attM = take(GH, SEQ)
    gtq = gt[:, :, 0:SEQ]
    blocks = gb[:, :, META:POS].rearrange("p g (s j) -> p g s j", s=NSUB)
    ref = blocks[:, :, :, SUB // 2 - 1:SUB // 2]
    gsq = xflat[:, 2 * GH * POS:2 * GH * POS + GDV]
    att = xflat[:, 0:2 * GH * POS].rearrange("p (t g s) -> p t g s", t=2, g=GH)
    attT = [w.rearrange("p a b -> p (a b)")[:, o:o + 3 * P] for w in (ga, gt) for o in (0, 3 * P)]
    gyT = hT[:, :, META:]

    ps = ctx.enter_context(nc.psum_tensor("ps", [P, 8, 512], F32))

    names = """in_h in_c in_small in_moe in_rows w_z w_q w_kv w_mo w_gqk w_gv w_gr w_go
        act_link dve_link pool_link zeroed consts
        m_squares rstd_ok xn_act xn_dve xn_pool xn_turned hT_ok
        z_done z_rstd z_kr z_scaled c_turned cT_ok
        a_job a_act a_dve q_squared k_squared q_sums k_sums k_rstd q_ready k_ready q_roped k_roped
        mq_s mq_dif mq_exp mq_p mq_t mq_c
        s_done s_shift p_exp p_scaled p_turned pt_act pt_dve pv_done o_copied mo_done mo_add
        g_job g_act g_dve g_abs g_log gq_dif gq_exp gq_ok gk_dif gk_exp gk_ok g_att g_attm
        g_attT g_aT_act g_aT_dve g_o g_orstd g_y g_yT g_yT_act g_yT_dve go_done go_add
        lg_done lg_copied lg_turned e_dif e_exp sel_ok rank_done count_done
        flag_ok moe_done stored"""
    S = {n: sem(n) for n in names.split()}
    (in_h, in_c, in_small, in_moe, in_rows, w_z, w_q, w_kv, w_mo, w_gqk, w_gv, w_gr, w_go,
     act_link, dve_link, pool_link, zeroed, consts,
     m_squares, rstd_ok, xn_act, xn_dve, xn_pool, xn_turned, hT_ok,
     z_done, z_rstd, z_kr, z_scaled, c_turned, cT_ok,
     a_job, a_act, a_dve, q_squared, k_squared, q_sums, k_sums, k_rstd, q_ready, k_ready, q_roped, k_roped,
     mq_s, mq_dif, mq_exp, mq_p, mq_t, mq_c,
     s_done, s_shift, p_exp, p_scaled, p_turned, pt_act, pt_dve, pv_done, o_copied, mo_done, mo_add,
     g_job, g_act, g_dve, g_abs, g_log, gq_dif, gq_exp, gq_ok, gk_dif, gk_exp, gk_ok, g_att, g_attm,
     g_attT, g_aT_act, g_aT_dve, g_o, g_orstd, g_y, g_yT, g_yT_act, g_yT_dve, go_done, go_add,
     lg_done, lg_copied, lg_turned, e_dif, e_exp, sel_ok, rank_done, count_done,
     flag_ok, moe_done, stored) = S.values()

    class GroupSems:

        def __init__(self, tag, parities):
            self.a, self.b, self.d = [sem(f"{tag}_a{i}") for i in range(parities)], sem(f"{tag}_b"), sem(f"{tag}_d")
            self.a_read, self.b_read, self.d_read = sem(f"{tag}_a_read"), sem(f"{tag}_b_read"), sem(f"{tag}_d_read")
            self.send = sem(f"{tag}_send")
            self.rows = sem(f"{tag}_rows")
            self.rows_in = sem(f"{tag}_rows_in")
            self.turn = sem(f"{tag}_turn")
            self.turned = sem(f"{tag}_turned")
            self.silu = sem(f"{tag}_silu")
            self.hid = sem(f"{tag}_hid")
            self.hid_t = sem(f"{tag}_hid_t")
            self.hid_c = sem(f"{tag}_hid_c")
            self.ya, self.yd = sem(f"{tag}_ya"), sem(f"{tag}_yd")
            self.comb = sem(f"{tag}_comb")
            self.add = sem(f"{tag}_add")
            self.seen = sem(f"{tag}_seen")

    FAST = GroupSems("fast", 2)
    OVER = [GroupSems(f"over{l}", 1) for l in range(2)]

    def rep(ap, n):
        return ap.unsqueeze(2).to_broadcast([ap.shape[0], ap.shape[1], n])

    def rep3(ap, n):
        return ap.unsqueeze(3).to_broadcast([*ap.shape, n])

    def over(ap, n):
        return ap.unsqueeze(1).to_broadcast([ap.shape[0], n, ap.shape[1]])

    def flat(ap):
        return ap.rearrange("p a b -> p (a b)")

    NT = [3, 2]
    COMB0 = [0, 2 * NT[0] * GROUPS]
    ADD0 = [0, 2 * NT[0] * GROUPS + 1]
    NORM_TILES = [3, 3, 3, 2]
    NB = [sum(NORM_TILES[:i]) for i in range(5)]
    ORDER = [[0, 1, 2], [2, 0, 1], [0, 1, 2], [0, 1]]
    H_DONE = [{0: (in_h, 48), 1: (in_h, 48), 2: (in_h, 48)}, {2: (mo_add, 4), 0: (mo_add, 6), 1: (mo_add, 8)},
              {0: (moe_done, 1), 1: (moe_done, 1), 2: (moe_done, 1)}, {0: (go_add, 2), 1: (go_add, 4)}]
    N_SMALL, N_ROWS = 11, 2 * MASK_ROWS

    wz = ring[:, 0:KD * (ZA + ZB)].rearrange("p (k n) -> p k n", k=KD)
    o_q = KD * (ZA + ZB)
    wq = ring[:, o_q:o_q + 3 * HEADS * QK].rearrange("p (k n) -> p k n", k=3)
    o_kv = o_q + 3 * HEADS * QK
    wkv = ring[:, o_kv:o_kv + 2 * HEADS * (NOPE + VD)].rearrange("p (k n) -> p k n", k=2)
    o_cq = o_kv + 2 * HEADS * (NOPE + VD)
    cq = [ring[:, o_cq + i * 5 * P:o_cq + (i + 1) * 5 * P].rearrange("p (k q) -> p k q", k=5) for i in range(3)]
    assert o_sq + QW <= o_q and o_cq + 15 * P <= 2 * PART
    wmo, wqk, wv, wrr, wgo = (r.rearrange("p (k n) -> p k n", k=KD) for r in (RD, RA, RB, RD, RA))
    HK = KD // 2
    moeA0, moeA1, moeB = (r.rearrange("p (m e n) -> p m e n", m=2, e=GE) for r in (RA, RA1, RB))
    moeA = [moeA0, moeA1]
    moeD = RD.rearrange("p (e n) -> p e n", e=GE)
    VO = 2 * GH * GDK
    LRO = VO + GH * GDV
    RO = LRO + GRANK

    AJOBS = []

    def abank(j):
        return (j + 3) % 8

    for i in range(3):
        AJOBS += [("q", i, n, "act") for n in range(3 if i < 2 else 1)]
        AJOBS += [("kv", i, n, "dve") for n in range(4 if i < 2 else 1)]
    for kind, i in (("tq", 0), ("tk", 0), ("tq", 1), ("tq", 2), ("tk", 1), ("tk", 2)):
        AJOBS += [(kind, i, n, {"tq": "act", "tk": "dve"}[kind]) for n in range(4 if i < 2 else 1)]
    a_counts = {"act": 0, "dve": 0}
    a_empty = []
    for *_, who in AJOBS:
        a_counts[who] += 1
        a_empty.append(({"act": a_act, "dve": a_dve}[who], a_counts[who]))

    def ajobs(kind, i):
        return [j for j, (k, t, _, _) in enumerate(AJOBS) if (k, t) == (kind, i)]

    JOBS = [("lr", 0, "act", 0)] + [("q", n, "act", 1 + n) for n in range(GH)]
    JOBS += [("a", n, "dve", (5 + n) % 8) for n in range(GH)] + [("k", n, "act", 1 + n) for n in range(GH)]
    JOBS += [("v", n, "act", (5 + n) % 8) for n in range(5)] + [("r", n, "act", 4 + n) for n in range(4)]
    counts = {"act": 0, "dve": 0}
    emptied = []
    for _, _, who, _ in JOBS:
        counts[who] += 1
        emptied.append(({"act": g_act, "dve": g_dve}[who], counts[who]))
    before_me = [max((i for i in range(j) if JOBS[i][3] == JOBS[j][3]), default=None) for j in range(len(JOBS))]
    K_END, V_END, R_END = 13, 18, 22

    BY_ACT = [(n, i) for n in range(4) for i in ORDER[n] if i == 1 or n % 2]
    RSTD = [(n, i) for n in range(4) for i in ORDER[n] if not i or n % 2]

    def xn_ready(n, i):
        return (xn_act, BY_ACT.index((n, i)) + 1) if (n, i) in BY_ACT else ({0: xn_dve, 2: xn_pool}[i], n // 2 + 1)

    def rstd_count(n, i):
        return RSTD.index((n, i)) + 1

    block = ctx.enter_context(nc.Block())

    def overflow(eng, l):
        eng.wait_ge(flag_ok, l + 1)
        return eng.value_load(flag[0:1, l:l + 1], min_val=0, max_val=1) != 0

    @block.sync
    def _(sp):
        sp.dma_start(h[:, 0, :], a["x"][0, 0:P, :]).then_inc(in_h, 16)
        sp.dma_start(h[:, 1, :], a["x"][0, P:SEQ, :]).then_inc(in_h, 16)
        sp.wait_ge(zeroed, 1)
        sp.dma_start(h[0:META, 2, :], a["meta_tokens"]).then_inc(in_h, 16)
        sp.dma_start(cst[:, :], a["const"]).then_inc(in_c, 16)
        with nc.allow_non_contiguous_dma(reason="gains, a column per block"):
            for n in range(4):
                src = a["norm_mix" if n % 2 == 0 else "norm_ffn"][n // 2]
                sp.dma_start(gn[:, n, :], src.rearrange("(p k) -> p k", k=KD)).then_inc(in_small, 16)
            sp.dma_start(gc5[:, 0:3], a["mla_g_q"][0].rearrange("(p k) -> p k", k=3)).then_inc(in_small, 16)
            sp.dma_start(gc5[:, 3:5], a["mla_g_kv"][0].rearrange("(p k) -> p k", k=2)).then_inc(in_small, 16)
            sp.dma_start(gcol[0:NOPE, 0:1], a["mla_g_qn"][0, 0:NOPE].rearrange("(p o) -> p o", o=1)).then_inc(in_small, 16)
            sp.dma_start(gcol[0:NOPE, 1:2], a["mla_g_kn"][0, 0:NOPE].rearrange("(p o) -> p o", o=1)).then_inc(in_small, 16)
            sp.dma_start(bg[:, :], a["gla_b_gate"][0].rearrange("(g p) -> p g", p=P)).then_inc(in_small, 16)
        sp.dma_start(gqk[:, 0, :], a["mla_g_qn"].to_broadcast([P, QK])).then_inc(in_small, 16)
        sp.dma_start(gqk[:, 1, :], a["mla_g_kn"].to_broadcast([P, QK])).then_inc(in_small, 16)
        sp.dma_start(wz, a["mla_w_in"][0].rearrange("(p k) n -> p k n", k=KD)).then_inc(w_z, 16)
        sp.dma_start(wq, a["mla_w_uq"][0].rearrange("(p k) n -> p k n", k=3)).then_inc(w_q, 16)
        sp.dma_start(wkv, a["mla_w_ukv"][0].rearrange("(p k) n -> p k n", k=2)).then_inc(w_kv, 16)
        for m, t in ((0, qT), (1, kT)):
            for r in range(MASK_ROWS):
                sp.dma_start(t[QK + r:QK + r + 1, :, :],
                             a["mask_rows"][m, r:r + 1].unsqueeze(1).to_broadcast([1, HEADS, POS])).then_inc(in_rows, 16)
        sp.dma_start(wmo, a["mla_w_o"][0].rearrange("(k p) n -> p k n", p=P)).then_inc(w_mo, 16)
        for l in range(2):
            sp.dma_start(wr[:, l, :, 0:NG], a["moe_w_rg"][l].rearrange("(p k) n -> p k n", k=KD)).then_inc(in_moe, 16)
            sp.dma_start(wr[:, l, :, NG:], a["moe_w_re"][l].rearrange("(p k) n -> p k n", k=KD)).then_inc(in_moe, 16)
            sp.dma_start(rb[:, l, 0:NG], a["moe_b_rg"][l:l + 1].to_broadcast([P, NG])).then_inc(in_moe, 16)
            sp.dma_start(rb[:, l, NG:], a["moe_b_re"][l:l + 1].to_broadcast([P, NE])).then_inc(in_moe, 16)
        sp.dma_start(wlr[:, :, :], a["gla_w_in"][0].rearrange("(p k) n -> p k n", k=KD)[:, :, LRO:RO]).then_inc(in_moe, 16)
        sp.dma_start(wgu[0:GRANK, :], a["gla_w_gate_up"][0]).then_inc(in_moe, 16)
        with nc.allow_non_contiguous_dma(reason="gains, a column per block"):
            sp.dma_start(gout[:, :], a["gla_g_out"][0].rearrange("(k p) -> p k", p=P)).then_inc(in_moe, 16)

        def load(l, K, g, part, odd=0):
            if part == "D":
                src = a["moe_w_down"][l].rearrange("(g e) (p k) n -> g p e (k n)", e=GE, k=2)
                sp.dma_start(moeD, src[bass.ds(g, 1)].rearrange("g p e n -> (g p) e n")).then_inc(K.d, 16)
                return
            dst, lo, landed = (moeA[odd], 0, K.a[odd]) if part == "A" else (moeB, HK, K.b)
            for m, name in ((0, "moe_w_gate"), (1, "moe_w_up")):
                src = a[name][l].rearrange("(g e) (p k) n -> g p e (k n)", e=GE, k=KD)
                sp.dma_start(dst[:, m], src[bass.ds(g, 1), :, :, lo * FE:(lo + HK) * FE]
                             .rearrange("g p e n -> (g p) e n")).then_inc(landed, 16)

        def experts(l, first):
            K = FAST
            for part, group, wait in first:
                sp.wait_ge(*wait)
                load(l, K, group, part, group % 2)

            def follow(g, n, odd):
                sp.wait_ge(K.b_read, n)
                sp.sem_inc(K.seen, 1)
                load(l, K, g, "B")
                sp.wait_ge(K.d_read, n)
                sp.sem_inc(K.seen, 1)
                load(l, K, g, "D")
                if odd is not None:
                    sp.wait_ge(K.a_read, n)
                    sp.sem_inc(K.seen, 1)
                    load(l, K, g + 1, "A", odd)

            with sp.Fori(0, GROUPS // 2 - 1) as i:
                for u in range(2):
                    follow(2 * i + (1 + u), 2 * i + (1 + u + GROUPS * l), u)
            follow(GROUPS - 1, GROUPS * (l + 1) - 1, None)
            with sp.If(overflow(sp, l)):
                K = OVER[l]
                for s in (FAST.a_read, FAST.b_read, FAST.d_read):
                    sp.wait_ge(s, GROUPS * (l + 1))
                with sp.Fori(0, ROUNDS) as r:
                    with sp.Fori(0, GROUPS) as g:
                        for part in "ABD":
                            load(l, K, g, part)
                        for s in (K.a_read, K.b_read, K.d_read):
                            sp.wait_ge(s, r * GROUPS + g + 1)
                        sp.sem_inc(K.seen, 1)

        sp.wait_ge(k_sums, 3)
        turned = (a_job, len(AJOBS))
        experts(0, [("A", 0, turned), ("B", 0, turned), ("A", 1, (mo_done, 5)), ("D", 0, (mo_done, 8))])
        gw_in = a["gla_w_in"][0].rearrange("(p k) n -> p k n", k=KD)
        sp.wait_ge(FAST.a_read, GROUPS)
        sp.dma_start(wqk, gw_in[:, :, 0:VO]).then_inc(w_gqk, 16)
        sp.wait_ge(FAST.b_read, GROUPS)
        sp.dma_start(wv, gw_in[:, :, VO:LRO]).then_inc(w_gv, 16)
        sp.wait_ge(FAST.d_read, GROUPS)
        sp.dma_start(wrr, gw_in[:, :, RO:RO + D]).then_inc(w_gr, 16)
        sp.wait_ge(g_job, K_END)
        sp.dma_start(wgo, a["gla_w_o"][0].rearrange("(k p) n -> p k n", p=P)).then_inc(w_go, 16)
        experts(1, [("B", 0, (g_job, V_END)), ("D", 0, (g_job, R_END)), ("A", 1, (g_yT, 2)), ("A", 0, (go_done, 4))])
        for i in range(2):
            sp.wait_ge(moe_done, 2)
            sp.dma_start(out[0, i * P:(i + 1) * P, :], h[:, i, :]).then_inc(stored, 16)
        sp.wait_ge(stored, 32)

    @block.gpsimd
    def _(pool):
        link = Links(pool, pool_link)

        def meta_scaled(n):
            pool.wait_ge(rstd_ok, rstd_count(n, 0))
            pool.tensor_scalar(xn[:, 2], h[:, 2, :].rearrange("p (q k) -> p k q", k=KD), rstd[:, 2:3], None,
                               ALU.mult).then_inc(xn_pool, 1)

        pool.memset(h[:, 2, :], 0.0).then_inc(zeroed, 1)
        pool.memset(eps_b, EPS).then_inc(consts, 1)
        pool.memset(epsqk_b, QK * EPS).then_inc(consts, 1)
        pool.memset(one_b, 1.0).then_inc(consts, 1)
        pool.memset(vt[:, 2, :, :], 0.0).then_inc(zeroed, 1)
        pool.memset(gprod, 1.0).then_inc(zeroed, 1)
        pool.memset(zst, 1.0).then_inc(zeroed, 1)
        pool.memset(mpT, 0.0).then_inc(zeroed, 1)
        pool.memset(L, 0.0).then_inc(zeroed, 1)
        pool.memset(rm, 0.0).then_inc(zeroed, 1)
        pool.memset(gates, 0.0).then_inc(zeroed, 1)
        meta_scaled(0)

        def queries_turned(i):
            x, half = q_sb[i][:, :, NOPE:QK], ROPE // 2
            ra, rb_ = (rpp[:, i, m].rearrange("p (h f) -> p h f", h=HEADS) for m in range(2))
            pool.wait_ge(q_squared, i + 1)
            pool.tensor_tensor(ra, x, over(tcq[:, i, :], HEADS), ALU.mult)
            link(pool.tensor_tensor(rb_, x, over(tsq[:, i, :], HEADS), ALU.mult))
            pool.tensor_tensor(x[:, :, 0:half], ra[:, :, 0:half], rb_[:, :, half:], ALU.subtract)
            pool.tensor_tensor(x[:, :, half:], ra[:, :, half:], rb_[:, :, 0:half], ALU.add).then_inc(q_roped, 1)

        def keys_scaled(i):
            n = HEADS if i < 2 else MH
            pool.wait_ge(k_rstd, i + 1)
            if i == 0:
                k = k_sb[i][:, :, 0:NOPE]
                pool.tensor_tensor(k, k, rep(krst[:, i, 0:n], NOPE), ALU.mult)
            pool.tensor_tensor(k_sb[i][:, :, NOPE:QK], over(kr[:, i, :], n), rep(krst[:, i, 0:n], ROPE),
                               ALU.mult).then_inc(k_roped, 1)

        pool.wait_ge(cT_ok, 3)
        queries_turned(0)
        keys_scaled(0)
        queries_turned(1)
        keys_scaled(1)
        keys_scaled(2)
        pool.wait_ge(a_act, a_counts["act"])
        pool.wait_ge(a_dve, a_counts["dve"])
        for i in range(2):
            pool.memset(pM[i], 0.0).then_inc(zeroed, 1)
        pool.wait_ge(moe_done, 1)
        pool.memset(gv[:, 2, :], 0.0).then_inc(zeroed, 1)
        pool.memset(attM, 0.0).then_inc(zeroed, 1)
        meta_scaled(2)
        pool.wait_ge(xn_turned, NB[3])
        pool.memset(att, 0.0).then_inc(zeroed, 1)
        pool.wait_ge(gq_dif, 1)
        for s in range(NSUB):
            n = META + SUB * (s + 1)
            if s >= 3:
                pool.wait_ge(g_att, s - 2)
            pool.tensor_tensor(gk[s % 3][:, :, 0:n], gb[:, :, 0:n], ref[:, :, s, :].to_broadcast([P, GH, n]),
                               ALU.subtract).then_inc(gk_dif, 1)

    @block.tensor
    def _(pe):
        def norm(n):
            for i in ORDER[n]:
                pe.wait_ge(*xn_ready(n, i))
                turn(i, xn[:, i])

        def turn(i, src):
            for k in range(KD):
                R = WID[i]
                dst = ps[:, 2 * i + k // 4, (k % 4) * P:(k % 4 + 1) * P] if i < 2 else ps[:, 4, k * R:(k + 1) * R]
                mm = pe.transpose(dst, src[0:R, k, :], ident[0:R, 0:R])
            mm.then_inc(xn_turned, 1)

        def mixer_out(l, w, done, ready):
            n = 2 * l + 1
            for i in range(2):
                for sem_, v in ready[i]:
                    pe.wait_ge(sem_, v)
                for b in range(2):
                    if (i, b) == (1, 1):
                        for t in ORDER[n][:-1]:
                            pe.wait_ge(*H_DONE[n][t])
                            turn(t, h[:, t, :].rearrange("p (q k) -> p k q", k=KD))
                    for k in range(KD):
                        mm = pe.matmul(ps[:, 2 * i + b, :], hT[:, k, META + i * P:META + (i + 1) * P],
                                       w[:, k, b * 512:(b + 1) * 512], start=k == 0, stop=k == KD - 1)
                    mm.then_inc(done, 1)
            pe.wait_ge(hT_ok, NB[n] + NORM_TILES[n] - 1)
            pe.wait_ge(in_moe, 16 * 11)
            c0 = COL[2] if NT[l] == 3 else META
            logits(l, 5, c0, COL[1])
            pe.wait_ge(*H_DONE[n][1])
            turn(1, h[:, 1, :].rearrange("p (q k) -> p k q", k=KD))
            pe.wait_ge(hT_ok, NB[n] + NORM_TILES[n])
            logits(l, 7, COL[1], POS)

        def logits(l, bank, c0, c1):
            for k in range(KD):
                mm = pe.matmul(ps[0:NG + NE, bank, 0:c1 - c0], wr[:, l, k, :], hT[:, k, c0:c1],
                               start=k == 0, stop=k == KD - 1)
            mm.then_inc(lg_done, 1)

        def meta_product(bank, src, ks, w, width):
            for n, k in enumerate(ks):
                for j in range(4):
                    mm = pe.matmul(ps[QUAD * j:QUAD * (j + 1), bank, 0:width], src[:, k, 0:QUAD],
                                   w[:, n, j * width:(j + 1) * width], start=n == 0, stop=n == len(ks) - 1)
            return mm

        def mla():
            pe.wait_ge(w_z, 16)
            for i in range(2):
                pe.wait_ge(hT_ok, i + 1)
                for n0, n1, b in ((0, ZA, 5 + 2 * i), (ZA, ZA + ZB, 6 + 2 * i)):
                    if b % 8 == 0:
                        pe.wait_ge(hT_ok, 1)
                    for k in range(KD):
                        mm = pe.matmul(ps[:, b % 8, 0:n1 - n0], hT[:, k, COL[i]:COL[i] + P],
                                       wz[:, k, n0:n1], start=k == 0, stop=k == KD - 1)
                mm.then_inc(z_done, 1)
            pe.wait_ge(hT_ok, 3)
            for k in range(KD):
                pe.matmul(ps[0:QUAD, 1, 0:ZA], hT[:, k, 0:QUAD], wz[:, k, 0:ZA], start=k == 0, stop=k == KD - 1)
                mm = pe.matmul(ps[QUAD:2 * QUAD, 2, 0:ZB], hT[:, k, 0:QUAD], wz[:, k, ZA:ZA + ZB],
                               start=k == 0, stop=k == KD - 1)
            mm.then_inc(z_done, 1)

            def latents_turned(i):
                pe.wait_ge(z_scaled, i + 1)
                R = WID[i]
                for k in range(5):
                    q = QUAD if i == 2 and k >= 3 else 0
                    b, o = (3 + 2 * i, k * R) if k < 3 else ((4 + 2 * i) % 8, (k - 3) * R)
                    mm = pe.transpose(ps[:, b, o:o + R], cq[i][q:q + R, k, :], ident[q:q + R, q:q + R])
                mm.then_inc(c_turned, 1)

            latents_turned(0)
            pe.wait_ge(w_q, 16)
            pe.wait_ge(w_kv, 16)
            for j, (kind, i, n, _) in enumerate(AJOBS):
                b = abank(j)
                if j >= 8:
                    pe.wait_ge(*a_empty[j - 8])
                elif j == 0:
                    pe.wait_ge(cT_ok, 1)
                elif j == 2:
                    latents_turned(1)
                    pe.wait_ge(cT_ok, 2)
                elif j == 4:
                    latents_turned(2)
                    pe.wait_ge(cT_ok, 3)
                ks, w, width = (range(3), wq, 512) if kind == "q" else (range(3, 5), wkv, 512)
                if kind in ("q", "kv") and i < 2:
                    for m, k in enumerate(ks):
                        mm = pe.matmul(ps[:, b, :], cT[:, k, COL[i]:COL[i] + P], w[:, m, n * 512:(n + 1) * 512],
                                       start=m == 0, stop=k == ks[-1])
                elif kind in ("q", "kv"):
                    mm = meta_product(b, cT, ks, w, MH * QK if kind == "q" else MH * (NOPE + VD))
                else:
                    if kind == "tk" or i < 2:
                        pe.wait_ge(q_roped if kind == "tq" else k_roped, i + 1)
                    if kind == "tk" and i:
                        pe.wait_ge(k_ready, i)
                    if kind == "tq" and i == 2:
                        pe.wait_ge(q_ready, 1)
                    src = (q_sb if kind == "tq" else k_sb)[i]
                    for m in range(4):
                        mm = pe.transpose(ps[0:QK, b, m * P:(m + 1) * P], src[:, 4 * n + m, :], ident)
                mm.then_inc(a_job, 1)
            pe.wait_ge(a_act, a_counts["act"])
            pe.wait_ge(a_dve, a_counts["dve"])
            pe.wait_ge(in_rows, 16 * N_ROWS)
            KM = QK + MASK_ROWS

            def scores(hd):
                if hd >= 2:
                    pe.wait_ge(p_exp, hd - 1)
                pe.matmul(ps[:, hd % 2, 0:COL[1]], qT[0:KM, hd, META:META + P], kT[0:KM, hd, 0:COL[1]],
                          start=True, stop=True)
                pe.matmul(ps[:, hd % 2, COL[1]:PR], qT[0:KM, hd, COL[1]:POS], kT[0:KM, hd, :],
                          start=True, stop=True).then_inc(s_done, 1)

            def weights(hd):
                pe.wait_ge(p_scaled, hd + 1)
                if hd >= 2:
                    pe.wait_ge(pt_dve, hd - 1)
                    pe.wait_ge(pt_act, hd - 1)
                pr, b, o = prob[hd % 2], 2 + 2 * (hd % 2), COL[1]
                pe.transpose(ps[:, b, 0:P], pr[:, META:META + P], ident)
                pe.transpose(ps[:, b, P:2 * P], pr[:, o + META:o + META + P], ident)
                pe.transpose(ps[:, b, 2 * P:3 * P], pr[:, o + COL[1]:o + POS], ident)
                pe.transpose(ps[0:META, b + 1, 0:P], pr[:, 0:META], ident)
                pe.transpose(ps[0:META, b + 1, P:2 * P], pr[:, o:o + META], ident).then_inc(p_turned, 1)

            def values(hd):
                pe.wait_ge(pt_dve, hd + 1)
                pe.wait_ge(pt_act, hd + 1)
                if hd % 2 == 0 and hd >= 4:
                    pe.wait_ge(o_copied, hd // 2 - 1)
                dst = ps[VD * (hd % 2):VD * (hd % 2) + VD, 6 + hd // 2 % 2, :]
                t = pT[hd % 2]
                pe.matmul(dst[:, 0:META], vt[:, 2, hd, :], mpT[:, hd, :], start=True, stop=True)
                pe.matmul(dst[:, META:POS], vt[:, 2, hd, :], pM[hd % 2], start=True, stop=False)
                pe.matmul(dst[:, META:POS], vt[:, 0, hd, :], t[:, 0:2 * P], start=False, stop=False)
                pe.matmul(dst[:, COL[1]:POS], vt[:, 1, hd, :], t[:, 2 * P:3 * P], start=False, stop=True)\
                  .then_inc(pv_done, 1)

            for s in range(MH):
                for j in range(4):
                    hd = j * MH + s
                    mm = pe.matmul(ps[QUAD * j:QUAD * (j + 1), 7, s * META:(s + 1) * META], qT[0:KM, hd, 0:QUAD],
                                   kT[0:KM, hd, 0:META], start=True, stop=True)
            mm.then_inc(mq_s, 1)
            scores(0)
            scores(1)
            pe.wait_ge(mq_p, 1)
            for s in range(MH):
                mm = pe.transpose(ps[0:META, 6, s * P:(s + 1) * P], mp[:, s, :], ident)
            mm.then_inc(mq_t, 1)
            pe.wait_ge(mq_c, 1)
            for hd in range(HEADS):
                if hd + 2 < HEADS:
                    scores(hd + 2)
                weights(hd)
                if hd:
                    values(hd - 1)
            values(HEADS - 1)
            pe.wait_ge(w_mo, 16)
            pe.wait_ge(o_copied, HEADS // 2)
            meta_product(4, oT, range(KD), wmo, D // 4).then_inc(mo_done, 4)
            mixer_out(0, wmo, mo_done, [[], []])

        def moe(l):
            nt = NT[l]
            for m, i in enumerate(ORDER[2 * l + 1]):
                if m == 0:
                    pe.wait_ge(lg_copied, 2 * l + 1)
                if i == 1:
                    pe.wait_ge(lg_copied, 2 * l + 2)
                mm = pe.transpose(ps[0:WID[i], 6, (NG + NE) * i:(NG + NE) * (i + 1)],
                                  lgT[0:NG + NE, COL[i]:COL[i] + WID[i]], ident[0:NG + NE, 0:NG + NE])
            mm.then_inc(lg_turned, 1)
            pe.wait_ge(sel_ok, l + 1)
            for i in range(nt):
                for j in range(i + 1):
                    mm = pe.matmul(ps[:, 7, NE * i:NE * (i + 1)], before01 if j == i else ones01, sel01[:, j, :],
                                   start=j == 0, stop=j == i)
            mm.then_inc(rank_done, 1)
            for j in range(nt):
                mm = pe.matmul(ps[:, 5, 0:NE], ones01, sel01[:, j, :], start=j == 0, stop=j == nt - 1)
            mm.then_inc(count_done, 1)
            pe.wait_ge(*xn_ready(2 * l + 1, 1))

            def group(K, n, sent, added, odd, landed_a):
                pe.wait_ge(K.send, 2 * sent + (-1))
                pe.wait_ge(K.add, added)
                for k in range(KD):
                    for i in range(nt):
                        mm = pe.matmul(ps[:, k // 4, (k % 4) * P:(k % 4 + 1) * P], xn[:, i, k, :], Sg[:, i, :],
                                       start=i == 0, stop=i == nt - 1)
                    if k % 4 == 3:
                        mm.then_inc(K.rows, 1)
                pe.wait_ge(K.send, 2 * sent)
                for i in range(nt):
                    R = WID[i]
                    mm = pe.transpose(ps[:, 4, COL[i]:COL[i] + R], Gg[0:R, i, :], ident[0:R, 0:R])
                mm.then_inc(K.turn, 1)
                for part, w, landed, v, read in ((0, moeA[odd], K.a[odd], landed_a, K.a_read),
                                                 (1, moeB, K.b, 32 * n + 32, K.b_read)):
                    pe.wait_ge(K.rows_in, 2 * n + (part + 1))
                    pe.wait_ge(landed, v)
                    for kk in range(HK):
                        k = part * HK + kk
                        for m in range(2):
                            for j in range(GE):
                                mm = pe.matmul(ps[32 * j:32 * j + 32, 2, m * FE:(m + 1) * FE],
                                               xe[:, k, 32 * j:32 * j + 32], w[:, m, j, kk * FE:(kk + 1) * FE],
                                               start=k == 0 and m == 0, stop=k == KD - 1, skip_group_check=True)
                    mm.then_inc(read, 1)
                pe.wait_ge(K.hid, n + 1)
                for k in range(2):
                    mm = pe.transpose(ps[:, 3, k * P:(k + 1) * P], hid[:, k, :], ident)
                mm.then_inc(K.hid_t, 1)
                pe.wait_ge(K.hid_c, n + 1)
                pe.wait_ge(K.d, 16 * n + 16)
                for k in range(2):
                    for b in range(2):
                        for j in range(GE):
                            mm = pe.matmul(ps[32 * j:32 * j + 32, 5 + b, :], hidT[:, k, 32 * j:32 * j + 32],
                                           moeD[:, j, k * D + b * 512:k * D + (b + 1) * 512], start=k == 0, stop=k == 1)
                mm.then_inc(K.d_read, 1)
                pe.wait_ge(K.turned, n + 1)
                pe.wait_ge(K.ya, n + 1)
                pe.wait_ge(K.yd, n + 1)
                for i in range(nt):
                    for b in range(2):
                        pe.matmul(ps[0:WID[i], COMBINE[2 * i + b], :], GT[:, COL[i]:COL[i] + WID[i]],
                                  ysb[:, b * 512:(b + 1) * 512], start=True, stop=True).then_inc(K.comb, 1)

            with pe.Fori(0, GROUPS // 2) as i:
                for u in range(2):
                    group(FAST, 2 * i + (u + GROUPS * l), 2 * i + (u + (GROUPS + 1) * l + 1),
                          4 * nt * i + (2 * nt * u + ADD0[l] + 1), u, 32 * i + 32 * (l * (GROUPS // 2) + 1))
            with pe.If(overflow(pe, l)):
                with pe.Fori(0, ROUNDS) as r:
                    with pe.Fori(0, GROUPS) as g:
                        n = r * GROUPS + g
                        group(OVER[l], n, n + r + 1, 2 * nt * n + r + 1, 0, 32 * n + 32)

        def gla():
            pe.wait_ge(hT_ok, NB[3])

            def job(j):
                kind, n, _, bank = JOBS[j]
                if before_me[j] is not None:
                    pe.wait_ge(*emptied[before_me[j]])
                b = ps[:, bank, :]
                if kind == "a":
                    if n == 0:
                        pe.wait_ge(*emptied[0])
                    mm = pe.matmul(b[:, 0:POS], wgu[0:GRANK, n * GDK:(n + 1) * GDK], glr[0:GRANK, :], start=True, stop=True)
                elif kind in ("lr", "q", "k"):
                    if kind == "q" and n == 0:
                        pe.wait_ge(w_gqk, 16)
                    o = (n if kind == "q" else GH + n) * GDK
                    c0 = META if kind == "q" else 0
                    for k in range(KD):
                        w = wlr[:, k, :] if kind == "lr" else wqk[:, k, o:o + GDK]
                        mm = pe.matmul(b[0:w.shape[1], 0:POS - c0], w, hT[:, k, c0:POS], start=k == 0, stop=k == KD - 1)
                elif kind == "v" and n == 4:
                    mm = meta_product(bank, hT, range(KD), wv, GDV)
                else:
                    i, hb = divmod(n, 2)
                    if n == 0:
                        pe.wait_ge(w_gv if kind == "v" else w_gr, 16)
                    w = wv if kind == "v" else wrr
                    for k in range(KD):
                        mm = pe.matmul(b[0:WID[i], :], hT[:, k, COL[i]:COL[i] + WID[i]],
                                       w[:, k, hb * 512:(hb + 1) * 512], start=k == 0, stop=k == KD - 1)
                mm.then_inc(g_job, 1)

            for j in range(V_END):
                job(j)
            pe.wait_ge(*emptied[V_END - 1])
            pe.wait_ge(gq_ok, 1)
            for s in range(NSUB):
                t, j = divmod(s, NSUB // 2)
                n = META + SUB * (s + 1)
                if s == NSUB // 2:
                    pe.wait_ge(g_attm, s)
                pe.wait_ge(gk_ok, s + 1)
                for g in range(GH):
                    mm = pe.matmul(ps[32 * j:32 * j + 32, g, 0:n], gqT[:, g, s * SUB:(s + 1) * SUB],
                                   gk[s % 3][:, g, 0:n], start=True, stop=True)
                mm.then_inc(g_att, 1)
                if s < NSUB // 2:
                    job(V_END + s)
            pe.wait_ge(g_attm, NSUB)
            pe.wait_ge(*emptied[R_END - 1])
            for g in range(GH):
                pe.transpose(ps[:, 2 * g, 0:P], att[:, 0, g, META:META + P], ident)
                pe.transpose(ps[:, 2 * g, P:2 * P], att[:, 1, g, META:META + P], ident)
                pe.transpose(ps[:, 2 * g, 2 * P:3 * P], att[:, 1, g, META + P:POS], ident)
                for t in range(2):
                    mm = pe.transpose(ps[0:META, 2 * g + 1, t * P:(t + 1) * P], att[:, t, g, 0:META], ident)
                mm.then_inc(g_attT, 1)
            pe.wait_ge(g_aT_act, GH)
            pe.wait_ge(g_aT_dve, GH)
            for t in range(2):
                for g in range(GH):
                    dst = ps[:, 2 * t + g // 2, (g % 2) * GDV:(g % 2 + 1) * GDV]
                    cols = slice(g * GDV, (g + 1) * GDV)
                    pe.matmul(dst, attM[:, g, t * P:(t + 1) * P], gv[:, 2, cols], start=True, stop=False)
                    mm = pe.matmul(dst, attT[g][:, t * P:(t + 1) * P], gv[:, 0, cols], start=False, stop=t == 0)
                    if t:
                        mm = pe.matmul(dst, attT[g][:, 2 * P:3 * P], gv[:, 1, cols], start=False, stop=True)
                mm.then_inc(g_o, 1)
            for t in range(2):
                pe.wait_ge(g_y, t + 1)
                for k in range(KD):
                    mm = pe.transpose(ps[:, 4 + 2 * t + k // 4, (k % 4) * P:(k % 4 + 1) * P],
                                      gr[:, t, k * P:(k + 1) * P], ident)
                mm.then_inc(g_yT, 1)
            mixer_out(1, wgo, go_done, [[(w_go, 16), (g_yT_act, 1), (g_yT_dve, 1)], [(g_yT_act, 2), (g_yT_dve, 2)]])

        pe.wait_ge(in_c, 16)
        norm(0)
        mla()
        moe(0)
        norm(2)
        gla()
        moe(1)

    @block.scalar
    def _(act):
        link = Links(act, act_link)

        def square(n, i):
            act.wait_ge(*H_DONE[n][i])
            return act.activation(xflat[:, i * D:(i + 1) * D], h[:, i, :], ACT.Square, scale=D ** -0.5,
                                  accum_out=ssq[:, i:i + 1])

        def scale_of(n, i):
            link(square(n, i))
            v = ssq[:, i:i + 1]
            link(act.activation(v, v, ACT.Ln, bias=eps_b))
            return act.activation(rstd[:, i:i + 1], v, ACT.Exp, scale=-0.5)

        def scaled(i):
            act.activation(xn[:, i], h[:, i, :].rearrange("p (q k) -> p k q", k=KD), ACT.Copy,
                           scale=rstd[:, i:i + 1]).then_inc(xn_act, 1)

        def norm(n):
            for i in range(2):
                ins = square(n, i)
            link(ins)
            act.wait_ge(m_squares, n // 2 + 1)
            link(act.activation(ssq[:, :], ssq[:, :], ACT.Ln, bias=eps_b))
            act.activation(rstd[:, :], ssq[:, :], ACT.Exp, scale=-0.5).then_inc(rstd_ok, 1)
            act.wait_ge(rstd_ok, rstd_count(n, 0))
            scaled(1)

        def mla():
            act.wait_ge(zeroed, 8)
            for i in range(3):
                act.wait_ge(z_done, i + 1)
                if i < 2:
                    ba, bb, ra, rb_ = (5 + 2 * i) % 8, (6 + 2 * i) % 8, slice(0, P), slice(0, P)
                    link(act.copy(kr[:, i, :], ps[:, bb, KVR:KVR + ROPE]))
                else:
                    ba, bb, ra, rb_ = 1, 2, slice(0, QUAD), slice(QUAD, 2 * QUAD)
                    for j in range(4):
                        ins = act.copy(kr[QUAD * j:QUAD * (j + 1), i, :], ps[rb_, bb, KVR:KVR + ROPE])
                    link(ins)
                act.activation(junk[:, 0:ROPE], kr[:, i, :], ACT.Square, scale=QK ** -0.5,
                               accum_out=krs[:, i:i + 1]).then_inc(z_kr, 1)
                act.wait_ge(z_kr, i + 1)
                act.activation(junk[ra, 0:QR], ps[ra, ba, 0:QR], ACT.Square, scale=QR ** -0.5,
                               accum_out=zst[ra, i, 0:1])
                link(act.activation(junk[rb_, QR:], ps[rb_, bb, 0:KVR], ACT.Square, scale=KVR ** -0.5,
                                    accum_out=zst[rb_, i, 1:2]))
                link(act.activation(zst[:, i, :], zst[:, i, :], ACT.Ln, bias=eps_b))
                act.activation(zrs[:, i, :], zst[:, i, :], ACT.Exp, scale=-0.5).then_inc(z_rstd, 1)

            def copies(i):
                H = HEADS if i < 2 else MH
                act.wait_ge(z_done, 3)
                W = 512 if i < 2 else MH * QK
                for n, j in enumerate(ajobs("q", i)):
                    act.wait_ge(a_job, j + 1)
                    act.copy(flat(q_sb[i])[:, n * W:(n + 1) * W], ps[:, abank(j), 0:W]).then_inc(a_act, 1)
                act.wait_ge(a_act, a_empty[j][1])
                if i:
                    act.wait_ge(k_sums, i)
                act.activation(sq[:, 0:H], q_sb[i], ACT.Square, scale=QK ** -0.5).then_inc(q_squared, 1)
                act.wait_ge(q_sums, i + 1)
                act.wait_ge(*a_empty[ajobs("kv", i)[-1]])
                act.activation(sq[:, 0:H, 0:NOPE], k_sb[i][:, :, 0:NOPE], ACT.Square, scale=QK ** -0.5)\
                    .then_inc(k_squared, 1)

            def scales(tiles, queries):
                n = lambda i: slice(0, HEADS if i < 2 else MH)
                act.wait_ge(k_sums, tiles[-1] + 1)
                for i in queries:
                    act.activation(qst[:, i, n(i)], qst[:, i, n(i)], ACT.Ln, scale=float(QK), bias=epsqk_b)
                for i in tiles:
                    ins = act.activation(kst[:, i, n(i)], kst[:, i, n(i)], ACT.Ln, bias=eps_b)
                link(ins)
                for i in tiles:
                    act.activation(krst[:, i, n(i)], kst[:, i, n(i)], ACT.Exp, scale=-0.5).then_inc(k_rstd, 1)
                for i in queries:
                    act.activation(scl[:, i, n(i)], qst[:, i, n(i)], ACT.Exp, scale=-0.5)

            def turned(i):
                for n, j in enumerate(ajobs("tq", i)):
                    act.wait_ge(a_job, j + 1)
                    src = ps[0:QK, abank(j), :].rearrange("p (h t) -> p h t", h=4)
                    if i < 2:
                        ins = act.copy(qT[0:QK, 4 * n:4 * n + 4, COL[i]:COL[i] + P], src)
                    else:
                        ins = act.copy(qT[0:QK, :, 0:META].rearrange("p (j s) t -> p s j t", j=4),
                                       src.rearrange("p s (j t) -> p s j t", j=4)[:, :, :, 0:META])
                    ins.then_inc(a_act, 1)

            copies(0)
            scales([0], [])
            copies(1)
            copies(2)
            turned(0)
            scales([1, 2], [0, 1, 2])
            turned(1)
            turned(2)

            def exps(hd):
                act.wait_ge(s_shift, hd + 1)
                if hd >= 2:
                    act.wait_ge(p_turned, hd - 1)
                for i, o, n in ((0, 0, COL[1]), (1, COL[1], POS)):
                    ins = act.activation(prob[hd % 2][:, o:o + n], ps[:, hd % 2, o:o + n], ACT.Exp,
                                         bias=nb[hd % 2][:, i:i + 1], scale=scl[:, i, hd:hd + 1],
                                         accum_out=rs[hd % 2][:, i:i + 1])
                ins.then_inc(p_exp, 1)

            def meta_weights(hd):
                act.wait_ge(p_turned, hd + 1)
                if hd >= 2:
                    act.wait_ge(pv_done, hd - 1)
                act.copy(pM[hd % 2][0:META, :], ps[0:META, 3 + 2 * (hd % 2), 0:SEQ]).then_inc(pt_act, 1)

            def heads_out(hp):
                act.wait_ge(pv_done, 2 * hp + 2)
                act.copy(oT[:, hp, :], ps[:, 6 + hp % 2, 0:POS]).then_inc(o_copied, 1)

            act.wait_ge(a_dve, a_counts["dve"])
            act.wait_ge(zeroed, 10)
            act.wait_ge(mq_dif, 1)
            act.activation(mp, mp, ACT.Exp).then_inc(mq_exp, 1)
            exps(0)
            for hd in range(HEADS):
                if hd + 1 < HEADS:
                    exps(hd + 1)
                meta_weights(hd)
                if hd >= 3 and hd % 2:
                    heads_out((hd - 3) // 2)
            heads_out(HEADS // 2 - 1)

        def moe(l):
            n = 2 * l + 1
            c0 = 0 if NT[l] == 3 else META
            for i in ORDER[n]:
                scale_of(n, i).then_inc(rstd_ok, 1)
                act.wait_ge(rstd_ok, rstd_count(n, i))
                if i != 1:
                    scaled(i)
            for m, (bank, lo, hi) in enumerate(((5, c0, COL[1]), (7, COL[1], POS))):
                act.wait_ge(lg_done, 2 * l + m + 1)
                act.copy(lgT[0:NG + NE, lo:hi], ps[0:NG + NE, bank, 0:hi - lo]).then_inc(lg_copied, 1)
            scaled(1)
            act.wait_ge(e_dif, l + 1)
            act.activation(E5[:, 0:NT[l], :], E5[:, 0:NT[l], :], ACT.Exp).then_inc(e_exp, 1)

            def group(K, n):
                act.wait_ge(K.turn, n + 1)
                act.copy(GT[:, c0:POS], ps[:, 4, c0:POS]).then_inc(K.turned, 1)
                act.wait_ge(K.b_read, n + 1)
                act.activation(ex, ps[:, 2, 0:FE], ACT.Silu).then_inc(K.silu, 1)
                act.wait_ge(K.hid_t, n + 1)
                act.copy(flat(hidT), ps[:, 3, 0:2 * P]).then_inc(K.hid_c, 1)
                act.wait_ge(K.d_read, n + 1)
                act.copy(ysb[:, 0:512], ps[:, 5, :]).then_inc(K.ya, 1)

            with act.Fori(0, GROUPS) as g:
                group(FAST, g + GROUPS * l)
            with act.If(overflow(act, l)):
                with act.Fori(0, ROUNDS) as r:
                    with act.Fori(0, GROUPS) as g:
                        group(OVER[l], r * GROUPS + g)

        def gla():
            def evac(j):
                kind, n, _, bank = JOBS[j]
                act.wait_ge(g_job, j + 1)
                b = ps[:, bank, :]
                if kind == "lr":
                    ins = act.copy(glr[0:GRANK, :], b[0:GRANK, 0:POS])
                elif kind == "q":
                    ins = act.mul(gqT[:, n, :], b[:, 0:SEQ], GDK ** -0.5)
                elif kind == "k":
                    ins = act.copy(gkT[:, n, :], b[:, 0:POS])
                elif kind == "r":
                    ins = act.activation(gr[:, n // 2, (n % 2) * 512:(n % 2 + 1) * 512], b, ACT.Silu)
                elif n == 4:
                    for g in range(GH):
                        ins = act.copy(gv[0:META, 2, g * GDV:(g + 1) * GDV], b[QUAD * g:QUAD * g + META, 0:GDV])
                else:
                    i, hb = divmod(n, 2)
                    ins = act.copy(gv[0:WID[i], i, hb * 512:(hb + 1) * 512], b[0:WID[i], :])
                ins.then_inc(g_act, 1)

            mine = [j for j in range(len(JOBS)) if JOBS[j][2] == "act"]
            for j in mine[:5]:
                evac(j)
            act.wait_ge(g_abs, 1)
            link(act.activation(gt, gt, ACT.Exp, scale=-1.0))
            act.activation(gt, gt, ACT.Ln, bias=one_b).then_inc(g_log, 1)
            for j in mine[5:9]:
                evac(j)
            act.wait_ge(gq_dif, 1)
            act.activation(gtq, gtq, ACT.Exp, scale=1.0 / TAU).then_inc(gq_exp, 1)
            act.wait_ge(zeroed, 11)
            for s in range(NSUB):
                n = META + SUB * (s + 1)
                act.wait_ge(gk_dif, s + 1)
                act.activation(gk[s % 3][:, :, 0:n], gk[s % 3][:, :, 0:n], ACT.Exp, scale=-1.0 / TAU).then_inc(gk_exp, 1)
                for j in mine[9 + 2 * s:11 + 2 * s]:
                    if j < V_END:
                        evac(j)
            for j in range(V_END, R_END):
                evac(j)
            act.wait_ge(zeroed, 12)
            for g in range(GH):
                act.wait_ge(g_attT, g + 1)
                act.copy(attM[0:META, g, :], ps[0:META, 2 * g + 1, 0:SEQ]).then_inc(g_aT_act, 1)
            for t in range(2):
                act.wait_ge(g_o, t + 1)
                for g in range(GH):
                    ins = act.activation(gsq, ps[:, 2 * t + g // 2, (g % 2) * GDV:(g % 2 + 1) * GDV],
                                         ACT.Square, scale=GDV ** -0.5, accum_out=gos[:, t, g:g + 1])
                    link(ins)
            link(act.activation(flat(gos), flat(gos), ACT.Ln, bias=eps_b))
            act.activation(flat(gor), flat(gos), ACT.Exp, scale=-0.5).then_inc(g_orstd, 1)
            for t in range(2):
                act.wait_ge(g_yT, t + 1)
                for j in range(2):
                    ins = act.activation(gyT[:, j:4:2, t * P:(t + 1) * P],
                                         ps[:, 4 + 2 * t, :].rearrange("p (k q) -> p k q", k=4)[:, j::2, :],
                                         ACT.Copy, scale=gout[:, j:j + 1])
                ins.then_inc(g_yT_act, 1)

        act.wait_ge(consts, 3)
        norm(0)
        mla()
        moe(0)
        norm(2)
        gla()
        moe(1)

    @block.vector
    def _(dve):
        link = Links(dve, dve_link)
        TT, TS, STT = dve.tensor_tensor, dve.tensor_scalar, dve.scalar_tensor_tensor

        def gained(n, i):
            dve.wait_ge(xn_turned, NB[n] + ORDER[n].index(i) + 1)
            cols = slice(COL[i], COL[i] + WID[i])
            if i < 2:
                for b in range(2):
                    ins = TT(hT[:, 4 * b:4 * b + 4, cols], ps[:, 2 * i + b, :].rearrange("p (k q) -> p k q", k=4),
                             rep(gn[:, n, 4 * b:4 * b + 4], P), ALU.mult)
            else:
                ins = TT(hT[:, :, cols], ps[:, 4, 0:KD * META].rearrange("p (k q) -> p k q", k=KD),
                         rep(gn[:, n, :], META), ALU.mult)
            ins.then_inc(hT_ok, 1)

        def mixer_added(l, done, done0, added):
            n = 2 * l + 1
            for i in range(2):
                for b in range(2):
                    if (i, b) == (1, 1):
                        for t in ORDER[n][:-1]:
                            gained(n, t)
                    dve.wait_ge(done, done0 + 2 * i + b + 1)
                    hh = h[:, i, b * 512:(b + 1) * 512]
                    TT(hh, hh, ps[:, 2 * i + b, :], ALU.add).then_inc(added, 1)
            gained(n, 1)

        def norm(n):
            dve.wait_ge(*H_DONE[n][2])
            v = xflat[:, 2 * D:3 * D]
            link(STT(v, h[:, 2, :], 1.0 / D, h[:, 2, :], ALU.mult, ALU.mult))
            dve.tensor_reduce(ssq[:, 2:3], v, AX.X, ALU.add).then_inc(m_squares, 1)
            for m, i in enumerate(ORDER[n]):
                if i == 0:
                    dve.wait_ge(rstd_ok, rstd_count(n, i))
                    TS(xn[:, 0], h[:, 0, :].rearrange("p (q k) -> p k q", k=KD), rstd[:, 0:1], None, ALU.mult)\
                        .then_inc(xn_dve, 1)
                if m == 0 and n == 0:
                    dve.wait_ge(in_small, 16 * N_SMALL)
                gained(n, i)

        def mla():
            dve.wait_ge(in_c, 16)
            dve.tensor_copy(before01, before)
            dve.tensor_copy(ones01, ones[:, 0:P])
            dve.wait_ge(zeroed, 8)
            cos, sin = (c(n).rearrange("p (t f) -> p t f", t=3) for n in ("cos", "sin"))
            for tab, trig, m in ((tcq, cos, 0), (tsq, sin, 0), (tck, cos, 1), (tsk, sin, 1)):
                TT(tab, trig, over(gqk[:, m, NOPE:], 3), ALU.mult)
            link(TT(gprod[0:NOPE, :], gcol[0:NOPE, 0:1], gcol[0:NOPE, 1:2], ALU.mult))
            H = ROPE // 2
            for i in range(3):
                ba, bb, ra, rb_ = ((5 + 2 * i) % 8, (6 + 2 * i) % 8, slice(0, P), slice(0, P)) if i < 2 else \
                    (1, 2, slice(0, QUAD), slice(QUAD, 2 * QUAD))
                dve.wait_ge(z_rstd, i + 1)
                TS(cq[i][ra, 0:3, :], ps[ra, ba, 0:QR].rearrange("p (q k) -> p k q", k=3), zrs[ra, i, 0:1], None, ALU.mult)
                TS(cq[i][rb_, 3:5, :], ps[rb_, bb, 0:KVR].rearrange("p (q k) -> p k q", k=2), zrs[rb_, i, 1:2], None,
                   ALU.mult).then_inc(z_scaled, 1)
                TT(rp[:, 0, 0:ROPE], kr[:, i, :], tck[:, i, :], ALU.mult)
                link(TT(rp[:, 1, 0:ROPE], kr[:, i, :], tsk[:, i, :], ALU.mult))
                TT(kr[:, i, 0:H], rp[:, 0, 0:H], rp[:, 1, H:ROPE], ALU.subtract)
                link(TT(kr[:, i, H:ROPE], rp[:, 0, H:ROPE], rp[:, 1, 0:H], ALU.add))
                dve.wait_ge(c_turned, i + 1)
                R = WID[i]
                cols = slice(COL[i], COL[i] + R)
                src = [ps[:, 7, 0:3 * R], ps[:, 0, 0:2 * R]] if i == 2 else \
                    [ps[:, 3 + 2 * i, 0:3 * R], ps[:, 4 + 2 * i, 0:2 * R]]
                TT(cT[:, 0:3, cols], src[0].rearrange("p (k q) -> p k q", k=3), rep(gc5[:, 0:3], R), ALU.mult)
                TT(cT[:, 3:5, cols], src[1].rearrange("p (k q) -> p k q", k=2), rep(gc5[:, 3:5], R),
                   ALU.mult).then_inc(cT_ok, 1)

            def keys_values(i):
                for n, j in enumerate(ajobs("kv", i)):
                    dve.wait_ge(a_job, j + 1)
                    src = ps[:, abank(j), :].rearrange("p (h f) -> p h f", h=4)
                    dve.tensor_copy(k_sb[i][:, 4 * n:4 * n + 4, 0:NOPE], src[:, :, 0:NOPE])
                    if i < 2:
                        ins = dve.tensor_copy(vt[:, i, 4 * n:4 * n + 4, :], src[:, :, NOPE:])
                    else:
                        for q in range(4):
                            ins = dve.tensor_copy(vt[0:META, i, MH * q:MH * (q + 1), :],
                                                  src[QUAD * q:QUAD * q + META, :, NOPE:])
                    ins.then_inc(a_dve, 1)

            def rotary(i):
                Hn = HEADS if i < 2 else MH
                ra, rb_ = (rp[:, m].rearrange("p (h f) -> p h f", h=HEADS)[:, 0:Hn] for m in range(2))
                dve.wait_ge(q_squared, i + 1)
                dve.tensor_reduce(qst[:, i, 0:Hn], sq[:, 0:Hn], AX.X, ALU.add).then_inc(q_sums, 1)
                if i == 2:
                    x = q_sb[i][:, :, NOPE:QK]
                    TT(ra, x, over(tcq[:, i, :], Hn), ALU.mult)
                    link(TT(rb_, x, over(tsq[:, i, :], Hn), ALU.mult))
                    TT(q_sb[i][:, :, NOPE:NOPE + H], ra[:, :, 0:H], rb_[:, :, H:ROPE], ALU.subtract)
                    TT(q_sb[i][:, :, NOPE + H:QK], ra[:, :, H:ROPE], rb_[:, :, 0:H], ALU.add).then_inc(q_ready, 1)
                dve.wait_ge(k_squared, i + 1)
                link(dve.tensor_reduce(kst[:, i, 0:Hn], sq[:, 0:Hn, 0:NOPE], AX.X, ALU.add))
                TS(kst[:, i, 0:Hn], kst[:, i, 0:Hn], krs[:, i:i + 1], None, ALU.add).then_inc(k_sums, 1)

            def keys_scaled(i):
                Hn = HEADS if i < 2 else MH
                dve.wait_ge(k_rstd, i + 1)
                TT(k_sb[i][:, :, 0:NOPE], k_sb[i][:, :, 0:NOPE], rep(krst[:, i, 0:Hn], NOPE), ALU.mult)\
                    .then_inc(k_ready, 1)

            keys_values(0)
            rotary(0)
            keys_values(1)
            keys_values(2)
            rotary(1)
            rotary(2)
            for i in range(3):
                if i == 1:
                    keys_scaled(1)
                    keys_scaled(2)
                for n, j in enumerate(ajobs("tk", i)):
                    dve.wait_ge(a_job, j + 1)
                    src = ps[0:QK, abank(j), :].rearrange("p (h t) -> p h t", h=4)
                    if i < 2:
                        dst = kT[0:QK, 4 * n:4 * n + 4, COL[i]:COL[i] + P]
                    else:
                        dst = kT[0:QK, :, 0:META].rearrange("p (j s) t -> p s j t", j=4)
                        src = src.rearrange("p s (j t) -> p s j t", j=4)[:, :, :, 0:META]
                    TS(dst, src, gprod[0:QK, 0:1], None, ALU.mult).then_inc(a_dve, 1)

            dve.wait_ge(mq_s, 1)
            sm = ps[:, 7, 0:MH * META].rearrange("p (s k) -> p s k", s=MH)
            link(dve.tensor_reduce(mmx, sm, AX.X, ALU.max))
            link(TT(mp, sm, rep(mmx, META), ALU.subtract))
            TT(mp, mp, rep(scl[:, 2, 0:MH], META), ALU.mult).then_inc(mq_dif, 1)

            def shift(hd):
                dve.wait_ge(s_done, hd + 1)
                if hd >= 2:
                    dve.wait_ge(p_exp, hd - 1)
                dve.tensor_reduce(mx[hd % 2][:, 0:1], ps[:, hd % 2, 0:COL[1]], AX.X, ALU.max)
                link(dve.tensor_reduce(mx[hd % 2][:, 1:2], ps[:, hd % 2, COL[1]:PR], AX.X, ALU.max))
                STT(nb[hd % 2], mx[hd % 2], -1.0, scl[:, 0:2, hd], ALU.mult, ALU.mult).then_inc(s_shift, 1)

            def scale(hd):
                dve.wait_ge(p_exp, hd + 1)
                link(dve.reciprocal(ri[hd % 2], rs[hd % 2]))
                for i, o, n in ((0, 0, COL[1]), (1, COL[1], POS)):
                    pr = prob[hd % 2][:, o:o + n]
                    ins = TS(pr, pr, ri[hd % 2][:, i:i + 1], None, ALU.mult)
                ins.then_inc(p_scaled, 1)

            def frame_weights(hd):
                dve.wait_ge(p_turned, hd + 1)
                if hd >= 2:
                    dve.wait_ge(pv_done, hd - 1)
                dve.tensor_copy(pT[hd % 2], ps[:, 2 + 2 * (hd % 2), 0:3 * P]).then_inc(pt_dve, 1)

            shift(0)
            dve.wait_ge(mq_exp, 1)
            link(dve.tensor_reduce(mmx, mp, AX.X, ALU.add))
            link(dve.reciprocal(mri, mmx))
            TT(mp, mp, rep(mri, META), ALU.mult).then_inc(mq_p, 1)
            dve.wait_ge(mq_t, 1)
            dve.tensor_copy(mpT[0:META].rearrange("p (j s) t -> p s j t", j=4),
                            ps[0:META, 6, :].rearrange("p (s j t) -> p s j t", s=MH, j=4)[:, :, :, 0:META])\
                .then_inc(mq_c, 1)
            for hd in range(HEADS):
                if hd + 1 < HEADS:
                    shift(hd + 1)
                scale(hd)
                if hd:
                    frame_weights(hd - 1)
            frame_weights(HEADS - 1)
            dve.wait_ge(mo_done, 4)
            for j in range(4):
                hh = h[0:META, 2, j * 256:(j + 1) * 256]
                TT(hh, hh, ps[QUAD * j:QUAD * j + META, 4, 0:256], ALU.add).then_inc(mo_add, 1)
            mixer_added(0, mo_done, 4, mo_add)

        def route(l):
            nt = NT[l]
            V = slice(0, nt)
            first = c("first")
            dve.wait_ge(lg_turned, l + 1)
            W = NG + NE
            src = ps[:, 6, 0:nt * W].rearrange("p (t n) -> p t n", t=nt)
            dve.wait_ge(rstd_ok, rstd_count(2 * l + 1, 1))
            for i in range(nt):
                R = slice(0, WID[i])
                ins = STT(L[R, i, :], src[R, i, :], rstd[R, i:i + 1], rb[R, l, :], ALU.mult, ALU.add)
            link(ins)

            def choose(x, best, out):
                n = x.shape[2]
                link(TT(out, x, rep(best, n), ALU.is_equal))
                link(TT(out, out, over(first[:, NE - n:], nt), ALU.mult))
                link(dve.tensor_reduce(pm[:, V], out, AX.X, ALU.max))
                link(TT(out, out, rep(pm[:, V], n), ALU.is_equal))

            lg, lx = L[:, V, 0:NG], L[:, V, NG:]
            link(dve.tensor_reduce(mg[:, V], lg, AX.X, ALU.max))
            TT(E5[:, V, 0:NG], lg, rep(mg[:, V], NG), ALU.subtract).then_inc(FAST.add, 1)
            choose(lg, mg[:, V], g4[:, V, :])
            link(TS(g4[:, V, :], g4[:, V, :], BIG, -BIG, ALU.mult, ALU.add))
            link(TT(le[:, V, :].rearrange("p t (g e) -> p t g e", g=NG), lx.rearrange("p t (g e) -> p t g e", g=NG),
                    rep3(g4[:, V, :], EPG), ALU.add))
            link(dve.tensor_reduce(m1[:, V], le[:, V, :], AX.X, ALU.max))
            choose(le[:, V, :], m1[:, V], s1[:, V, :])
            link(STT(le[:, V, :], s1[:, V, :], -3 * BIG, le[:, V, :], ALU.mult, ALU.add))
            link(dve.tensor_reduce(m2[:, V], le[:, V, :], AX.X, ALU.max))
            TT(E5[:, V, NG:], rep(m2[:, V], 1), rep(m1[:, V], 1), ALU.subtract).then_inc(e_dif, 1)
            choose(le[:, V, :], m2[:, V], s2[:, V, :])
            link(TT(sel[:, V, :], s1[:, V, :], s2[:, V, :], ALU.add))
            TT(sel01[:, V, :], sel[:, V, :], rep(c("valid")[:, V], NE), ALU.mult).then_inc(sel_ok, 1)
            dve.wait_ge(rank_done, l + 1)
            link(STT(rm[:, V, 0:NE], sel01[:, V, :], -OFF, ps[:, 7, 0:nt * NE].rearrange("p (t n) -> p t n", t=nt),
                     ALU.mult, ALU.add))

        def gate(l):
            V = slice(0, NT[l])
            dve.wait_ge(e_exp, l + 1)
            link(dve.tensor_reduce(mg[:, V], E5[:, V, 0:NG], AX.X, ALU.add))
            e2 = E5[:, V, NG:].rearrange("p t o -> p (t o)")
            link(STT(m1[:, V], e2, 1.0, mg[:, V], ALU.add, ALU.mult))
            link(dve.reciprocal(w1[:, V], m1[:, V]))
            link(TT(w2[:, V], w1[:, V], e2, ALU.mult))
            TT(s1[:, V, :], s1[:, V, :], rep(w1[:, V], NE), ALU.mult)
            link(TT(s2[:, V, :], s2[:, V, :], rep(w2[:, V], NE), ALU.mult))
            link(TT(gates[:, V, 0:NE], s1[:, V, :], s2[:, V, :], ALU.add))

        def moe(l):
            route(l)
            nt, norm_n = NT[l], 2 * l + 1

            def dispatch(K, e0, sent, between=None):
                s4, g4_ = (t[:, 0:nt, :].rearrange("p t (e s) -> p t e s", e=GE) for t in (Sg, Gg))
                slot = c("slot").unsqueeze(1).unsqueeze(1).to_broadcast([P, nt, GE, SLOTS])
                TT(s4, slot, rep3(rm[:, 0:nt, e0], SLOTS), ALU.is_equal).then_inc(K.send, 1)
                if between:
                    between()
                dve.wait_ge(K.send, 2 * sent + (-1))
                TT(g4_, s4, rep3(gates[:, 0:nt, e0], SLOTS), ALU.mult).then_inc(K.send, 1)

            def group(K, n, g, sent, combined):
                for b in range(2):
                    dve.wait_ge(K.rows, 2 * n + (b + 1))
                    TT(xe[:, 4 * b:4 * b + 4, :], ps[:, b, :].rearrange("p (k q) -> p k q", k=4),
                       rep(gn[:, norm_n, 4 * b:4 * b + 4], P), ALU.mult).then_inc(K.rows_in, 1)
                dve.wait_ge(K.turn, n + 1)
                dispatch(K, bass.ds(GE * g + GE, GE), sent)
                dve.wait_ge(K.silu, n + 1)
                TT(hid.rearrange("p k q -> p q k"), ex.rearrange("p (q k) -> p q k", k=2),
                   ps[:, 2, FE:2 * FE].rearrange("p (q k) -> p q k", k=2), ALU.mult).then_inc(K.hid, 1)
                dve.wait_ge(K.d_read, n + 1)
                dve.tensor_copy(ysb[:, 512:], ps[:, 6, :]).then_inc(K.yd, 1)
                for i in range(nt):
                    for b in range(2):
                        dve.wait_ge(K.comb, combined + (2 * i + b + 1))
                        hh = h[0:WID[i], i, b * 512:(b + 1) * 512]
                        TT(hh, hh, ps[0:WID[i], COMBINE[2 * i + b], :], ALU.add).then_inc(K.add, 1)

            K = FAST
            dispatch(K, slice(0, GE), (GROUPS + 1) * l + 1, lambda: gate(l))
            dve.wait_ge(count_done, l + 1)
            link(dve.tensor_reduce(most[0:1], ps[0:1, 5, 0:NE], AX.X, ALU.max))
            TS(flag[0:1, l:l + 1], most[0:1], float(SLOTS), None, ALU.is_gt).then_inc(flag_ok, 1)
            with dve.Fori(0, GROUPS) as g:
                group(K, g + GROUPS * l, g, g + ((GROUPS + 1) * l + 2), g * (2 * nt) + COMB0[l])
            with dve.If(overflow(dve, l)):
                K = OVER[l]
                with dve.Fori(0, ROUNDS) as r:
                    opened = r * (2 * nt * GROUPS + 1) + 1
                    TS(flat(rm), flat(rm), -float(SLOTS), None, ALU.add).then_inc(K.add, 1)
                    dve.wait_ge(K.add, opened)
                    dispatch(K, slice(0, GE), r * (GROUPS + 1) + 1)
                    with dve.Fori(0, GROUPS) as g:
                        n = r * GROUPS + g
                        group(K, n, g, n + r + 2, n * (2 * nt))
            dve.memset(marker[0:1, l:l + 1], 0.0).then_inc(moe_done, 1)

        def gla():
            mine = [j for j in range(len(JOBS)) if JOBS[j][2] == "dve"]
            for j in mine[:4]:
                _, n, _, bank = JOBS[j]
                dve.wait_ge(g_job, j + 1)
                TS(ga[:, n, :], ps[:, bank, 0:POS], bg[:, n:n + 1], None, ALU.add).then_inc(g_dve, 1)
            dve.wait_ge(g_dve, 4)
            STT(flat(gt), flat(ga), -1.0, flat(ga), ALU.mult, ALU.max).then_inc(g_abs, 1)
            dve.wait_ge(g_log, 1)
            link(STT(flat(ga), flat(ga), 0.0, flat(gt), ALU.min, ALU.subtract))
            for g in range(GH):
                ins = dve.tensor_tensor_scan(gb[:, g, :], ones, ga[:, g, :], 0.0, ALU.mult, ALU.add)
            link(ins)
            tq4 = gtq.rearrange("p g (s j) -> p g s j", s=NSUB)
            TT(tq4, blocks, ref.to_broadcast([P, GH, NSUB, SUB]), ALU.subtract).then_inc(gq_dif, 1)

            def mul(s):
                n = META + SUB * (s + 1)
                dve.wait_ge(gk_exp, s + 1)
                v = gk[s % 3][:, :, 0:n]
                TT(v, v, gkT[:, :, 0:n], ALU.mult).then_inc(gk_ok, 1)

            def masked(s):
                t, j = divmod(s, NSUB // 2)
                n = META + SUB * (s + 1)
                rows = slice(32 * j, 32 * j + 32)
                dve.wait_ge(g_att, s + 1)
                TT(att[rows, t, :, 0:n], ps[rows, 0:GH, 0:n],
                   over(c("causal")[rows, t * POS:t * POS + n], GH), ALU.mult).then_inc(g_attm, 1)

            dve.wait_ge(gq_exp, 1)
            TT(gqT, gqT, gtq, ALU.mult).then_inc(gq_ok, 1)
            dve.wait_ge(zeroed, 13)
            for s in range(NSUB):
                mul(s)
                if s >= 1:
                    masked(s - 1)
            masked(NSUB - 1)
            for g in range(GH):
                dve.wait_ge(g_attT, g + 1)
                dve.tensor_copy(attT[g], ps[:, 2 * g, 0:3 * P]).then_inc(g_aT_dve, 1)
            dve.wait_ge(g_orstd, 1)
            for t in range(2):
                for g in range(GH):
                    v = gr[:, t, g * GDV:(g + 1) * GDV]
                    ins = STT(v, ps[:, 2 * t + g // 2, (g % 2) * GDV:(g % 2 + 1) * GDV], gor[:, t, g:g + 1], v,
                              ALU.mult, ALU.mult)
                ins.then_inc(g_y, 1)
            for t in range(2):
                dve.wait_ge(g_yT, t + 1)
                TT(gyT[:, 4:8, t * P:(t + 1) * P].rearrange("p (g j) q -> p g j q", j=2),
                   ps[:, 5 + 2 * t, :].rearrange("p (g j q) -> p g j q", g=2, j=2),
                   gout[:, :].unsqueeze(1).unsqueeze(3).to_broadcast([P, 2, 2, P]), ALU.mult).then_inc(g_yT_dve, 1)
            mixer_added(1, go_done, 0, go_add)

        dve.wait_ge(in_h, 48)
        norm(0)
        mla()
        moe(0)
        norm(2)
        gla()
        moe(1)


NAMES = ["x", "meta_tokens", "norm_mix", "norm_ffn", "mla_w_in", "mla_g_q", "mla_w_uq", "mla_g_kv", "mla_w_ukv",
         "mla_g_qn", "mla_g_kn", "mla_w_o", "gla_w_in", "gla_w_gate_up", "gla_b_gate", "gla_g_out", "gla_w_o",
         "moe_w_rg", "moe_b_rg", "moe_w_re", "moe_b_re", "moe_w_gate", "moe_w_up", "moe_w_down"]


def kernel(**inputs):
    import concourse.bacc as bacc
    from concourse.bass_utils import run_bass_kernel_spmd

    nc = bacc.Bacc("TRN2", target_bir_lowering=False, num_devices=1)
    table, rows, _ = constants()
    arrays = {n: np.ascontiguousarray(inputs[n]) for n in NAMES}
    arrays["const"], arrays["mask_rows"] = table, rows
    aps = {n: nc.dram_tensor(f"in_{n}", v.shape, F32, kind="ExternalInput").ap() for n, v in arrays.items()}
    out = nc.dram_tensor("out_0", (1, SEQ, D), F32, kind="ExternalOutput").ap()
    program(nc, aps, out)
    r = run_bass_kernel_spmd(nc, [{f"in_{n}": v for n, v in arrays.items()}], core_ids=[0])
    return r.results[0]["out_0"]
```
